# Optimizing a Trainium2 kernel written in Bass

```python
import jax, jax.numpy as jnp
from jax import lax
import numpy as np
import math
import jax
import jax.numpy as jnp

D_MODEL = 1024
BATCH = 1
SEQ = 256
DEPTH = 2

N_BRANCH = 4
HEAD_DIM = 64
BRANCH_WIDTH = D_MODEL // N_BRANCH
N_HEADS = BRANCH_WIDTH // HEAD_DIM
NORM_EPS = 1e-6
RW_DECAY_LORA = 64
RW_AAA_LORA = 64
RW_GATE_LORA = 128
RW_DECAY_SCALE = 0.606531
RW_LN_EPS = 64e-5
SB_BLOCK = 128
RET_CHUNK = 128
RET_GN_EPS = 1e-5
ROPE_BASE = 10000.0
CONV_WIDTH = 31
CONV_LN_EPS = 1e-5
D_FF = 2816
N_EXPERTS = 8
TOP_K = 2
D_FF_EXPERT = 1408
MOE_BLOCK = 256

RW_IN = 3 * BRANCH_WIDTH + RW_DECAY_LORA + RW_AAA_LORA + RW_GATE_LORA
SB_IN = 3 * BRANCH_WIDTH
RET_IN = 4 * BRANCH_WIDTH
CONV_IN = 2 * BRANCH_WIDTH
N_IN = RW_IN + SB_IN + RET_IN + CONV_IN
MIX_SPLITS = [RW_IN, RW_IN + SB_IN, RW_IN + SB_IN + RET_IN]
RW_SPLITS = [BRANCH_WIDTH, 2 * BRANCH_WIDTH, 3 * BRANCH_WIDTH,
             3 * BRANCH_WIDTH + RW_DECAY_LORA, 3 * BRANCH_WIDTH + RW_DECAY_LORA + RW_AAA_LORA]


def _rmsnorm(x, gain, eps=NORM_EPS):
    x32 = x.astype(jnp.float32)
    y = x32 * lax.rsqrt(jnp.mean(x32 * x32, axis=-1, keepdims=True) + eps)
    return (y * gain).astype(x.dtype)

def _layernorm(x, gain, bias, eps):
    x32 = x.astype(jnp.float32)
    xc = x32 - jnp.mean(x32, axis=-1, keepdims=True)
    var = jnp.mean(xc * xc, axis=-1, keepdims=True)
    return (xc * lax.rsqrt(var + eps) * gain + bias).astype(x.dtype)

def _token_shift(x):
    return jnp.pad(x, ((0, 0), (1, 0), (0, 0)))[:, :-1]

def _split_heads(t):
    return t.reshape(t.shape[0], t.shape[1], N_HEADS, HEAD_DIM)

def _rwkv7_mixer(p, mu, w0, w2, a0, a2, g2, k_k, k_a, r_k, ln_w, ln_b):
    B, S, _ = p.shape
    p = p + (_token_shift(p) - p) * mu
    r, k, v, pw, pa, pg = jnp.split(p, RW_SPLITS, axis=-1)
    w = jnp.exp(-RW_DECAY_SCALE * jax.nn.sigmoid((w0 + jnp.tanh(pw) @ w2).astype(jnp.float32)))
    a = jax.nn.sigmoid(a0 + pa @ a2)
    g = jax.nn.sigmoid(pg) @ g2
    r, k, v, w, a = (_split_heads(t) for t in (r, k, v, w, a))
    kk32 = (k * k_k.reshape(N_HEADS, HEAD_DIM)).astype(jnp.float32)
    kk = kk32 / jnp.maximum(jnp.sqrt(jnp.sum(kk32 * kk32, axis=-1, keepdims=True)), 1e-12)
    k = k * (1.0 + (a - 1.0) * k_a.reshape(N_HEADS, HEAD_DIM))

    def step(state, inp):
        r_t, w_t, k_t, v_t, kk_t, a_t = inp
        sa = jnp.einsum('bhvk,bhk->bhv', state, -kk_t)
        state = (state * w_t[:, :, None, :] + sa[..., None] * (kk_t * a_t)[:, :, None, :]
                 + v_t[..., None] * k_t[:, :, None, :])
        return state, jnp.einsum('bhvk,bhk->bhv', state, r_t)

    seq_first = lambda t: jnp.moveaxis(t.astype(jnp.float32), 1, 0)
    state0 = jnp.zeros((B, N_HEADS, HEAD_DIM, HEAD_DIM), jnp.float32)
    _, y = lax.scan(step, state0, tuple(seq_first(t) for t in (r, w, k, v, kk, a)))
    y = jnp.moveaxis(y, 0, 1)
    y = _layernorm(y, ln_w.reshape(N_HEADS, HEAD_DIM), ln_b.reshape(N_HEADS, HEAD_DIM), RW_LN_EPS)
    y = y + jnp.sum(r * k * r_k, axis=-1, keepdims=True) * v
    return (y.reshape(B, S, BRANCH_WIDTH) * g).astype(p.dtype)

def _stick_breaking_mixer(p, q_norm, k_norm):
    B, S, _ = p.shape
    nb = S // SB_BLOCK
    blocks = lambda t: _split_heads(t).reshape(B, nb, SB_BLOCK, N_HEADS, HEAD_DIM).transpose(0, 3, 1, 2, 4)
    q, k, v = (blocks(t) for t in jnp.split(p, 3, axis=-1))
    q = _rmsnorm(q, q_norm) * (HEAD_DIM ** -0.5)
    k = _rmsnorm(k, k_norm)
    idx = jnp.arange(SB_BLOCK)
    rev_incl = (idx[:, None] >= idx[None, :]).astype(jnp.float32)
    diag_mask = idx[None, :] < idx[:, None]
    acc = jnp.zeros((B, N_HEADS, nb, SB_BLOCK), jnp.float32)
    o = jnp.zeros((B, N_HEADS, nb, SB_BLOCK, HEAD_DIM), jnp.float32)
    for d in range(nb):
        n = nb - d
        z = jnp.einsum('bhnqd,bhnkd->bhnqk', q[:, :, d:], k[:, :, :n]).astype(jnp.float32)
        ls = jax.nn.log_sigmoid(-z)
        if d == 0:
            ls = jnp.where(diag_mask, ls, 0.0)
        cum = jnp.einsum('bhnqk,kj->bhnqj', ls, rev_incl)
        log_a = z + cum + acc[:, :, d:, :, None]
        if d == 0:
            log_a = jnp.where(diag_mask, log_a, -jnp.inf)
        attn = jnp.exp(log_a)
        o = o.at[:, :, d:].add(jnp.einsum('bhnqk,bhnkd->bhnqd', attn.astype(v.dtype), v[:, :, :n]).astype(jnp.float32))
        acc = acc.at[:, :, d:].add(cum[..., 0])
    return o.transpose(0, 2, 3, 1, 4).reshape(B, S, BRANCH_WIDTH).astype(p.dtype)

def _rotary(t):
    S = t.shape[1]
    inv_freq = ROPE_BASE ** (-jnp.arange(0, HEAD_DIM, 2, dtype=jnp.float32) / HEAD_DIM)
    ang = jnp.arange(S, dtype=jnp.float32)[:, None] * inv_freq[None, :]
    cos = jnp.cos(ang)[None, :, None, :].astype(t.dtype)
    sin = jnp.sin(ang)[None, :, None, :].astype(t.dtype)
    t1, t2 = jnp.split(t, 2, axis=-1)
    return jnp.concatenate([t1 * cos - t2 * sin, t1 * sin + t2 * cos], axis=-1)

def _retention_mixer(p, gn_w):
    B, S, _ = p.shape
    dt = p.dtype
    q, k, v, gt = jnp.split(p, 4, axis=-1)
    q = _rotary(_split_heads(q))
    k = _rotary(_split_heads(k)) * (HEAD_DIM ** -0.5)
    v = _split_heads(v)
    nc = S // RET_CHUNK
    chunk = lambda t: t.reshape(B, nc, RET_CHUNK, N_HEADS, HEAD_DIM).transpose(0, 3, 1, 2, 4)
    qc, kc, vc = chunk(q), chunk(k), chunk(v)
    log_gamma = jnp.log(1.0 - 2.0 ** (-5.0 - jnp.arange(N_HEADS, dtype=jnp.float32)))
    idx = jnp.arange(RET_CHUNK, dtype=jnp.float32)
    rel = idx[:, None] - idx[None, :]
    intra_decay = jnp.where(rel >= 0, jnp.exp(jnp.maximum(rel, 0.0) * log_gamma[:, None, None]), 0.0)
    k_decay = jnp.exp((RET_CHUNK - 1 - idx)[None, :] * log_gamma[:, None])
    q_decay = jnp.exp((idx + 1.0)[None, :] * log_gamma[:, None])
    chunk_decay = jnp.exp(RET_CHUNK * log_gamma)
    scores = jnp.einsum('bhcqd,bhckd->bhcqk', qc, kc) * intra_decay[None, :, None].astype(dt)
    intra = jnp.einsum('bhcqk,bhckd->bhcqd', scores, vc)
    kv = jnp.einsum('bhckd,bhcke->cbhde', kc * k_decay[None, :, None, :, None].astype(dt), vc)

    def step(state, kv_c):
        return chunk_decay[None, :, None, None] * state + kv_c, state

    _, state_prev = lax.scan(step, jnp.zeros(kv.shape[1:], jnp.float32), kv.astype(jnp.float32))
    inter = jnp.einsum('bhcqd,cbhde->bhcqe', qc * q_decay[None, :, None, :, None].astype(dt),
                       state_prev.astype(dt))
    o = (intra + inter).transpose(0, 2, 3, 1, 4).reshape(B, S, N_HEADS, HEAD_DIM)
    o = _layernorm(o, gn_w.reshape(N_HEADS, HEAD_DIM), 0.0, RET_GN_EPS)
    return o.reshape(B, S, BRANCH_WIDTH) * jax.nn.silu(gt)

def _conformer_conv_mixer(p, dw, db, ln_w, ln_b):
    u_a, u_b = jnp.split(p, 2, axis=-1)
    u = u_a * jax.nn.sigmoid(u_b)
    u = lax.conv_general_dilated(u, dw[:, None, :].astype(u.dtype), window_strides=(1,),
                                 padding=[(CONV_WIDTH - 1, 0)],
                                 dimension_numbers=('NWC', 'WIO', 'NWC'),
                                 feature_group_count=BRANCH_WIDTH) + db
    return jax.nn.silu(_layernorm(u, ln_w, ln_b, CONV_LN_EPS))

def _swiglu(h, w1, w3, w2):
    return (jax.nn.silu(h @ w1) * (h @ w3)) @ w2

def _moe_ffn(h, router, w1, w3, w2):
    B, S, D = h.shape
    T = B * S
    xt = h.reshape(T, D)
    logits = (xt @ router).astype(jnp.float32)
    top_logit, top_idx = lax.top_k(logits, TOP_K)
    gates = jax.nn.softmax(top_logit, axis=-1)
    n_assign = T * TOP_K
    expert = top_idx.reshape(-1)
    token = jnp.arange(n_assign) // TOP_K
    order = jnp.argsort(expert)
    expert_s, token_s, weight_s = expert[order], token[order], gates.reshape(-1)[order]
    x_s = xt[token_s]
    counts = jnp.bincount(expert, length=N_EXPERTS)
    n_blk = n_assign // MOE_BLOCK
    seg_start = jnp.sort(jnp.concatenate([jnp.arange(n_blk) * MOE_BLOCK, jnp.cumsum(counts)[:-1]]))
    seg_end = jnp.concatenate([seg_start[1:], jnp.array([n_assign], seg_start.dtype)])
    seg_blk = jnp.minimum(seg_start // MOE_BLOCK, n_blk - 1)
    seg_exp = expert_s[jnp.minimum(seg_start, n_assign - 1)]

    def segment(args):
        start, end, blk, e = args
        rows = blk * MOE_BLOCK + jnp.arange(MOE_BLOCK)
        xb = lax.dynamic_slice_in_dim(x_s, blk * MOE_BLOCK, MOE_BLOCK, axis=0)
        yb = _swiglu(xb, w1[e], w3[e], w2[e])
        return jnp.where(((rows >= start) & (rows < end))[:, None], yb, 0.0)

    y_seg = lax.map(segment, (seg_start, seg_end, seg_blk, seg_exp))
    y_s = jax.ops.segment_sum(y_seg, seg_blk, num_segments=n_blk).reshape(n_assign, D)
    out = jax.ops.segment_sum(y_s * weight_s[:, None].astype(y_s.dtype), token_s, num_segments=T)
    return out.reshape(B, S, D)

def first_inputs(seed: int = 0) -> dict:
    key = jax.random.key(seed)
    ks = iter(jax.random.split(key, 40))
    nrm = lambda shape, scale: scale * jax.random.normal(next(ks), shape, jnp.float32)
    L, C = DEPTH, BRANCH_WIDTH
    nd, nm = (DEPTH + 1) // 2, DEPTH // 2
    return {
        "x": nrm((BATCH, SEQ, D_MODEL), 1.0),
        "norm_mix": 1.0 + nrm((L, D_MODEL), 0.1),
        "w_in": nrm((L, D_MODEL, N_IN), D_MODEL ** -0.5),
        "rw_mu": jax.random.uniform(next(ks), (L, RW_IN), jnp.float32),
        "rw_w0": -1.5 + nrm((L, C), 0.5),
        "rw_w2": nrm((L, RW_DECAY_LORA, C), 0.5 * RW_DECAY_LORA ** -0.5),
        "rw_a0": nrm((L, C), 0.5),
        "rw_a2": nrm((L, RW_AAA_LORA, C), RW_AAA_LORA ** -0.5),
        "rw_g2": nrm((L, RW_GATE_LORA, C), RW_GATE_LORA ** -0.5),
        "rw_k_k": 0.85 + nrm((L, C), 0.1),
        "rw_k_a": 1.0 + nrm((L, C), 0.1),
        "rw_r_k": nrm((L, N_HEADS, HEAD_DIM), 0.1),
        "rw_ln_w": 1.0 + nrm((L, C), 0.1),
        "rw_ln_b": nrm((L, C), 0.01),
        "sb_q_norm": 1.0 + nrm((L, HEAD_DIM), 0.1),
        "sb_k_norm": 1.0 + nrm((L, HEAD_DIM), 0.1),
        "ret_gn": 1.0 + nrm((L, C), 0.1),
        "conv_dw": nrm((L, CONV_WIDTH, C), CONV_WIDTH ** -0.5),
        "conv_b": nrm((L, C), 0.01),
        "conv_ln_w": 1.0 + nrm((L, C), 0.1),
        "conv_ln_b": nrm((L, C), 0.01),
        "w_gate": nrm((L, N_BRANCH, D_MODEL, D_MODEL), D_MODEL ** -0.5),
        "w_branch": nrm((L, N_BRANCH, C, D_MODEL), C ** -0.5),
        "w_out": nrm((L, D_MODEL, D_MODEL), 0.5 * D_MODEL ** -0.5),
        "norm_ffn": 1.0 + nrm((L, D_MODEL), 0.1),
        "ffn_w1": nrm((nd, D_MODEL, D_FF), D_MODEL ** -0.5),
        "ffn_w3": nrm((nd, D_MODEL, D_FF), D_MODEL ** -0.5),
        "ffn_w2": nrm((nd, D_FF, D_MODEL), 0.5 * D_FF ** -0.5),
        "router": nrm((nm, D_MODEL, N_EXPERTS), D_MODEL ** -0.5),
        "moe_w1": nrm((nm, N_EXPERTS, D_MODEL, D_FF_EXPERT), D_MODEL ** -0.5),
        "moe_w3": nrm((nm, N_EXPERTS, D_MODEL, D_FF_EXPERT), D_MODEL ** -0.5),
        "moe_w2": nrm((nm, N_EXPERTS, D_FF_EXPERT, D_MODEL), 0.5 * D_FF_EXPERT ** -0.5),
    }

def first_block(x, norm_mix, w_in, rw_mu, rw_w0, rw_w2, rw_a0, rw_a2, rw_g2, rw_k_k, rw_k_a, rw_r_k,
              rw_ln_w, rw_ln_b, sb_q_norm, sb_k_norm, ret_gn, conv_dw, conv_b, conv_ln_w, conv_ln_b,
              w_gate, w_branch, w_out, norm_ffn, ffn_w1, ffn_w3, ffn_w2, router, moe_w1, moe_w3, moe_w2):
    for l in range(DEPTH):
        h = _rmsnorm(x, norm_mix[l])
        p_rw, p_sb, p_ret, p_conv = jnp.split(h @ w_in[l], MIX_SPLITS, axis=-1)
        branches = (
            _rwkv7_mixer(p_rw, rw_mu[l], rw_w0[l], rw_w2[l], rw_a0[l], rw_a2[l], rw_g2[l],
                         rw_k_k[l], rw_k_a[l], rw_r_k[l], rw_ln_w[l], rw_ln_b[l]),
            _stick_breaking_mixer(p_sb, sb_q_norm[l], sb_k_norm[l]),
            _retention_mixer(p_ret, ret_gn[l]),
            _conformer_conv_mixer(p_conv, conv_dw[l], conv_b[l], conv_ln_w[l], conv_ln_b[l]),
        )
        merged = jax.nn.sigmoid(h @ w_gate[l, 0]) * (branches[0] @ w_branch[l, 0])
        for i in range(1, N_BRANCH):
            merged = merged + jax.nn.sigmoid(h @ w_gate[l, i]) * (branches[i] @ w_branch[l, i])
        x = x + merged @ w_out[l]
        h = _rmsnorm(x, norm_ffn[l])
        if l % 2 == 0:
            x = x + _swiglu(h, ffn_w1[l // 2], ffn_w3[l // 2], ffn_w2[l // 2])
        else:
            x = x + _moe_ffn(h, router[l // 2], moe_w1[l // 2], moe_w3[l // 2], moe_w2[l // 2])
    return x


RMS_EPS = 1e-6
ROPE_THETA = 500000.0

SSD_HEAD_DIM = 64
SSD_D_INNER = D_MODEL
SSD_HEADS = SSD_D_INNER // SSD_HEAD_DIM
SSD_GROUPS = 4
SSD_D_STATE = 128
SSD_CONV = 4
SSD_CHUNK = 256
SSD_CONV_DIM = SSD_D_INNER + 2 * SSD_GROUPS * SSD_D_STATE

DIL_PAIRS = ((128, 1), (512, 4), (2048, 16))
DIL_HEAD_DIM = 64
DIL_HEADS_PER_GROUP = 8
DIL_HEADS = DIL_HEADS_PER_GROUP * len(DIL_PAIRS)
DIL_QKV = DIL_HEADS * DIL_HEAD_DIM
DIL_OUT = DIL_HEADS_PER_GROUP * DIL_HEAD_DIM

MOBA_HEAD_DIM = 64
MOBA_WIDTH = D_MODEL
MOBA_HEADS = MOBA_WIDTH // MOBA_HEAD_DIM
MOBA_BLOCK = 256
MOBA_TOPK = 3
MOBA_Q_CHUNK = 16

EVEN_IN_SIZES = (SSD_D_INNER, SSD_CONV_DIM, SSD_HEADS, DIL_QKV, DIL_QKV, DIL_QKV, DIL_OUT)
EVEN_IN = sum(EVEN_IN_SIZES)
EVEN_MIX = SSD_D_INNER + DIL_OUT
ODD_IN = 4 * MOBA_WIDTH
N_EVEN = (DEPTH + 1) // 2
N_ODD = DEPTH // 2


def rms_norm(x, w):
    xf = x.astype(jnp.float32)
    y = xf * lax.rsqrt(jnp.mean(xf * xf, axis=-1, keepdims=True) + RMS_EPS)
    return (y * w.astype(jnp.float32)).astype(x.dtype)

def partial_rope(x, pos):
    e = x.shape[-1]
    rd = e // 4
    half = rd // 2
    inv = ROPE_THETA ** (-jnp.arange(half, dtype=jnp.float32) * 2.0 / rd)
    ang = pos.astype(jnp.float32)[:, None] * inv[None, :]
    cos = jnp.cos(ang)[:, None, :]
    sin = jnp.sin(ang)[:, None, :]
    xr = x[..., :rd].astype(jnp.float32)
    x1, x2 = xr[..., :half], xr[..., half:]
    rot = jnp.concatenate([x1 * cos - x2 * sin, x2 * cos + x1 * sin], axis=-1)
    return jnp.concatenate([rot.astype(x.dtype), x[..., rd:]], axis=-1)

def split_cols(t, sizes):
    outs, o = [], 0
    for s in sizes:
        outs.append(t[..., o:o + s])
        o += s
    return outs

def causal_dwconv(x, w, b):
    K = w.shape[1]
    rhs = jnp.transpose(w)[:, None, :].astype(x.dtype)
    y = lax.conv_general_dilated(x, rhs, window_strides=(1,), padding=((K - 1, 0),),
                                 dimension_numbers=("NWC", "WIO", "NWC"),
                                 feature_group_count=x.shape[-1])
    return y + b.astype(x.dtype)

def segsum(a):
    T = a.shape[-1]
    cs = jnp.cumsum(a, axis=-1)
    diff = cs[..., :, None] - cs[..., None, :]
    mask = jnp.tril(jnp.ones((T, T), dtype=bool))
    return jnp.where(mask, diff, -jnp.inf)

def ssd_chunked_scan(x, dt, A, Bm, Cm):
    Bsz, S, H, P = x.shape
    G, N = Bm.shape[2], Bm.shape[3]
    J = H // G
    L = SSD_CHUNK
    pad = (-S) % L
    xdt = x.astype(jnp.float32) * dt[..., None]
    a = dt * A
    Bf = Bm.astype(jnp.float32)
    Cf = Cm.astype(jnp.float32)
    if pad:
        padseq = lambda t: jnp.pad(t, [(0, 0), (0, pad)] + [(0, 0)] * (t.ndim - 2))
        xdt, a, Bf, Cf = padseq(xdt), padseq(a), padseq(Bf), padseq(Cf)
    nc = (S + pad) // L
    xdt = xdt.reshape(Bsz, nc, L, G, J, P)
    Bc = Bf.reshape(Bsz, nc, L, G, N)
    Cc = Cf.reshape(Bsz, nc, L, G, N)
    a = a.reshape(Bsz, nc, L, G, J).transpose(0, 3, 4, 1, 2)
    a_cs = jnp.cumsum(a, axis=-1)
    cb = jnp.einsum("bclgn,bcsgn->bgcls", Cc, Bc)
    m = cb[:, :, None] * jnp.exp(segsum(a))
    y_diag = jnp.einsum("bgjcls,bcsgjp->bclgjp", m, xdt)
    w_end = jnp.exp(a_cs[..., -1:] - a_cs).transpose(0, 3, 4, 1, 2)
    states = jnp.einsum("bclgn,bclgjp->bcgjpn", Bc, xdt * w_end[..., None])
    a_last = jnp.pad(a_cs[..., -1], [(0, 0)] * 3 + [(1, 0)])
    decay_chunk = jnp.exp(segsum(a_last))
    states0 = jnp.concatenate([jnp.zeros_like(states[:, :1]), states], axis=1)
    entering = jnp.einsum("bgjzc,bcgjpn->bzgjpn", decay_chunk, states0)[:, :-1]
    w_start = jnp.exp(a_cs).transpose(0, 3, 4, 1, 2)
    y_off = jnp.einsum("bclgn,bcgjpn->bclgjp", Cc, entering) * w_start[..., None]
    return (y_diag + y_off).reshape(Bsz, nc * L, H, P)[:, :S]

def dilated_group(q, k, v, window, dil):
    Bsz, S, h, e = q.shape
    band = window // dil
    Lsub = S // dil
    nb = -(-Lsub // band)
    Lp = nb * band

    def to_sub(t):
        t = t.astype(jnp.float32).reshape(Bsz, Lsub, dil, h, e).transpose(0, 3, 2, 1, 4)
        t = jnp.pad(t, ((0, 0), (0, 0), (0, 0), (0, Lp - Lsub), (0, 0)))
        return t.reshape(Bsz, h, dil, nb, band, e)

    def with_prev(t):
        prev = jnp.pad(t, ((0, 0), (0, 0), (0, 0), (1, 0), (0, 0), (0, 0)))[:, :, :, :-1]
        return jnp.concatenate([prev, t], axis=4)

    qs = to_sub(q)
    kb = with_prev(to_sub(k))
    vb = with_prev(to_sub(v))
    s = jnp.einsum("bhrnqe,bhrnke->bhrnqk", qs, kb) * (e ** -0.5)
    i = jnp.arange(band)[:, None]
    j = jnp.arange(2 * band)[None, :]
    dist = i + band - j
    n = jnp.arange(nb)[:, None, None]
    valid = (dist >= 0) & (dist <= band) & ((n * band + j[None] - band) >= 0)
    s = jnp.where(valid, s, -jnp.inf)
    mx = jnp.max(s, axis=-1, keepdims=True)
    p = jnp.exp(s - mx)
    den = jnp.sum(p, axis=-1)
    o = jnp.einsum("bhrnqk,bhrnke->bhrnqe", p, vb) / den[..., None]
    lse = mx[..., 0] + jnp.log(den)
    o = o.reshape(Bsz, h, dil, Lp, e)[:, :, :, :Lsub].transpose(0, 3, 2, 1, 4).reshape(Bsz, S, h, e)
    lse = lse.reshape(Bsz, h, dil, Lp)[:, :, :, :Lsub].transpose(0, 3, 2, 1).reshape(Bsz, S, h)
    return o, lse

def moba_attention(q, k, v):
    Bsz, S, H, e = q.shape
    blk = MOBA_BLOCK
    nblk = -(-S // blk)
    Sp = nblk * blk
    scale = e ** -0.5

    def heads_first(t):
        t = t.astype(jnp.float32).transpose(0, 2, 1, 3)
        return jnp.pad(t, ((0, 0), (0, 0), (0, Sp - S), (0, 0)))

    qh = heads_first(q)
    kb = heads_first(k).reshape(Bsz, H, nblk, blk, e)
    vb = heads_first(v).reshape(Bsz, H, nblk, blk, e)
    kmean = jnp.mean(kb, axis=3)
    gate = jnp.einsum("bhte,bhne->bhtn", qh, kmean)
    tblk = jnp.arange(Sp) // blk
    past = jnp.arange(nblk)[None, :] < tblk[:, None]
    gate = jnp.where(past, gate, -jnp.inf)
    ksel = min(MOBA_TOPK, nblk)
    _, sel = lax.top_k(gate, ksel)
    sel_valid = sel < tblk[:, None]

    Qc = MOBA_Q_CHUNK
    nq = Sp // Qc
    qc = qh.reshape(Bsz, H, nq, Qc, e).transpose(2, 0, 1, 3, 4)
    selc = sel.reshape(Bsz, H, nq, Qc, ksel).transpose(2, 0, 1, 3, 4)
    valc = sel_valid.reshape(Bsz, H, nq, Qc, ksel).transpose(2, 0, 1, 3, 4)
    bi = jnp.arange(Bsz)[:, None, None, None]
    hi = jnp.arange(H)[None, :, None, None]

    def one_chunk(args):
        c, q_c, sel_c, val_c = args
        own = (c * Qc) // blk
        k_sel = kb[bi, hi, sel_c]
        v_sel = vb[bi, hi, sel_c]
        s_sel = jnp.einsum("bhqe,bhqjke->bhqjk", q_c, k_sel) * scale
        s_sel = jnp.where(val_c[..., None], s_sel, -jnp.inf).reshape(Bsz, H, Qc, ksel * blk)
        k_own = lax.dynamic_index_in_dim(kb, own, axis=2, keepdims=False)
        v_own = lax.dynamic_index_in_dim(vb, own, axis=2, keepdims=False)
        s_own = jnp.einsum("bhqe,bhke->bhqk", q_c, k_own) * scale
        qpos = c * Qc + jnp.arange(Qc)
        kpos = own * blk + jnp.arange(blk)
        s_own = jnp.where(kpos[None, :] <= qpos[:, None], s_own, -jnp.inf)
        p = jax.nn.softmax(jnp.concatenate([s_sel, s_own], axis=-1), axis=-1)
        p_sel = p[..., :ksel * blk].reshape(Bsz, H, Qc, ksel, blk)
        return (jnp.einsum("bhqjk,bhqjke->bhqe", p_sel, v_sel)
                + jnp.einsum("bhqk,bhke->bhqe", p[..., ksel * blk:], v_own))

    out = lax.map(one_chunk, (jnp.arange(nq), qc, selc, valc))
    return out.transpose(1, 0, 3, 2, 4).reshape(Bsz, Sp, H, e)[:, :S]

def ssd_dilated_layer(x, norm_w, w_in, conv_w, conv_b, dt_bias, a_log, d_skip, ssd_norm_w,
                      q_norm, k_norm, w_out, pos):
    Bsz, S, _ = x.shape
    h = rms_norm(x, norm_w)
    proj = jnp.einsum("bsd,df->bsf", h, w_in.astype(h.dtype))
    z, xbc, dt, q, k, v, g = split_cols(proj, EVEN_IN_SIZES)
    xbc = jax.nn.silu(causal_dwconv(xbc, conv_w, conv_b))
    xs, bm, cm = split_cols(xbc, (SSD_D_INNER, SSD_GROUPS * SSD_D_STATE, SSD_GROUPS * SSD_D_STATE))
    xs = xs.reshape(Bsz, S, SSD_HEADS, SSD_HEAD_DIM)
    dt = jax.nn.softplus(dt.astype(jnp.float32) + dt_bias.astype(jnp.float32))
    A = -jnp.exp(a_log.astype(jnp.float32))
    y = ssd_chunked_scan(xs, dt, A, bm.reshape(Bsz, S, SSD_GROUPS, SSD_D_STATE),
                         cm.reshape(Bsz, S, SSD_GROUPS, SSD_D_STATE))
    y = y + d_skip.astype(jnp.float32)[:, None] * xs.astype(jnp.float32)
    y = y.reshape(Bsz, S, SSD_D_INNER) * jax.nn.silu(z.astype(jnp.float32))
    y = rms_norm(y.reshape(Bsz, S, SSD_GROUPS, -1),
                 ssd_norm_w.reshape(SSD_GROUPS, -1)).reshape(Bsz, S, SSD_D_INNER)
    q = partial_rope(rms_norm(q.reshape(Bsz, S, DIL_HEADS, DIL_HEAD_DIM), q_norm), pos)
    k = partial_rope(rms_norm(k.reshape(Bsz, S, DIL_HEADS, DIL_HEAD_DIM), k_norm), pos)
    v = v.reshape(Bsz, S, DIL_HEADS, DIL_HEAD_DIM)
    outs, lses = [], []
    for gi, (window, dil) in enumerate(DIL_PAIRS):
        hs = slice(gi * DIL_HEADS_PER_GROUP, (gi + 1) * DIL_HEADS_PER_GROUP)
        o_g, lse_g = dilated_group(q[:, :, hs], k[:, :, hs], v[:, :, hs], window, dil)
        outs.append(o_g)
        lses.append(lse_g)
    wts = jax.nn.softmax(jnp.stack(lses, axis=0), axis=0)
    o = jnp.sum(wts[..., None] * jnp.stack(outs, axis=0), axis=0)
    o = o.reshape(Bsz, S, DIL_OUT) * jax.nn.silu(g.astype(jnp.float32))
    mixed = jnp.concatenate([y.astype(jnp.float32), o], axis=-1).astype(x.dtype)
    return x + jnp.einsum("bsf,fd->bsd", mixed, w_out.astype(x.dtype))

def moba_layer(x, norm_w, w_in, q_norm, k_norm, w_out, pos):
    Bsz, S, _ = x.shape
    h = rms_norm(x, norm_w)
    proj = jnp.einsum("bsd,df->bsf", h, w_in.astype(h.dtype))
    q, k, v, g = split_cols(proj, (MOBA_WIDTH,) * 4)
    q = partial_rope(rms_norm(q.reshape(Bsz, S, MOBA_HEADS, MOBA_HEAD_DIM), q_norm), pos)
    k = partial_rope(rms_norm(k.reshape(Bsz, S, MOBA_HEADS, MOBA_HEAD_DIM), k_norm), pos)
    v = v.reshape(Bsz, S, MOBA_HEADS, MOBA_HEAD_DIM)
    o = moba_attention(q, k, v).reshape(Bsz, S, MOBA_WIDTH) * jax.nn.silu(g.astype(jnp.float32))
    return x + jnp.einsum("bsf,fd->bsd", o.astype(x.dtype), w_out.astype(x.dtype))

def second_inputs(seed: int = 0) -> dict:
    key = jax.random.key(seed)
    ks = jax.random.split(key, 20)
    f32 = jnp.float32
    nrm = lambda k, shape, s: jax.random.normal(k, shape, f32) * s
    x = jax.random.normal(ks[0], (BATCH, SEQ, D_MODEL), f32)
    even_norm_w = 1.0 + nrm(ks[1], (N_EVEN, D_MODEL), 0.05)
    even_w_in = nrm(ks[2], (N_EVEN, D_MODEL, EVEN_IN), D_MODEL ** -0.5)
    even_conv_w = nrm(ks[3], (N_EVEN, SSD_CONV_DIM, SSD_CONV), SSD_CONV ** -0.5)
    even_conv_b = nrm(ks[4], (N_EVEN, SSD_CONV_DIM), 0.01)
    dt0 = jnp.exp(jax.random.uniform(ks[5], (N_EVEN, SSD_HEADS), f32,
                                     math.log(1e-3), math.log(1e-1)))
    even_dt_bias = dt0 + jnp.log(-jnp.expm1(-dt0))
    even_a_log = jnp.log(jax.random.uniform(ks[6], (N_EVEN, SSD_HEADS), f32, 1.0, 16.0))
    even_d_skip = 1.0 + nrm(ks[7], (N_EVEN, SSD_HEADS), 0.1)
    even_ssd_norm_w = 1.0 + nrm(ks[8], (N_EVEN, SSD_D_INNER), 0.05)
    even_q_norm = 1.0 + nrm(ks[9], (N_EVEN, DIL_HEAD_DIM), 0.05)
    even_k_norm = 1.0 + nrm(ks[10], (N_EVEN, DIL_HEAD_DIM), 0.05)
    even_w_out = nrm(ks[11], (N_EVEN, EVEN_MIX, D_MODEL), EVEN_MIX ** -0.5)
    odd_norm_w = 1.0 + nrm(ks[12], (N_ODD, D_MODEL), 0.05)
    odd_w_in = nrm(ks[13], (N_ODD, D_MODEL, ODD_IN), D_MODEL ** -0.5)
    odd_q_norm = 1.0 + nrm(ks[14], (N_ODD, MOBA_HEAD_DIM), 0.05)
    odd_k_norm = 1.0 + nrm(ks[15], (N_ODD, MOBA_HEAD_DIM), 0.05)
    odd_w_out = nrm(ks[16], (N_ODD, MOBA_WIDTH, D_MODEL), MOBA_WIDTH ** -0.5)
    return {"x": x, "even_norm_w": even_norm_w, "even_w_in": even_w_in,
            "even_conv_w": even_conv_w, "even_conv_b": even_conv_b,
            "even_dt_bias": even_dt_bias, "even_a_log": even_a_log, "even_d_skip": even_d_skip,
            "even_ssd_norm_w": even_ssd_norm_w, "even_q_norm": even_q_norm,
            "even_k_norm": even_k_norm, "even_w_out": even_w_out,
            "odd_norm_w": odd_norm_w, "odd_w_in": odd_w_in, "odd_q_norm": odd_q_norm,
            "odd_k_norm": odd_k_norm, "odd_w_out": odd_w_out}

def second_block(x, even_norm_w, even_w_in, even_conv_w, even_conv_b, even_dt_bias, even_a_log,
              even_d_skip, even_ssd_norm_w, even_q_norm, even_k_norm, even_w_out,
              odd_norm_w, odd_w_in, odd_q_norm, odd_k_norm, odd_w_out):
    pos = jnp.arange(x.shape[1], dtype=jnp.int32)
    for layer in range(DEPTH):
        li = layer // 2
        if layer % 2 == 0:
            x = ssd_dilated_layer(x, even_norm_w[li], even_w_in[li], even_conv_w[li],
                                  even_conv_b[li], even_dt_bias[li], even_a_log[li],
                                  even_d_skip[li], even_ssd_norm_w[li], even_q_norm[li],
                                  even_k_norm[li], even_w_out[li], pos)
        else:
            x = moba_layer(x, odd_norm_w[li], odd_w_in[li], odd_q_norm[li], odd_k_norm[li],
                           odd_w_out[li], pos)
    return x


def setup_inputs(seed=0):
    out = dict(first_inputs(seed))
    for name, value in second_inputs(seed + 1).items():
        if name != "x":
            out[name + "_2"] = value
    return out


def reference(
    x, norm_mix, w_in, rw_mu, rw_w0, rw_w2, rw_a0, rw_a2, rw_g2, rw_k_k, rw_k_a, rw_r_k,
    rw_ln_w, rw_ln_b, sb_q_norm, sb_k_norm, ret_gn, conv_dw, conv_b, conv_ln_w, conv_ln_b,
    w_gate, w_branch, w_out, norm_ffn, ffn_w1, ffn_w3, ffn_w2, router, moe_w1, moe_w3, moe_w2,
    even_norm_w_2, even_w_in_2, even_conv_w_2, even_conv_b_2, even_dt_bias_2, even_a_log_2,
    even_d_skip_2, even_ssd_norm_w_2, even_q_norm_2, even_k_norm_2, even_w_out_2, odd_norm_w_2,
    odd_w_in_2, odd_q_norm_2, odd_k_norm_2, odd_w_out_2,
):
    x = first_block(
        x, norm_mix, w_in, rw_mu, rw_w0, rw_w2, rw_a0, rw_a2, rw_g2, rw_k_k, rw_k_a, rw_r_k,
        rw_ln_w, rw_ln_b, sb_q_norm, sb_k_norm, ret_gn, conv_dw, conv_b, conv_ln_w, conv_ln_b,
        w_gate, w_branch, w_out, norm_ffn, ffn_w1, ffn_w3, ffn_w2, router, moe_w1, moe_w3,
        moe_w2,
    )
    return second_block(
        x, even_norm_w_2, even_w_in_2, even_conv_w_2, even_conv_b_2, even_dt_bias_2,
        even_a_log_2, even_d_skip_2, even_ssd_norm_w_2, even_q_norm_2, even_k_norm_2,
        even_w_out_2, odd_norm_w_2, odd_w_in_2, odd_q_norm_2, odd_k_norm_2, odd_w_out_2,
    )


_drawn_inputs = setup_inputs


def setup_inputs(seed=0):
    import zlib

    import numpy as np

    out = dict(_drawn_inputs(seed))
    spreads = {}
    factors = {'rw_k_k': 3.319,
     'rw_ln_b': 8.0,
     'sb_q_norm': 2.706,
     'conv_b': 6.321,
     'conv_ln_b': 8.0,
     'even_conv_b_2': 6.727,
     'even_q_norm_2': 8.0,
     'even_k_norm_2': 8.0,
     'odd_norm_w_2': 6.285,
     'odd_q_norm_2': 8.0,
     'odd_k_norm_2': 8.0}
    for name, (base, spread) in spreads.items():
        noise = np.random.default_rng([zlib.crc32(name.encode()), seed]).standard_normal(out[name].shape)
        drawn = base * np.exp(spread * noise) if base else spread * noise
        out[name] = jnp.asarray(drawn.astype(out[name].dtype))
    for name, factor in factors.items():
        out[name] = (out[name] * factor).astype(out[name].dtype)
    return out
```

```python
import concourse.bass as bass
from concourse import mybir
from contextlib import ExitStack
import numpy as np

F = mybir.dt.float32
U32 = mybir.dt.uint32
I32 = mybir.dt.int32
ALU = mybir.AluOpType
ACT = mybir.ActivationFunctionType
AX = mybir.AxisListType

T = 256
DM = 1024
EPS = 1e-6
RWS = 0.606531
NEG = -1.0e30
RING = 4
SLOT = 4096
ARENA = 26550

PARAM_COLS = []
for _l in range(2):
    PARAM_COLS += [(f"nm{_l}", 8), (f"nf{_l}", 8), (f"mu{_l}", 8), (f"w0{_l}", 2), (f"a0{_l}", 2), (f"kk{_l}", 2),
                   (f"ka{_l}", 2), (f"rk{_l}", 2), (f"lw{_l}", 2), (f"lb{_l}", 2), (f"sq{_l}", 1), (f"sk{_l}", 1),
                   (f"gn{_l}", 2), (f"dw{_l}", 62), (f"cb{_l}", 2), (f"cw{_l}", 2), (f"cl{_l}", 2)]
PARAM_COLS += [("rt", 64), ("en", 8), ("ecw", 64), ("ecb", 16), ("edt", 1), ("eal", 1), ("eds", 8), ("esn", 8),
               ("eqn", 1), ("ekn", 1), ("on", 8), ("oqn", 1), ("okn", 1)]
CONST_COLS = [("id", 128), ("blk", 128), ("ones", 128), ("nones", 128), ("pr", 128), ("pp", 128), ("cr", 256),
              ("sr", 256), ("cp", 256), ("sp", 256), ("dec", 1024), ("rneg", 128), ("sbadd", 384), ("sb01", 128),
              ("dil", 768), ("ssd", 256), ("rwm", 256), ("lvl", 384), ("rst", 256), ("iota", 8)]


def offsets(cols):
    out, n = {}, 0
    for k, w in cols:
        out[k] = (n, w)
        n += w
    return out, n


def consts():
    off, n = offsets(CONST_COLS)
    C = np.zeros((128, n), np.float32)

    def put(k, a):
        o, w = off[k]
        C[:a.shape[0], o:o + w] = a.reshape(a.shape[0], w)

    i = np.arange(128)
    put("id", np.eye(128))
    put("blk", (i[:, None] // 64 == i[None, :] // 64) * 1.0)
    put("ones", np.ones((128, 128)))
    put("nones", -np.ones((128, 128)))
    for key, half, width in (("pr", 32, 64), ("pp", 8, 16)):
        m = np.zeros((128, 128))
        for b in (0, 64):
            for j in range(half):
                m[b + j + half, b + j] = -1.0
                m[b + j, b + j + half] = 1.0
        put(key, m)
    t = np.arange(T, dtype=np.float32)
    inv = np.float32(10000.0) ** (-np.arange(0, 64, 2, dtype=np.float32) / np.float32(64))
    ang = (t[None, :] * inv[:, None]).astype(np.float32)
    put("cr", np.tile(np.cos(ang), (4, 1)))
    put("sr", np.tile(np.sin(ang), (4, 1)))
    inv = np.float32(500000.0) ** (-np.arange(8, dtype=np.float32) * np.float32(2.0) / np.float32(16))
    ang = (t[None, :] * inv[:, None]).astype(np.float32)
    c, s = np.ones((64, T)), np.zeros((64, T))
    c[0:16] = np.tile(np.cos(ang), (2, 1))
    s[0:16] = np.tile(np.sin(ang), (2, 1))
    put("cp", np.tile(c, (2, 1)))
    put("sp", np.tile(s, (2, 1)))
    dec = np.zeros((128, 4, T))
    rel = np.arange(T)[None, :] - i[:, None]
    for h in range(4):
        lg = np.log(1.0 - 2.0 ** (-5.0 - h))
        dec[:, h] = np.where(rel >= 0, np.exp(np.maximum(rel, 0) * lg), 0.0) * 0.125
    put("dec", dec)
    put("rneg", (i[:, None] >= i[None, :]) * -1.0)
    lt = i[:, None] < i[None, :]
    d = np.where(lt, 0.0, NEG)
    put("sbadd", np.concatenate([d, np.zeros((128, 128)), d], 1))
    put("sb01", lt * 1.0)
    dil = np.zeros((128, 3, 256))
    dist = i[:, None] + 128 - np.arange(256)[None, :]
    for g, (w, r) in enumerate(((128, 1), (512, 4), (2048, 16))):
        ok = (dist >= 0) & (dist <= w) & (dist % r == 0)
        dil[:, g] = np.where(ok, 0.0, NEG)
    put("dil", dil)
    put("ssd", (np.arange(256)[None, :] >= i[:, None]) * 1.0)
    j = np.arange(64)
    st, inc = (j[:, None] < j[None, :]) * 1.0, (j[:, None] <= j[None, :]) * 1.0
    put("rwm", np.concatenate([st, inc, st, inc], 1))
    lvl = np.zeros((64, 6, 64))
    for v in range(6):
        b = 1 << v
        lvl[:, v] = (j[:, None] // (2 * b) == j[None, :] // (2 * b)) & (j[:, None] % (2 * b) < b) & (j[None, :] % (2 * b) >= b)
    put("lvl", lvl)
    put("rst", np.tile((np.arange(T) % 64 != 0) * 1.0, (128, 1)))
    put("iota", np.tile(np.arange(8), (128, 1)) * 1.0)
    return C


def col(a):
    return a.reshape(-1, 128).T


def params(i):
    P = {}
    for l in range(2):
        P[f"nm{l}"], P[f"nf{l}"], P[f"mu{l}"] = col(i["norm_mix"][l]), col(i["norm_ffn"][l]), col(i["rw_mu"][l])
        for k, n in (("w0", "rw_w0"), ("a0", "rw_a0"), ("kk", "rw_k_k"), ("ka", "rw_k_a"), ("rk", "rw_r_k"),
                     ("lw", "rw_ln_w"), ("lb", "rw_ln_b"), ("gn", "ret_gn"), ("cb", "conv_b"), ("cw", "conv_ln_w"),
                     ("cl", "conv_ln_b")):
            P[f"{k}{l}"] = col(i[n][l].reshape(-1))
        P[f"sq{l}"], P[f"sk{l}"] = col(np.tile(i["sb_q_norm"][l], 2)), col(np.tile(i["sb_k_norm"][l], 2))
        P[f"dw{l}"] = i["conv_dw"][l].reshape(31, 2, 128).transpose(2, 1, 0).reshape(128, 62)
    P["rt"] = i["router"][0].reshape(8, 128, 8).transpose(1, 0, 2).reshape(128, 64)
    P["en"], P["on"] = col(i["even_norm_w_2"][0]), col(i["odd_norm_w_2"][0])
    P["ecw"] = i["even_conv_w_2"][0].reshape(16, 128, 4).transpose(1, 0, 2).reshape(128, 64)
    P["ecb"], P["esn"] = col(i["even_conv_b_2"][0]), col(i["even_ssd_norm_w_2"][0])
    P["edt"], P["eal"] = i["even_dt_bias_2"][0].reshape(16, 1), i["even_a_log_2"][0].reshape(16, 1)
    P["eds"] = col(np.repeat(i["even_d_skip_2"][0], 64))
    for k, n in (("eqn", "even_q_norm_2"), ("ekn", "even_k_norm_2"), ("oqn", "odd_q_norm_2"), ("okn", "odd_k_norm_2")):
        P[k] = col(np.tile(i[n][0], 2))
    off, n = offsets(PARAM_COLS)
    out = np.zeros((128, n), np.float32)
    for k, (o, w) in off.items():
        out[:P[k].shape[0], o:o + w] = P[k]
    return out


class Op:

    def __init__(self, eng, fn, after, sem=None, val=0):
        self.eng, self.fn, self.after, self.sem, self.val = eng, fn, after, sem, val
        self.count = 0
        self.signals = sem is not None


def flat(a):
    if a is None:
        return []
    return [o for x in a for o in flat(x)] if isinstance(a, (list, tuple)) else [a]


class Engine:

    def __init__(self, name, done, chained):
        self.name, self.done, self.chained, self.ops = name, done, chained, []

    def __call__(self, fn, *after):
        after = flat(after)
        if self.chained and self.ops:
            after = after + [self.ops[-1]]
        op = Op(self, fn, after)
        op.index = len(self.ops)
        self.ops.append(op)
        return op

    def run(self, e):
        seen = {}
        for op in self.ops:
            need = {}
            for o in op.after:
                k, v = (o.sem, o.val) if o.sem is not None else (o.eng.done, o.count)
                need[k.name] = max(need.get(k.name, (0, None))[0], v), k
            for name, (v, k) in need.items():
                if v > seen.get(name, 0):
                    seen[name] = v
                    e.wait_ge(k, v)
            ins = op.fn(e)
            if op.sem is not None:
                ins.then_inc(op.sem, 16)
            elif op.signals:
                ins.then_inc(self.done, 1)


def number(engines):
    for E in engines:
        for op in E.ops:
            for o in op.after:
                if o.sem is None:
                    o.signals = True
    for E in engines:
        n = 0
        for op in E.ops:
            if op.sem is None and op.signals:
                n += 1
                op.count = n


class Bank:
    def __init__(self, t):
        self.t, self.free = t, []


class Ring:
    def __init__(self, items):
        self.items, self.n = items, 0

    def __call__(self):
        self.n += 1
        return self.items[(self.n - 1) % len(self.items)]


def build(nc, w, cst, par, xT, outT):
    ctx = ExitStack()
    with ctx:
        def sb(name, n, p=128):
            return ctx.enter_context(nc.sbuf_tensor("s_" + name, [p, n], F))

        def sem(name):
            return ctx.enter_context(nc.semaphore(name))

        coff, cn = offsets(CONST_COLS)
        poff, pn = offsets(PARAM_COLS)
        C_, P_ = sb("cst", cn), sb("par", pn)
        X_, H_, ring_, A_ = sb("X", 2048), sb("H", 2048), sb("ring", RING * SLOT), sb("arena", ARENA)
        R_ = sb("roots", 336)
        banks = [Bank(ctx.enter_context(nc.psum_tensor(f"b{i}", [128, 512], F))) for i in range(8)]
        PE, V, A, G, SP = (Engine(n, sem("done_" + n), n in "VAG") for n in ("PE", "V", "A", "G", "SP"))
        engines = [PE, V, A, G, SP]

        def c(k, p=128):
            o, n = coff[k]
            return C_[0:p, o:o + n]

        def pc(k, j=0, p0=0, p1=128):
            o, n = poff[k]
            return P_[p0:p1, o + j:o + j + 1]

        X = X_[:, :].rearrange("p (t n) -> p t n", n=T)
        H = H_[:, :].rearrange("p (t n) -> p t n", n=T)

        dma_sems = {}

        def dma(eng, key, fn, *after):
            if key not in dma_sems:
                dma_sems[key] = [sem("dma_" + key), 0]
            s, n = dma_sems[key]
            dma_sems[key][1] = n + 16
            op = eng(fn, *after)
            op.sem, op.val, op.signals = s, n + 16, True
            return op

        t_cst = dma(SP, "cst", lambda e: e.dma_start(C_[:, :], cst))
        t_par = dma(SP, "par", lambda e: e.dma_start(P_[:, :], par))
        t_x = dma(SP, "x", lambda e: e.dma_start(X, xT.rearrange("(t p) n -> p t n", p=128)))

        class Slot:
            def __init__(self, i):
                self.i, self.free = i, []
        slots = Ring([Slot(i) for i in range(RING)])

        def load(src):
            k, n = src.shape
            kt = k // 128
            s = slots()
            dst = ring_[:, s.i * SLOT:s.i * SLOT + kt * n].rearrange("p (k n) -> p k n", k=kt)
            t = dma(SP, f"w{s.i}", lambda e: e.dma_start(dst, src.rearrange("(k p) n -> p k n", p=128)), s.free)
            return s, dst, t

        def tt(out, a, b, op, *af, E=None):
            return (E or V)(lambda e: e.tensor_tensor(out, a, b, op), *af)

        def ts(out, a, s1, s2, o0, o1=None, *af, E=None):
            if o1 is None:
                return (E or V)(lambda e: e.tensor_scalar(out, a, s1, None, o0), *af)
            return (E or V)(lambda e: e.tensor_scalar(out, a, s1, s2, o0, o1), *af)

        def stt(out, a, s, b, o0, o1, *af):
            return V(lambda e: e.scalar_tensor_tensor(out=out, in0=a, scalar=s, in1=b, op0=o0, op1=o1), *af)

        def cp(out, a, *af):
            return V(lambda e: e.tensor_copy(out, a), *af)

        def act(out, a, f, *af, bias=0.0, scale=1.0, acc=None):
            kw = dict(bias=bias, scale=scale)
            if acc is not None:
                kw["accum_out"] = acc
            return A(lambda e: e.activation(out, a, f, **kw), *af)

        def acp(out, a, *af, scale=1.0):
            return A(lambda e: e.activation(out, a, ACT.Copy, scale=scale), *af)

        def root(x, y, a_, t, scale=1.0):
            V(lambda e: e.tensor_scalar(y.bitcast(I32), x.bitcast(I32), 1, None, ALU.logical_shift_right), t)
            V(lambda e: e.tensor_scalar(y.bitcast(I32), y.bitcast(I32), -1.0, 1597463007.0, MUL, ADD))
            for i in range(3):
                stt(a_, y, -0.5, y, MUL, MUL)
                tt(a_, a_, x, MUL)
                t = stt(y, a_, 1.5, y, ADD, MUL)
            return t if scale == 1.0 else ts(y, y, scale, None, MUL)

        def sums(cols_, tiles, *af):
            return mm([(cols_[:, i, j, :], s_[:, 128 * i:128 * i + 128], c("blk")[:, 0:65:64], True)
                       for i in range(2) for j, s_ in enumerate(tiles)], af)

        def spread(b, rs, js, *af):
            return mm([(b.t[64 * h:64 * h + 64, T * q + 128 * i:T * q + 128 * i + 128], rs[:, i, j, h:h + 1].broadcast_to([128, 64]), ident, True)
                       for q, j in enumerate(js) for i in range(2) for h in range(2)], b.free, af)

        def factors(b, rs, n, wide, eps, t, scale=1.0, floor=None):
            r, x, a_ = (z[:, 0:4 * n] for z in rs)
            if floor is None:
                t = ts(x, b.t[:, 0:4 * n], 1.0 / wide, eps, MUL, ADD, t)
            else:
                t = ts(x, b.t[:, 0:4 * n], floor, None, MAX, None, t)
            b.free = [t]
            t = root(x, r, a_, t, scale)
            return r.rearrange("p (i j h) -> p i j h", i=2, h=2), t

        def table(b, n):
            return b.t[:, 0:4 * n].rearrange("p (i j h) -> p i j h", i=2, h=2)

        def half_tanh(out, x, *af, bias=0.0):
            return act(out, x, ACT.Tanh, *af, bias=bias, scale=0.5)

        def one_plus(out, th, x, *af):
            return stt(out, th, 1.0, x, ADD, MUL, *af)

        def recip(out, a, *af):
            return V(lambda e: e.reciprocal(out, a), *af)

        def mset(out, v, *af):
            return G(lambda e: e.memset(out, v), *af)

        def mm(items, *af):
            items = list(items)

            def f(e):
                for o, l, r, st in items:
                    x = e.matmul(o, l, r, start=st, stop=True, skip_group_check=True)
                return x
            return PE(f, *af)

        def tr(items, *af):
            items = list(items)

            def f(e):
                for o, i_, idn in items:
                    x = e.transpose(o, i_, idn)
                return x
            return PE(f, *af)

        MUL, ADD, SUB, MAX, MIN, POW = ALU.mult, ALU.add, ALU.subtract, ALU.max, ALU.min, ALU.pow
        ident = c("id")
        last = lambda: [E.ops[-1] for E in (PE, V, A, G) if E.ops]

        class Arena:
            def __init__(self, lo, hi):
                self.lo, self.hi, self.at = lo, hi, lo

            def __call__(self, *shape, p=128):
                n = int(np.prod(shape))
                assert self.at + n <= self.hi, ("arena", self.at + n, self.hi)
                v = A_[0:p, self.at:self.at + n]
                self.at += n
                if len(shape) == 2:
                    v = v.rearrange("p (a b) -> p a b", a=shape[0])
                if len(shape) == 3:
                    v = v.rearrange("p (a b c) -> p a b c", a=shape[0], b=shape[1])
                if len(shape) == 4:
                    v = v.rearrange("p (a b c d) -> p a b c d", a=shape[0], b=shape[1], c=shape[2])
                return v

        def barrier():
            tk = last()
            for E in (PE, V, A, G):
                fence[E] = tk

        fence = {}

        def fenced(E):
            return fence.get(E, [])

        for E in (PE, V, A, G):
            def hook(fn, *after, E=E):
                extra = fence.pop(E, None)
                return Engine.__call__(E, fn, *after, *( [extra] if extra else []))
            E.q = hook
        PE_, V_, Aq_, G_ = PE, V, A, G
        PE = lambda fn, *a: PE_.q(fn, *a)
        V = lambda fn, *a: V_.q(fn, *a)
        A = lambda fn, *a: Aq_.q(fn, *a)
        G = lambda fn, *a: G_.q(fn, *a)
        last = lambda: [E.ops[-1] for E in (PE_, V_, Aq_, G_) if E.ops]

        def barrier():
            tk = last()
            for E in (PE_, V_, Aq_, G_):
                fence[E] = tk

        def run(*gens):
            gens = [g if isinstance(g, tuple) else (g, 1) for g in gens]
            while gens:
                for g in list(gens):
                    for _ in range(g[1]):
                        try:
                            next(g[0])
                        except StopIteration:
                            gens.remove(g)
                            break

        def two(b):
            return b.t[:, :].rearrange("p (t n) -> p t n", t=2)

        def proj(src, rhs, nk, bring, evac, t_rhs):
            f0 = 0
            for s_ in src:
                s, wv, tw = load(s_)
                n = s_.shape[1]
                for j in range(0, n, 256):
                    b = bring()
                    m = min(256, n - j)
                    items = []
                    for i in range(0, m, 128):
                        mw = min(128, m - i)
                        for k in range(nk):
                            items.append((b.t[0:mw, 2 * i:2 * i + 256], wv[:, k, j + i:j + i + mw], rhs[:, k, :], k == 0))
                    t = mm(items, tw, t_rhs, b.free)
                    s.free = [t]
                    b.free = evac(b, f0, (m + 127) // 128, t)
                    f0 += (m + 127) // 128
                    yield

        def cols(W, c0, c1, step=512):
            return [W[:, i:min(i + step, c1)] for i in range(c0, c1, step)]

        def to_sbuf(dst, E="A"):
            def evac(b, f0, nt, t):
                o = dst[:, f0:f0 + nt, :]
                i = two(b)[:, 0:nt, :]
                return [acp(o, i, t)] if E == "A" else [cp(o, i, t)]
            return evac

        def proj_tok(src, bring, dst, t_rhs):
            n0 = 0
            for s_ in src:
                s, wv, tw = load(s_)
                n = s_.shape[1]
                for i in range(2):
                    b = bring()
                    t = mm([(b.t[:, 0:n], H[:, k, 128 * i:128 * i + 128], wv[:, k, :], k == 0) for k in range(8)],
                           tw, t_rhs, b.free)
                    b.free = [acp(dst[:, i, n0:n0 + n], b.t[:, 0:n], t)]
                    yield
                s.free = [t]
                n0 += n

        rt_ = [R_[:, 96 * j:96 * j + 96] for j in range(3)]
        rt2 = [R_[:, 288 + 8 * j:288 + 8 * j + 8] for j in range(3)]
        rt3 = [R_[:, 312 + 8 * j:312 + 8 * j + 8] for j in range(3)]

        def all_rows(b, tiles, src, t, n, eps, b2):
            x, r, a_ = (z[:, 0:2] for z in rt2)
            t = mm([(b.t[:, i:i + 1], src[:, k, 128 * i:128 * i + 128], c("ones")[:, 0:1], k == tiles[0])
                    for i in range(2) for k in tiles], t, b.free, t_cst)
            t = ts(x, b.t[:, 0:2], 1.0 / n, eps, MUL, ADD, t, t_par)
            b.free = [t]
            t = root(x, r, a_, t)
            return mm([(b2.t[:, 128 * i:128 * i + 128], r[:, i:i + 1].broadcast_to([128, 128]), ident, True) for i in range(2)],
                      t, b2.free)

        def norm(key, tmp, bank, *af):
            t = act(tmp, X, ACT.Square, af, t_x, t_par)
            t = all_rows(bank, range(8), tmp, t, DM, EPS, bank)
            for k in range(8):
                t = stt(H[:, k, :], X[:, k, :], pc(key, k), bank.t[:, 0:T], MUL, MUL, t)
            bank.free = [t]
            return t

        def bsum(bank, src, n, lhs, *af):
            return mm([(bank.t[:, T * i:T * i + T], lhs, src[:, i, :], True) for i in range(n)], bank.free, af)

        def layernorm(y, bring, tmp, eps, across=False, tabs=None):
            b = bring()
            if across:
                f = lambda s_: [(b.t[:, T * i:T * i + T], c("ones"), s_[:, j, :], j == 0) for i in range(2) for j in range(2)]
                n = 256.0
            else:
                f = lambda s_: [(b.t[:, T * i:T * i + T], c("blk"), s_[:, i, :], True) for i in range(2)]
                n = 64.0
            t = mm(f(y), V_.ops[-1], Aq_.ops[-1], b.free)
            yield
            t = stt(y, two(b), -1.0 / n, y, MUL, ADD, t)
            b.free = [t]
            t = tt(tmp, y, y, MUL)
            b, b2 = bring(), bring()
            if across:
                t = all_rows(b, range(2), tmp, t, 256, eps, b2)
                yield
                f_ = b2.t[:, 0:T].unsqueeze(1).broadcast_to([128, 2, T])
            else:
                t = sums(table(b, 2), [tmp[:, i, :] for i in range(2)], t, b.free)
                yield
                r, t = factors(b, tabs, 2, 64, eps, t)
                t = spread(b2, r, (0, 1), t)
                yield
                f_ = two(b2)
            t = tt(y, y, f_, MUL, t)
            b2.free = [t]

        def sigm(x, out, *af):
            t = half_tanh(out, x, *af)
            return ts(out, out, 0.5, 0.5, MUL, ADD, t)

        def rwkv(l, pz, lora, BT, ar, bring):
            p = ar(8, T)
            d = ar(8, T)
            ar.at -= 16 * T
            Gm = ar(4, 4, 256, p=64)
            Ym = ar(4, 4, 64, p=64)
            t = tt(d, pz[:, :, 0:T], pz[:, :, 1:T + 1], SUB, last())
            for i in range(8):
                t = stt(p[:, i, :], d[:, i, :], pc(f"mu{l}", i), pz[:, i, 1:T + 1], MUL, ADD)
            r, k, v = p[:, 0:2, :], p[:, 2:4, :], p[:, 4:6, :]
            t = act(p[0:64, 6, :], p[0:64, 6, :], ACT.Tanh, t)
            b, b2 = bring(), bring()
            t_l = lora["t"]
            t1 = mm([(b.t[:, T * i:T * i + T], lora["w"][:, 128 * i:128 * i + 128], p[:, 6, :], True) for i in range(2)], t, b.free, t_l)
            t2 = mm([(b2.t[:, T * i:T * i + T], lora["a"][:, 128 * i:128 * i + 128], p[:, 6, :], True) for i in range(2)], b2.free)
            yield
            nb = ar(4)
            t = ts(nb[:, 0:2], P_[:, poff[f"w0{l}"][0]:poff[f"w0{l}"][0] + 2], 0.5, None, MUL)
            t = ts(nb[:, 2:4], P_[:, poff[f"a0{l}"][0]:poff[f"a0{l}"][0] + 2], 0.5, None, MUL)
            sig, aa, cum, kk, tmp, tm2, gg = (ar(2, T) for _ in range(7))
            for i in range(2):
                tb = half_tanh(sig[:, i, :], two(b)[:, i, :], t1, t, bias=nb[:, i:i + 1])
            b.free = [tb]
            for i in range(2):
                tb2 = half_tanh(aa[:, i, :], two(b2)[:, i, :], t2, t, bias=nb[:, 2 + i:3 + i])
            b2.free = [tb2]
            ts(sig, sig, 0.5, 0.5, MUL, ADD, tb)
            ts(aa, aa, 0.5, 0.5, MUL, ADD, tb2)
            t = sigm(p[:, 7, :], tmp[:, 0, :])
            b = bring()
            tg = mm([(b.t[:, T * i:T * i + T], lora["g"][:, 128 * i:128 * i + 128], tmp[:, 0, :], True) for i in range(2)], t, b.free)
            b.free = [acp(gg, two(b), tg)]
            yield
            for i in range(2):
                t = V(lambda e, i=i: e.tensor_tensor_scan(cum[:, i, :], c("rst"), sig[:, i, :], 0.0, MUL, ADD))
            Pp, Pi, Pm = ar(2, T), ar(2, T), ar(2, T)
            t1 = act(Pp, cum, ACT.Exp, t, scale=-RWS)
            t2 = act(Pi, cum, ACT.Exp, scale=RWS)
            t = tt(cum, cum, sig, SUB, t2)
            t3 = act(Pm, cum, ACT.Exp, t, scale=-RWS)
            for i in range(2):
                ts(kk[:, i, :], k[:, i, :], pc(f"kk{l}", i), None, MUL)
            t = tt(tmp, kk, kk, MUL, tg)
            b = bring()
            t = sums(table(b, 2), [tmp[:, i, :] for i in range(2)], t, b.free)
            yield
            r_, t = factors(b, rt3, 2, 1, 0, t, floor=1e-24)
            b = bring()
            t = spread(b, r_, (0, 1), t)
            yield
            t = tt(kk, kk, two(b), MUL, t)
            b.free = [t]
            om = ar(2)
            ts(om, P_[:, poff[f"ka{l}"][0]:poff[f"ka{l}"][0] + 2], -1.0, 1.0, MUL, ADD)
            for i in range(2):
                ts(tmp[:, i, :], aa[:, i, :], pc(f"ka{l}", i), om[:, i:i + 1], MUL, ADD)
            tt(k, k, tmp, MUL)
            AR = ar(2, 4, 2, 64)
            ch = lambda a_: a_.rearrange("p t (c n) -> p t c n", c=4)
            for i in range(2):
                tt(AR[:, i, :, 0, :], ch(kk)[:, i], ch(Pm)[:, i], MUL, t3)
                t_ar = tt(AR[:, i, :, 1, :], ch(r)[:, i], ch(Pp)[:, i], MUL, t1)
            be, ka = sig, aa
            bz, kz = ar(2, 2, T), ar(2, 2, T)
            mset(bz, 0.0)
            tz = mset(kz, 0.0)
            tt(be, kk, aa, MUL)
            tt(be, be, Pi, MUL)
            t = tt(ka, k, Pi, MUL)
            for s_, z in ((be, bz), (ka, kz)):
                for q in range(2):
                    tzz = acp(z[64 * q:64 * q + 64, q, :, :], s_[64 * q:64 * q + 64, :, :], t, tz)
            yield
            for i in range(2):
                t_b = stt(tmp[:, i, :], r[:, i, :], pc(f"rk{l}", i), k[:, i, :], MUL, MUL)
            bon = tm2
            b = bring()
            t_b = bsum(b, tmp, 2, c("blk"), t_b)
            pzf = pz.rearrange("p a b -> p (a b)")
            tok = [ar(4, 256, p=64)] + [pzf[0:64, 1024 * j:1024 * j + 1024].rearrange("p (a b) -> p a b", a=4) for j in range(2)]
            b.free = [tt(bon, two(b), v, MUL, t_b)]
            for s_, dst in zip((v, be, ka), tok):
                for q in range(2):
                    b = bring()
                    t = tr([(b.t[0:64, 256 * j + 128 * i:256 * j + 128 * i + 128], s_[:, i, 64 * (2 * q + j):64 * (2 * q + j) + 64], ident)
                            for j in range(2) for i in range(2)], t_b, b.free, V_.ops[-1])
                    t_tok = acp(dst[:, 2 * q:2 * q + 2, :], b.t[0:64, :].rearrange("p (a n) -> p a n", a=2), t)
                    b.free = [t_tok]
                    yield
            vt, bt, kt = tok
            rwm = c("rwm", 64).unsqueeze(1).broadcast_to([64, 2, 256])
            for q in range(4):
                for h2 in range(2):
                    b = bring()
                    items = []
                    for hh in range(2):
                        h = 2 * h2 + hh
                        for s_, z in ((0, bz), (1, kz)):
                            o = 256 * hh + 128 * s_
                            items.append((b.t[0:64, o:o + 128], z[:, h % 2, h // 2, 64 * q:64 * q + 64],
                                          AR[:, h // 2, q, :, :], True))
                    t = mm(items, tzz, t_ar, b.free)
                    t = tt(Gm[:, q, 2 * h2:2 * h2 + 2, :], b.t[0:64, :].rearrange("p (a n) -> p a n", a=2), rwm, MUL, t)
                    b.free = [t]
                    yield
            eye = c("id", 64)[:, 0:64].unsqueeze(1).broadcast_to([64, 16, 64])
            m3 = lambda a_: a_.rearrange("p a b c -> p (a b) c")
            t_i = V(lambda e: e.tensor_copy(m3(Ym), eye))
            h8 = lambda a_: a_.rearrange("p a b -> p (a b)")[0:64, :].rearrange("p (a b) -> p a b", a=8)
            Xh, Th, Ah = h8(sig), h8(Pi), h8(Pm)
            b3 = lambda b_: b_.t[0:64, :].rearrange("p (a n) -> p a n", a=8)
            for hf in range(2):
                sl = slice(8 * hf, 8 * hf + 8)
                Yh = m3(Ym)[:, sl, :]
                t_i = V(lambda e: e.tensor_copy(Xh, eye[:, 0:8, :]))
                for lv in range(6):
                    o = coff["lvl"][0] + 64 * lv
                    msk = C_[0:64, o:o + 64].unsqueeze(1).broadcast_to([64, 8, 64])
                    t_a = tt(Ah, m3(Gm)[:, sl, 0:64], msk, MUL, t_i, E=G)
                    b = bring()
                    t = mm([(b.t[0:64, 64 * j:64 * j + 64], Ah[:, j, :], Xh[:, j, :], True) for j in range(8)], t_a, t_i, b.free)
                    yield
                    t = acp(Th, b3(b), t)
                    b.free = [t]
                    bx, by = bring(), bring()
                    tx = mm([(bx.t[0:64, 64 * j:64 * j + 64], Yh[:, j, :], Th[:, j, :], True) for j in range(8)], t, bx.free)
                    ty = mm([(by.t[0:64, 64 * j:64 * j + 64], Th[:, j, :], Yh[:, j, :], True) for j in range(8)], by.free)
                    yield
                    bx.free = [tt(Xh, Xh, b3(bx), SUB, tx, ty)]
                    t_i = tt(Yh, Yh, b3(by), SUB, ty)
                    by.free = [t_i]
            S = ar(2, 128)
            W, U = tmp[0:64, 0, :], tmp[0:64, 1, :]
            y = cum
            t_s = None
            for q in range(4):
                b = bring()
                items = []
                for i in range(2):
                    if q:
                        items.append((b.t[0:64, 128 * i:128 * i + 128], AR[:, i, q, 0, :], S[:, i, :], True))
                    for h in (2 * i, 2 * i + 1):
                        items.append((b.t[0:64, 64 * h:64 * h + 64], Gm[:, q, h, 128:192], vt[:, q, 64 * h:64 * h + 64], not q))
                t = mm(items, t_s, t_tok, t_i, V_.ops[-1], b.free)
                yield
                t = acp(W, b.t[0:64, 0:256], t, V_.ops[-1], scale=-1.0)
                b.free = [t]
                b = bring()
                t = mm([(b.t[0:64, 64 * h:64 * h + 64], Ym[:, q, h, :], W[:, 64 * h:64 * h + 64], True) for h in range(4)], t, b.free)
                yield
                t_u = acp(U, b.t[0:64, 0:256], t)
                b.free = [t_u]
                b = bring()
                items = []
                for i in range(2):
                    if q:
                        items.append((b.t[:, 64 * i:64 * i + 64], S[:, i, :], AR[:, i, q, 1, :], True))
                    for hh in range(2):
                        h = 2 * i + hh
                        o = b.t[64 * hh:64 * hh + 64, 64 * i:64 * i + 64]
                        items.append((o, U[:, 64 * h:64 * h + 64], Gm[:, q, h, 64:128], not q))
                        items.append((o, vt[:, q, 64 * h:64 * h + 64], Gm[:, q, h, 192:256], False))
                t = mm(items, t_u, b.free)
                b.free = [acp(y[:, :, 64 * q:64 * q + 64], b.t[:, 0:128].rearrange("p (t n) -> p t n", t=2), t)]
                if q < 3:
                    b = bring()
                    items = []
                    for i in range(2):
                        o = b.t[:, 128 * i:128 * i + 128]
                        items.append((o, bt[:, q, 128 * i:128 * i + 128], U[:, 128 * i:128 * i + 128], True))
                        items.append((o, kt[:, q, 128 * i:128 * i + 128], vt[:, q, 128 * i:128 * i + 128], False))
                    t = mm(items, b.free)
                    yield
                    ps = b.t[:, 0:256].rearrange("p (t n) -> p t n", t=2)
                    if q:
                        t = tt(S, S, ps, ADD, t)
                        ps = S
                    for i in range(2):
                        t = stt(S[:, i, :], ps[:, i, :], Pp[:, i, 64 * q + 63:64 * q + 64], c("blk"), MUL, MUL, t)
                    t_s = t
                    b.free = [t]
            yield from layernorm(y, bring, tmp, 64e-5, tabs=rt3)
            for i in range(2):
                ts(y[:, i, :], y[:, i, :], pc(f"lw{l}", i), pc(f"lb{l}", i), MUL, ADD)
            tt(y, y, bon, ADD)
            BT["t"] = tt(BT["v"], y, gg, MUL)

        def kq(b, kzp, par_, i, q):
            return [(b.t[:, 0:256], kzp[:, par_, i, 0:128], q[:, i, :], True),
                    (b.t[:, 256:384], kzp[:, par_, i, 128:256], q[:, i, 128:256], False)]

        def av(b, h, v, at):
            o = b.t[64 * (h % 2):64 * (h % 2) + 64, :]
            return [(o[:, 0:256], v[:, 0, 64 * h:64 * h + 64], at[:, 0:256], True),
                    (o[:, 128:256], v[:, 1, 64 * h:64 * h + 64], at[:, 256:384], False)]

        def stick(l, qk, v, BT, ar, bring):
            tmp, kz, q = ar(4, T), ar(2, 2, T), ar(2, T)
            tz = mset(kz, 0.0)
            t = tt(tmp, qk, qk, MUL, last())
            b = bring()
            t = sums(table(b, 4), [tmp[:, i, :] for i in range(4)], t, b.free)
            yield
            r_, t = factors(b, rt_, 4, 64, EPS, t)
            bq, bk = bring(), bring()
            t1 = spread(bq, r_, (0, 1), t)
            t2 = spread(bk, r_, (2, 3))
            yield
            for i in range(2):
                t = stt(q[:, i, :], qk[:, i, :], pc(f"sq{l}"), two(bq)[:, i, :], MUL, MUL, t1)
            bq.free = [t]
            ts(q, q, 0.125, None, MUL)
            for i in range(2):
                for z in range(2):
                    h = slice(64 * z, 64 * z + 64)
                    t_k = stt(kz[h, z, i, :], qk[h, 2 + i, :], pc(f"sk{l}", 0, 64 * z, 64 * z + 64), two(bk)[h, i, :], MUL, MUL, tz, t2)
            bk.free = [t_k]
            u = [tmp.rearrange("p a b -> p (a b)")[:, 0:384], tmp.rearrange("p a b -> p (a b)")[:, 512:896]]
            w_ = [ar(384), ar(384)]
            ends = [None, None]
            for h in range(4):
                m = h % 2
                if m == 0:
                    bo = bring()
                b = bring()
                t = mm(kq(b, kz, m, h // 2, q), t_k, b.free)
                yield
                z = b.t[:, 0:384]
                act(u[m], z, ACT.Abs, t, t_k, ends[m])
                act(u[m], u[m], ACT.Exp, scale=-1.0)
                t = act(u[m], u[m], ACT.Ln, bias=1.0)
                t = stt(u[m], z, 0.0, u[m], MAX, ADD, t)
                for o in (0, 256):
                    t = tt(u[m][:, o:o + 128], u[m][:, o:o + 128], c("sb01"), MUL)
                t = mm([(b.t[:, 0:256], c("rneg"), u[m][:, 0:256], False),
                        (b.t[:, 256:384], c("rneg"), u[m][:, 256:384], False),
                        (b.t[:, 128:256], c("nones"), u[m][:, 256:384], False)], t)
                yield
                t = tt(w_[m], z, c("sbadd"), ADD, t, ends[m])
                b.free = [t]
                t = act(w_[m], w_[m], ACT.Exp, t)
                t = mm(av(bo, h, v, w_[m]), t, bo.free)
                ends[m] = t
                if m == 1:
                    bo.free = [acp(BT["v"][:, h // 2, :], bo.t[:, 0:256], t)]
                    BT["t"] = bo.free[0]
                yield

        def rotate(src, n, perm, cos, sin, bring, tmp, tm2, dst, *af):
            for i in range(0, n, 2):
                b = bring()
                s_ = src[:, i:i + 2, :]
                t = mm([(b.t[:, T * j:T * j + T], c(perm), s_[:, j, :], True) for j in range(2)], b.free, af)
                bc = lambda k_: c(k_).unsqueeze(1).broadcast_to([128, 2, T])
                tt(tmp, s_, bc(cos), MUL, af)
                t = tt(tm2, two(b), bc(sin), MUL, t)
                b.free = [t]
                dst(i, tmp, tm2)
                yield

        def retention(l, qk, g, v, BT, ar, bring):
            tmp, tm2, kz, q = ar(2, T), ar(2, T), ar(2, 2, T), ar(2, T)
            tz = mset(kz, 0.0)
            tok = {}

            def dst(i, a_, b_):
                if i == 0:
                    tok["q"] = tt(q, a_, b_, ADD)
                else:
                    for z in range(2):
                        h = slice(64 * z, 64 * z + 64)
                        tok["k"] = tt(kz[h, z, :, :], a_[h], b_[h], ADD, tz)
            yield from rotate(qk, 4, "pr", "cr", "sr", bring, tmp, tm2, dst, last())
            o0 = coff["dec"][0]
            y = qk[:, 0:2, :]
            u = [a_.rearrange("p a b -> p (a b)")[:, 0:384] for a_ in (tmp, tm2)]
            ends = [None, None]
            for h in range(4):
                m = h % 2
                if m == 0:
                    bo = bring()
                b = bring()
                t = mm(kq(b, kz, m, h // 2, q), tok["k"], tok["q"], b.free)
                yield
                d = C_[:, o0 + T * h:o0 + T * h + T]
                t1 = tt(u[m][:, 0:256], b.t[:, 0:256], d, MUL, t, ends[m])
                t = tt(u[m][:, 256:384], b.t[:, 256:384], d[:, 0:128], MUL)
                b.free = [t]
                t = mm(av(bo, h, v, u[m]), t, bo.free)
                ends[m] = t
                if m == 1:
                    bo.free = [acp(y[:, h // 2, :], bo.t[:, 0:256], t)]
                yield
            yield from layernorm(y, bring, tmp, 1e-5, tabs=rt_)
            for i in range(2):
                ts(y[:, i, :], y[:, i, :], pc(f"gn{l}", i), None, MUL)
            t = half_tanh(tmp, g, V_.ops[-1])
            one_plus(tmp, tmp, g, t)
            BT["t"] = stt(BT["v"], y, 0.5, tmp, MUL, MUL)

        def conformer(l, ab, BT, ar, bring):
            up, acc, e_ = ar(2, 286), ar(2, T), ar(2, T)
            tz = mset(up[:, :, 0:30], 0.0)
            t = sigm(ab[:, 2:4, :], e_, last())
            t = tt(up[:, :, 30:286], ab[:, 0:2, :], e_, MUL, tz)
            o = poff[f"dw{l}"][0]
            for i in range(2):
                ts(acc[:, i, :], up[:, i, 0:T], P_[:, o + 31 * i:o + 31 * i + 1], pc(f"cb{l}", i), MUL, ADD)
            for j in range(1, 31):
                for i in range(2):
                    stt(acc[:, i, :], up[:, i, j:j + T], P_[:, o + 31 * i + j:o + 31 * i + j + 1], acc[:, i, :], MUL, ADD)
                if j % 8 == 0:
                    yield
            yield from layernorm(acc, bring, e_, 1e-5, across=True)
            for i in range(2):
                t = ts(acc[:, i, :], acc[:, i, :], pc(f"cw{l}", i), pc(f"cl{l}", i), MUL, ADD)
            t = half_tanh(e_, acc, t)
            one_plus(e_, e_, acc, t)
            BT["t"] = ts(BT["v"], e_, 0.5, None, MUL)

        def merge(l, i, BT, M, e_, bring, first):
            sB, wB, tB = load(w["w_branch"][l, i])
            for u in range(2):
                s, wv, tw = load(w["w_gate"][l, i][:, 512 * u:512 * u + 512])
                for j in range(2):
                    f0 = 4 * u + 2 * j
                    b, b2 = bring(), bring()
                    t = mm([(b.t[:, T * q:T * q + T], wv[:, k, 256 * j + 128 * q:256 * j + 128 * q + 128], H[:, k, :], k == 0)
                            for q in range(2) for k in range(8)], tw, b.free)
                    s.free = [t]
                    t2 = mm([(b2.t[:, T * q:T * q + T], wB[:, k, 128 * (f0 + q):128 * (f0 + q) + 128], BT["v"][:, k, :], k == 0)
                             for q in range(2) for k in range(2)], tB, BT["t"], b2.free)
                    sB.free = [t2]
                    e = e_()
                    t = half_tanh(e["v"], two(b), t, e["t"])
                    b.free = [t]
                    tm = one_plus(e["v"], e["v"], two(b2), t, t2)
                    b2.free = [tm]
                    Mo = M[:, f0:f0 + 2, :]
                    if first:
                        tm = ts(Mo, e["v"], 0.5, None, MUL)
                    else:
                        tm = stt(Mo, e["v"], 0.5, Mo, MUL, ADD)
                    e["t"] = tm
                    yield

        def residual(b, f0, nt, t):
            return [tt(X[:, f0:f0 + nt, :], X[:, f0:f0 + nt, :], two(b)[:, 0:nt, :], ADD, t)]

        def mix_block(l):
            barrier()
            ar = Arena(0, ARENA)
            pz = ar(8, T + 1)
            M = ar(8, T)
            BT = [dict(v=ar(2, T), t=None) for _ in range(2)]
            es = Ring([dict(v=ar(2, T), t=None) for _ in range(2)])
            lora = {k: ar(256) for k in "wag"}
            zt = [mset(pz[:, :, 0:1], 0.0), mset(lora["w"][64:128, :], 0.0), mset(lora["a"][0:64, :], 0.0)]
            f = fence.get(G_, []) + zt
            t1 = dma(SP, "l0", lambda e: e.dma_start(lora["w"][0:64, :], w["rw_w2"][l]), f)
            t2 = dma(SP, "l1", lambda e: e.dma_start(lora["a"][64:128, :], w["rw_a2"][l]), f)
            t3 = dma(SP, "l2", lambda e: e.dma_start(lora["g"], w["rw_g2"][l]), f)
            lora["t"] = [t1, t2, t3]
            t_h = norm(f"nm{l}", M, banks[0], t_x, t_par, zt)
            W = w["w_in"][l]
            bulk, small = Ring(banks[0:4]), Ring(banks[4:8])

            def ev(b, f0, nt, t):
                return [acp(pz[:, f0:f0 + nt, 1:T + 1], two(b)[:, 0:nt, :], t)]
            for _ in proj(cols(W, 0, 1024), H, 8, bulk, ev, t_h):
                pass
            sub = Arena(ar.at, ar.at + 4864)
            rw_ar = Arena(sub.hi, ARENA)

            def others():
                sub.at = sub.lo
                qk, v = sub(4, T), sub(2, T)
                yield from proj([W[:, 1024:1536]], H, 8, bulk, to_sbuf(qk), t_h)
                yield from proj_tok([W[:, 1536:1792]], bulk, v, t_h)
                yield from stick(l, qk, v, BT[1], sub, bulk)
                yield from merge(l, 1, BT[1], M, es, bulk, True)
                sub.at = sub.lo
                f_ = last()
                qk, v, g = sub(4, T), sub(2, T), sub(2, T)
                barrier()
                yield from proj([W[:, 1792:2304]], H, 8, bulk, to_sbuf(qk), t_h)
                yield from proj_tok([W[:, 2304:2560]], bulk, v, t_h)
                yield from proj([W[:, 2560:2816]], H, 8, bulk, to_sbuf(g), t_h)
                yield from retention(l, qk, g, v, BT[1], sub, bulk)
                yield from merge(l, 2, BT[1], M, es, bulk, False)
                sub.at = sub.lo
                ab = sub(4, T)
                barrier()
                yield from proj([W[:, 2816:3328]], H, 8, bulk, to_sbuf(ab), t_h)
                yield from conformer(l, ab, BT[1], sub, bulk)
                yield from merge(l, 3, BT[1], M, es, bulk, False)

            run(others(), rwkv(l, pz, lora, BT[0], rw_ar, small))
            for _ in merge(l, 0, BT[0], M, es, bulk, False):
                pass
            for _ in proj(cols(w["w_out"][l], 0, 1024), M, 8, bulk, residual, last()):
                pass

        def swiglu(w1, w3, hid, nt, bring, es, t_h, gate=None):
            n = nt * 128
            for c0 in range(0, n, 512):
                c1 = min(c0 + 512, n)
                s1, v1, t1 = load(w1[:, c0:c1])
                s3, v3, t3 = load(w3[:, c0:c1])
                for j in range(0, c1 - c0, 256):
                    m = min(256, c1 - c0 - j) // 128
                    b, b2 = bring(), bring()
                    ta = mm([(b.t[:, T * q:T * q + T], v1[:, k, j + 128 * q:j + 128 * q + 128], H[:, k, :], k == 0)
                             for q in range(m) for k in range(8)], t1, t_h, b.free)
                    s1.free = [ta]
                    tb = mm([(b2.t[:, T * q:T * q + T], v3[:, k, j + 128 * q:j + 128 * q + 128], H[:, k, :], k == 0)
                             for q in range(m) for k in range(8)], t3, b2.free)
                    s3.free = [tb]
                    e = es()
                    ev = e["v"][:, 0:m, :]
                    t = half_tanh(ev, two(b)[:, 0:m, :], ta, e["t"])
                    t = one_plus(ev, ev, two(b)[:, 0:m, :], t)
                    b.free = [t]
                    f0 = (c0 + j) // 128
                    ho = hid[:, f0:f0 + m, :]
                    t = stt(ho, ev, 0.5, two(b2)[:, 0:m, :], MUL, MUL, tb)
                    e["t"] = t
                    b2.free = [t]
                    if gate is not None:
                        t = tt(ho, ho, gate.unsqueeze(1).broadcast_to([128, m, T]), MUL)
            return t

        def down(w2, hid, nt, acc, first, t_hid):
            for k0 in range(0, nt, 4):
                k1 = min(nt, k0 + 4)
                s, wv, tw = load(w2[128 * k0:128 * k1, :])
                items = []
                for k in range(k0, k1):
                    for d in range(8):
                        items.append((acc[d // 2].t[:, T * (d % 2):T * (d % 2) + T], wv[:, k - k0, 128 * d:128 * d + 128],
                                      hid[:, k, :], first and k == 0 and d % 2 == 0))
                t = mm(items, tw, t_hid, [b.free for b in acc] if first and k0 == 0 else None)
                s.free = [t]
            return t

        def add_acc(acc, t):
            for j in range(4):
                acc[j].free = [tt(X[:, 2 * j:2 * j + 2, :], X[:, 2 * j:2 * j + 2, :], two(acc[j]), ADD, t)]

        def ffn(l):
            barrier()
            ar = Arena(0, ARENA)
            tmp = ar(8, T)
            t_h = norm(f"nf{l}", tmp, banks[0], last())
            hid = ar(22, T)
            es = Ring([dict(v=ar(2, T), t=None) for _ in range(2)])
            t = swiglu(w["ffn_w1"][0], w["ffn_w3"][0], hid, 22, Ring(banks[0:4]), es, t_h)
            t = down(w["ffn_w2"][0], hid, 22, banks[4:8], True, t)
            add_acc(banks[4:8], t)

        def moe(l):
            barrier()
            ar = Arena(0, ARENA)
            tmp = ar(8, T)
            t_h = norm(f"nf{l}", tmp, banks[0], last())
            b = banks[0]
            o = poff["rt"][0]
            t = mm([(b.t[:, 8 * i:8 * i + 8], H[:, k, 128 * i:128 * i + 128], P_[:, o + 8 * k:o + 8 * k + 8], k == 0)
                    for i in range(2) for k in range(8)], t_h, b.free)
            lg, mx, gt, e1 = ar(2, 8), ar(2, 8), ar(2, 8), ar(2, 8)
            idx = ar(2, 8).bitcast(U32)
            fx, gs = ar(2, 8), ar(2, 8)
            t = cp(lg, b.t[:, 0:16].rearrange("p (i e) -> p i e", i=2), t)
            b.free = [t]
            for i in range(2):
                V(lambda e, i=i: e.max(mx[:, i, :], lg[:, i, :]))
                V(lambda e, i=i: e.max_index(idx[:, i, :], mx[:, i, :], lg[:, i, :]))
                cp(fx[:, i, :], idx[:, i, :])
                t = tt(gs[:, i, 0:1], mx[:, i, 1:2], mx[:, i, 0:1], SUB)
                t = act(gs[:, i, 0:1], gs[:, i, 0:1], ACT.Exp, t)
                ts(gs[:, i, 1:2], gs[:, i, 0:1], 1.0, None, ADD, None, t)
                recip(gs[:, i, 1:2], gs[:, i, 1:2])
                tt(gs[:, i, 2:3], gs[:, i, 0:1], gs[:, i, 1:2], MUL)
                ts(gt[:, i, :], c("iota"), fx[:, i, 0:1], gs[:, i, 1:2], ALU.is_equal, MUL)
                ts(e1[:, i, :], c("iota"), fx[:, i, 1:2], gs[:, i, 2:3], ALU.is_equal, MUL)
                t = tt(gt[:, i, :], gt[:, i, :], e1[:, i, :], ADD)
            gT = ar(T, p=8)
            b = banks[1]
            t = tr([(b.t[0:8, 128 * i:128 * i + 128], gt[:, i, :], ident) for i in range(2)], t, b.free)
            t_g = acp(gT, b.t[0:8, 0:T], t)
            b.free = [t_g]
            hids = [ar(11, T) for _ in range(2)]
            gbs = [ar(T) for _ in range(2)]
            es = Ring([dict(v=ar(2, T), t=None) for _ in range(2)])
            bring = Ring(banks[0:4])
            t_d = [None, None]
            pend = None
            for x in range(8):
                b = bring()
                t = mm([(b.t[:, 0:T], ident[0:8, x:x + 1].broadcast_to([8, 128]), gT, True)], t_g, b.free)
                gb = gbs[x % 2]
                t = acp(gb, b.t[:, 0:T], t, V_.ops[-1])
                b.free = [t]
                hid_free = t_d[x % 2]
                t = cp(hids[x % 2][:, 0, 0:1], gb[:, 0:1], t, hid_free)
                t = swiglu(w["moe_w1"][0, x], w["moe_w3"][0, x], hids[x % 2], 11, bring, es, t_h, gb)
                if pend is not None:
                    t_d[(x - 1) % 2] = down(*pend)
                pend = (w["moe_w2"][0, x], hids[x % 2], 11, banks[4:8], x == 0, t)
            t = down(*pend)
            add_acc(banks[4:8], t)

        def attend(cases, nk, es, bring, O, t_in):
            for (qs, keys, vals, o_dst, bo, first_o, last_o) in cases:
                e = es()
                wd = sum(k_.shape[1] for k_, _ in keys)
                at = 0
                bs = []
                tok = []
                b = None
                spans = []
                for k_, mk in keys:
                    n = k_.shape[1]
                    if b is None or at + n > 512:
                        b, at = bring(), 0
                        bs.append(b)
                    spans.append((b, at, n, mk))
                    at += n
                t = None
                for b in bs:
                    t = mm([(s_[0].t[:, s_[1]:s_[1] + s_[2]], qs[j], k_, True) for j, (s_, (k_, _)) in enumerate(zip(spans, keys)) if s_[0] is b],
                           t_in(), b.free)
                    tok.append(t)
                yield
                pos = 0
                for (b, a0, n, mk) in spans:
                    t = tt(e["v"][:, pos:pos + n], b.t[:, a0:a0 + n], mk, ADD, tok, e["t"])
                    b.free = [t]
                    pos += n
                t = V(lambda en, e=e, pos=pos: en.tensor_reduce(e["m"][:, 0:1], e["v"][:, 0:pos], AX.X, MAX))
                t = ts(e["m"][:, 1:2], e["m"][:, 0:1], -1.0, None, MUL)
                t = act(e["v"][:, 0:pos], e["v"][:, 0:pos], ACT.Exp, t, bias=e["m"][:, 1:2], acc=e["m"][:, 2:3])
                t_r = recip(e["m"][:, 3:4], e["m"][:, 2:3], t)
                blk = pos // 128
                pt = []
                for j0 in range(0, blk, 4):
                    j1 = min(blk, j0 + 4)
                    b = bring()
                    tp = tr([(b.t[:, 128 * (j - j0):128 * (j - j0) + 128], e["v"][:, 128 * j:128 * j + 128], ident) for j in range(j0, j1)], t, b.free)
                    pt.append(acp(e["p"][:, 128 * j0:128 * j1], b.t[:, 0:128 * (j1 - j0)], tp, e["t"]))
                    b.free = [pt[-1]]
                yield
                to = mm([(bo.t[:, 0:64], e["p"][:, 128 * j:128 * j + 128], vals[j], j == 0) for j in range(blk)], pt, bo.free)
                t = ts(o_dst, bo.t[:, 0:64], e["m"][:, 3:4], None, MUL, None, to, t_r)
                bo.free = [t]
                e["t"] = t
                yield

        def qk_factors(raw, n, bring, tmp, half):
            b = bring()
            ends = [None, None]
            for j in range(n):
                m = j % 2
                t = tt(tmp[m][:, 0, :], raw[:, j, :], raw[:, j, :], MUL, Aq_.ops[-1], ends[m])
                ends[m] = mm([(table(b, n)[:, i, j, :], tmp[m][:, 0, 128 * i:128 * i + 128], c("blk")[:, 0:65:64], True)
                              for i in range(2)], t, b.free)
            r, t = factors(b, rt_, n, 64, EPS, ends)
            t = ts(r[:, :, 0:half, :], r[:, :, 0:half, :], 0.125, None, MUL)
            return r, t

        def qk_ready(raw, js, rs, t_rs, key, tmps, bring, out):
            for q, j in enumerate(js):
                tmp, tm2, un = (tmps[3 * (q % 2) + z][:, 0, :] for z in range(3))
                b = bring()
                t = spread(b, rs, [j], t_rs)
                t = stt(un, raw[:, j, :], pc(key), b.t[:, 0:T], MUL, MUL, t)
                t2 = mm([(b.t[:, T:2 * T], c("pp"), un, True)], t)
                tt(tmp, un, c("cp"), MUL)
                t = tt(tm2, b.t[:, T:2 * T], c("sp"), MUL, t2)
                b.free = [t]
                t = out(q, tmp, tm2)
                yield
            qk_ready.t = t

        def softplus(x, a_, b_):
            t = act(a_, x, ACT.Abs, V_.ops[-1])
            act(a_, a_, ACT.Exp, scale=-1.0)
            t = act(a_, a_, ACT.Ln, bias=1.0)
            return stt(x, x, 0.0, a_, MAX, ADD, t)

        def even():
            barrier()
            W = w["even_w_in_2"][0]
            ar = Arena(0, ARENA)
            mixed = ar(12, T)
            t_h = norm("en", mixed[:, 0:8, :], banks[0], last())
            bulk = Ring(banks[0:8])
            xbc = ar(16, T)
            zs, dtT, dtm = ar(8, T), ar(T, p=16), ar(T, p=16)
            base = ar.at
            pad = Ring([dict(v=ar(2, T + 3), t=None) for _ in range(2)])
            acc = ar(2, T)
            tz = [mset(p_["v"][:, :, 0:3], 0.0) for p_ in pad.items]
            cw = poff["ecw"][0]

            def ev(b, f0, nt, t):
                p_ = pad()
                t = acp(p_["v"][:, 0:nt, 3:T + 3], two(b)[:, 0:nt, :], t, tz, p_["t"])
                for i in range(nt):
                    f = f0 + i
                    ts(acc[:, i, :], p_["v"][:, i, 0:T], P_[:, cw + 4 * f:cw + 4 * f + 1], pc("ecb", f), MUL, ADD, t)
                    for j in range(1, 4):
                        u = stt(acc[:, i, :], p_["v"][:, i, j:j + T], P_[:, cw + 4 * f + j:cw + 4 * f + j + 1], acc[:, i, :], MUL, ADD)
                p_["t"] = u
                xo = xbc[:, f0:f0 + nt, :]
                u = half_tanh(xo, acc[:, 0:nt, :], u)
                one_plus(xo, xo, acc[:, 0:nt, :], u)
                ts(xo, xo, 0.5, None, MUL)
                return [t]
            for _ in proj(cols(W, 1024, 3072), H, 8, bulk, ev, t_h):
                pass

            def evd(b, f0, nt, t):
                return [acp(dtT, b.t[0:16, 0:T], t)]
            for _ in proj([W[:, 3072:3088]], H, 8, bulk, evd, t_h):
                pass
            for _ in proj(cols(W, 0, 1024), H, 8, bulk, to_sbuf(zs), t_h):
                pass
            t = ts(dtT, dtT, pc("edt", 0, 0, 16), None, ADD, None, Aq_.ops[-1])
            softplus(dtT, dtm, None)
            nA = ar(1, p=16)
            t = act(nA, pc("eal", 0, 0, 16), ACT.Exp)
            ts(nA, nA, -1.0, None, MUL, None, t)
            ts(dtm, dtT, nA, None, MUL)
            cs = ar(T, p=16)
            t = V(lambda e: e.tensor_tensor_scan(cs, c("ones", 16)[:, 0:1].broadcast_to([16, T]), dtm, 0.0, MUL, ADD))
            b = bulk()
            tokd = ar(2, 2, 16)
            t = tr([(b.t[:, 16 * (2 * s_ + i):16 * (2 * s_ + i) + 16], src[:, 128 * i:128 * i + 128], ident[0:16, 0:16])
                    for s_, src in enumerate((dtT, cs)) for i in range(2)], t, b.free)
            t_dt = cp(tokd, b.t[:, 0:64].rearrange("p (s i h) -> p s i h", s=2, i=2), t)
            b.free = [t_dt]
            xd = ar(2, 1024)
            for i in range(2):
                for f0 in (0, 4):
                    b = bulk()
                    t = tr([(b.t[:, 128 * j:128 * j + 128], xbc[:, f0 + j, 128 * i:128 * i + 128], ident) for j in range(4)], V_.ops[-1], b.free)
                    t = tt(xd[:, i, 128 * f0:128 * f0 + 512].rearrange("p (h n) -> p h n", n=64),
                           b.t[:, :].rearrange("p (h n) -> p h n", n=64),
                           tokd[:, 0, i, 2 * f0:2 * f0 + 8].unsqueeze(2).broadcast_to([128, 8, 64]), MUL, t)
                    b.free = [t]
            t_xd = t
            cbm = ar(384)
            us = [ar(384), ar(384)]
            mask = c("ssd")
            ends = [None, None]
            for g in range(4):
                Bt, Ct = xbc[:, 8 + g, :], xbc[:, 12 + g, :]
                b = bulk()
                t = mm([(b.t[:, 0:256], Bt[:, 0:128], Ct, True), (b.t[:, 256:384], Bt[:, 128:256], Ct[:, 128:256], True)], V_.ops[-1], b.free)
                tt(cbm[:, 0:256], b.t[:, 0:256], mask, MUL, t)
                t = tt(cbm[:, 256:384], b.t[:, 256:384], mask[:, 0:128], MUL)
                b.free = [t]
                for hh in range(4):
                    h = 4 * g + hh
                    m = h % 2
                    b = bulk()
                    t = mm([(b.t[:, 0:T], ident[0:16, h:h + 1].broadcast_to([16, 128]), cs, True)], t_dt, b.free)
                    u = us[m]
                    ts(u[:, 0:256], b.t[:, 0:256], tokd[:, 1, 0, h:h + 1], 0.0, SUB, MIN, t, ends[m])
                    t = ts(u[:, 256:384], b.t[:, 128:256], tokd[:, 1, 1, h:h + 1], 0.0, SUB, MIN)
                    b.free = [t]
                    t = act(u, u, ACT.Exp, t)
                    t = tt(u, u, cbm, MUL, t)
                    if m == 0:
                        bo = bulk()
                    o = bo.t[64 * m:64 * m + 64, :]
                    t = mm([(o[:, 0:256], xd[:, 0, 64 * h:64 * h + 64], u[:, 0:256], True),
                            (o[:, 128:256], xd[:, 1, 64 * h:64 * h + 64], u[:, 256:384], False)], t, bo.free, t_xd)
                    ends[m] = t
                    if m == 1:
                        f = h // 2
                        t = stt(mixed[:, f, :], xbc[:, f, :], pc("eds", f), bo.t[:, 0:T], MUL, ADD, t)
                        bo.free = [t]
            t = half_tanh(xbc[:, 0:8, :], zs, t)
            one_plus(zs, xbc[:, 0:8, :], zs, t)
            stt(mixed[:, 0:8, :], mixed[:, 0:8, :], 0.5, zs, MUL, MUL)
            t = tt(zs, mixed[:, 0:8, :], mixed[:, 0:8, :], MUL)
            for g in range(4):
                b, b2 = bulk(), bulk()
                t2 = all_rows(b, range(2 * g, 2 * g + 2), zs, t, 256, EPS, b2)
                for j in range(2):
                    f = 2 * g + j
                    u = stt(mixed[:, f, :], mixed[:, f, :], pc("esn", f), b2.t[:, 0:T], MUL, MUL, t2)
                b2.free = [u]
            barrier()
            ar.at = 12 * T
            raw = ar(24, T)
            v = ar(2, 1536)
            g_ = ar(4, T)
            for _ in proj(cols(W, 3088, 6160), H, 8, bulk, to_sbuf(raw), t_h):
                pass
            for _ in proj_tok(cols(W, 6160, 7696), bulk, v, t_h):
                pass
            for _ in proj([W[:, 7696:8208]], H, 8, bulk, to_sbuf(g_), t_h):
                pass
            o_tok = ar(2, 512)
            tmps = [ar(1, T) for _ in range(6)]
            qz = [ar(2, 3, T) for _ in range(2)]
            kd = [ar(3, T) for _ in range(2)]
            tz = [mset(q, 0.0) for q in qz][-1]
            es = Ring([dict(v=ar(768), p=ar(768), m=ar(4), t=None) for _ in range(2)])
            dm = c("dil").rearrange("p (g n) -> p g n", g=3)
            br = Ring(banks[0:6])
            rs, t_rs = qk_factors(raw, 24, br, tmps[0:2], 12)
            bos = Ring(banks[6:8])
            fr = [None, None]
            for hp in range(4):
                z = hp % 2
                fr_ = [Aq_.ops[-1], fr[z]]

                def oq(q, a_, b_):
                    for y_ in range(2):
                        h = slice(64 * y_, 64 * y_ + 64)
                        t = tt(qz[z][h, y_, q, :], a_[h], b_[h], ADD, tz, fr_)
                    return t
                for _ in qk_ready(raw, [4 * g + hp for g in range(3)], rs, t_rs, "eqn", tmps, br, oq):
                    pass
                for _ in qk_ready(raw, [12 + 4 * g + hp for g in range(3)], rs, t_rs, "ekn", tmps, br,
                                  lambda q, a_, b_: tt(kd[z][:, q, :], a_, b_, ADD, fr_)):
                    pass
                t_q = qk_ready.t
                cases = []
                for hh in range(2):
                    h = 2 * hp + hh
                    for i in range(2):
                        keys, vals, qs = [], [], []
                        for g in range(3):
                            n = 128 * (i + 1)
                            keys.append((kd[z][:, g, 0:n], dm[:, g, 256 - n:256]))
                            qs.append(qz[z][:, hh, g, 128 * i:128 * i + 128])
                            vals += [v[:, j, 64 * (8 * g + h):64 * (8 * g + h) + 64] for j in range(i + 1)]
                        cases.append((qs, keys, vals, o_tok[:, i, 64 * h:64 * h + 64], bos(), 0, 0))
                for _ in attend(cases, 0, es, br, None, lambda t_q=t_q: t_q):
                    pass
                fr[z] = PE_.ops[-1]
            oT = mixed[:, 8:12, :]
            for i in range(2):
                b = br()
                t = tr([(b.t[:, 128 * j:128 * j + 128], o_tok[:, i, 128 * j:128 * j + 128], ident) for j in range(4)], V_.ops[-1], b.free)
                t = acp(oT[:, :, 128 * i:128 * i + 128], b.t[:, :].rearrange("p (j n) -> p j n", j=4), t)
                b.free = [t]
            t2 = half_tanh(raw[:, 0:4, :], g_)
            one_plus(raw[:, 0:4, :], raw[:, 0:4, :], g_, t2)
            t = stt(oT, oT, 0.5, raw[:, 0:4, :], MUL, MUL)
            out_proj(w["even_w_out_2"][0], mixed, 12, t)

        def out_proj(W, src, nt, t):
            t = down(W, src, nt, banks[4:8], True, last())
            add_acc(banks[4:8], t)

        def odd():
            barrier()
            W = w["odd_w_in_2"][0]
            ar = Arena(0, ARENA)
            raw = ar(16, T)
            t_h = norm("on", raw[:, 0:8, :], banks[0], last())
            bulk = Ring(banks[0:8])
            for _ in proj(cols(W, 0, 2048), H, 8, bulk, to_sbuf(raw), t_h):
                pass
            v, g_ = ar(2, 1024), ar(8, T)
            for _ in proj_tok(cols(W, 2048, 3072), bulk, v, t_h):
                pass
            for _ in proj(cols(W, 3072, 4096), H, 8, bulk, to_sbuf(g_), t_h):
                pass
            o_tok = ar(2, 1024)
            tmps = [ar(1, T) for _ in range(6)]
            qz = [ar(2, 1, T) for _ in range(2)]
            kd = [ar(1, T) for _ in range(2)]
            tz = [mset(q, 0.0) for q in qz][-1]
            zero = ar(128)
            tz = mset(zero, 0.0)
            es = Ring([dict(v=ar(768), p=ar(768), m=ar(4), t=None) for _ in range(2)])
            dm = c("dil")
            br = Ring(banks[0:6])
            rs, t_rs = qk_factors(raw, 16, br, tmps[0:2], 8)
            bos = Ring(banks[6:8])
            fr = [None, None]
            for hp in range(8):
                z = hp % 2
                fr_ = [Aq_.ops[-1], fr[z]]

                def oq(q, a_, b_):
                    for y_ in range(2):
                        h = slice(64 * y_, 64 * y_ + 64)
                        t = tt(qz[z][h, y_, q, :], a_[h], b_[h], ADD, tz, fr_)
                    return t
                for _ in qk_ready(raw, [hp], rs, t_rs, "oqn", tmps, br, oq):
                    pass
                for _ in qk_ready(raw, [8 + hp], rs, t_rs, "okn", tmps, br, lambda q, a_, b_: tt(kd[z][:, q, :], a_, b_, ADD, fr_)):
                    pass
                t_q = qk_ready.t
                cases = []
                for hh in range(2):
                    h = 2 * hp + hh
                    for i in range(2):
                        keys = [(kd[z][:, 0, 128 * j:128 * j + 128], dm[:, 128:256] if j == i else zero) for j in range(i + 1)]
                        qs = [qz[z][:, hh, 0, 128 * i:128 * i + 128]] * (i + 1)
                        vals = [v[:, j, 64 * h:64 * h + 64] for j in range(i + 1)]
                        cases.append((qs, keys, vals, o_tok[:, i, 64 * h:64 * h + 64], bos(), 0, 0))
                for _ in attend(cases, 0, es, br, None, lambda t_q=t_q: t_q):
                    pass
                fr[z] = PE_.ops[-1]
            oT = ar(8, T)
            for i in range(2):
                for f0 in (0, 4):
                    b = br()
                    t = tr([(b.t[:, 128 * j:128 * j + 128], o_tok[:, i, 128 * (f0 + j):128 * (f0 + j) + 128], ident) for j in range(4)],
                           V_.ops[-1], b.free)
                    t = acp(oT[:, f0:f0 + 4, 128 * i:128 * i + 128], b.t[:, :].rearrange("p (j n) -> p j n", j=4), t)
                    b.free = [t]
            t2 = half_tanh(raw[:, 0:8, :], g_)
            one_plus(raw[:, 0:8, :], raw[:, 0:8, :], g_, t2)
            t = stt(oT, oT, 0.5, raw[:, 0:8, :], MUL, MUL)
            out_proj(w["odd_w_out_2"][0], oT, 8, t)

        mix_block(0)
        ffn(0)
        mix_block(1)
        moe(1)
        even()
        odd()
        t_out = dma(SP, "out", lambda e: e.dma_start(outT.rearrange("(t p) n -> p t n", p=128), X), last())
        SP(lambda e: e.nop(), t_out)
        number(engines)

        block = ctx.enter_context(nc.Block())
        for E, name in ((PE_, "tensor"), (V_, "vector"), (Aq_, "scalar"), (G_, "gpsimd"), (SP, "sync")):
            def body(e, E=E):
                E.run(e)
            {"tensor": block.tensor, "vector": block.vector, "scalar": block.scalar, "gpsimd": block.gpsimd,
             "sync": block.sync}[name](body)


_W = ["w_in", "rw_w2", "rw_a2", "rw_g2", "w_gate", "w_branch", "w_out", "ffn_w1", "ffn_w3", "ffn_w2", "moe_w1", "moe_w3",
      "moe_w2", "even_w_in_2", "even_w_out_2", "odd_w_in_2", "odd_w_out_2"]


def kernel(**inputs):
    import concourse.bacc as _bacc
    from concourse.bass_utils import run_bass_kernel_spmd as _run

    nc = _bacc.Bacc("TRN2", target_bir_lowering=False, num_devices=1)
    i = {k: np.asarray(v) for k, v in inputs.items()}
    arrays = {k: np.ascontiguousarray(i[k]) for k in _W}
    arrays["cst"], arrays["par"] = consts(), params(i)
    arrays["xT"] = np.ascontiguousarray(i["x"][0].T)
    h = {k: nc.dram_tensor(k, a.shape, F, kind="ExternalInput").ap() for k, a in arrays.items()}
    outT = nc.dram_tensor("outT", (DM, T), F, kind="ExternalOutput").ap()
    build(nc, {k: h[k] for k in _W}, h["cst"], h["par"], h["xT"], outT)
    r = _run(nc, [arrays], core_ids=[0])
    return np.ascontiguousarray(r.results[0]["outT"].T)[None]
```

```python
import concourse.bass as bass
from concourse import mybir
from contextlib import ExitStack
import numpy as np

F = mybir.dt.float32
U32 = mybir.dt.uint32
I32 = mybir.dt.int32
R = mybir.dt.float32r
ALU = mybir.AluOpType
ACT = mybir.ActivationFunctionType
AX = mybir.AxisListType

T = 256
DM = 1024
EPS = 1e-6
RWS = 0.606531
NEG = -1.0e30
RAW = 4
PARTS = 3
AHEAD = 2
SLOT = 2048
ARENA = 22024

PARAM_COLS = []
for _l in range(2):
    PARAM_COLS += [(f"nm{_l}", 8), (f"nf{_l}", 8), (f"mu{_l}", 8), (f"w0{_l}", 2), (f"a0{_l}", 2), (f"kk{_l}", 2),
                   (f"ka{_l}", 2), (f"rk{_l}", 2), (f"lw{_l}", 2), (f"lb{_l}", 2), (f"sq{_l}", 1), (f"sk{_l}", 1),
                   (f"gn{_l}", 2), (f"dw{_l}", 62), (f"cb{_l}", 2), (f"cw{_l}", 2), (f"cl{_l}", 2)]
PARAM_COLS += [("rt", 64), ("en", 8), ("ecw", 64), ("ecb", 16), ("edt", 1), ("eal", 1), ("eds", 8), ("esn", 8),
               ("eqn", 1), ("ekn", 1), ("on", 8), ("oqn", 1), ("okn", 1)]
CONSTS = {
    "c0": [("id", 128), ("blk", 128), ("ones", 128), ("iota", 8)],
    "c1": [("nones", 128), ("pr", 128), ("cr", 256), ("sr", 256), ("dec", 1024), ("rneg", 128), ("sbadd", 384),
           ("sb01", 128), ("rwm", 256), ("lvl", 384), ("rst", 256)],
    "c2": [("pp", 128), ("cp", 256), ("sp", 256), ("dil", 768), ("ssd", 256)],
}


def offsets(cols):
    out, n = {}, 0
    for k, w in cols:
        out[k] = (n, w)
        n += w
    return out, n


def consts():
    C = {g: np.zeros((128, offsets(cols)[1]), np.float32) for g, cols in CONSTS.items()}
    where = {k: (g, o, w) for g, cols in CONSTS.items() for k, (o, w) in offsets(cols)[0].items()}

    def put(k, a):
        g, o, w = where[k]
        C[g][:a.shape[0], o:o + w] = a.reshape(a.shape[0], w)

    i = np.arange(128)
    put("id", np.eye(128))
    put("blk", (i[:, None] // 64 == i[None, :] // 64) * 1.0)
    put("ones", np.ones((128, 128)))
    put("nones", -np.ones((128, 128)))
    for key, half, width in (("pr", 32, 64), ("pp", 8, 16)):
        m = np.zeros((128, 128))
        for b in (0, 64):
            for j in range(half):
                m[b + j + half, b + j] = -1.0
                m[b + j, b + j + half] = 1.0
        put(key, m)
    t = np.arange(T, dtype=np.float32)
    inv = np.float32(10000.0) ** (-np.arange(0, 64, 2, dtype=np.float32) / np.float32(64))
    ang = (t[None, :] * inv[:, None]).astype(np.float32)
    put("cr", np.tile(np.cos(ang), (4, 1)))
    put("sr", np.tile(np.sin(ang), (4, 1)))
    inv = np.float32(500000.0) ** (-np.arange(8, dtype=np.float32) * np.float32(2.0) / np.float32(16))
    ang = (t[None, :] * inv[:, None]).astype(np.float32)
    c, s = np.ones((64, T)), np.zeros((64, T))
    c[0:16] = np.tile(np.cos(ang), (2, 1))
    s[0:16] = np.tile(np.sin(ang), (2, 1))
    put("cp", np.tile(c, (2, 1)))
    put("sp", np.tile(s, (2, 1)))
    dec = np.zeros((128, 4, T))
    rel = np.arange(T)[None, :] - i[:, None]
    for h in range(4):
        lg = np.log(1.0 - 2.0 ** (-5.0 - h))
        dec[:, h] = np.where(rel >= 0, np.exp(np.maximum(rel, 0) * lg), 0.0) * 0.125
    put("dec", dec)
    put("rneg", (i[:, None] >= i[None, :]) * -1.0)
    lt = i[:, None] < i[None, :]
    d = np.where(lt, 0.0, NEG)
    put("sbadd", np.concatenate([d, np.zeros((128, 128)), d], 1))
    put("sb01", lt * 1.0)
    dil = np.zeros((128, 3, 256))
    dist = i[:, None] + 128 - np.arange(256)[None, :]
    for g, (w, r) in enumerate(((128, 1), (512, 4), (2048, 16))):
        ok = (dist >= 0) & (dist <= w) & (dist % r == 0)
        dil[:, g] = np.where(ok, 0.0, NEG)
    put("dil", dil)
    put("ssd", (np.arange(256)[None, :] >= i[:, None]) * 1.0)
    j = np.arange(64)
    st, inc = (j[:, None] < j[None, :]) * 1.0, (j[:, None] <= j[None, :]) * 1.0
    put("rwm", np.tile(np.concatenate([st, inc, st, inc], 1), (2, 1)))
    lvl = np.zeros((64, 6, 64))
    for v in range(6):
        b = 1 << v
        lvl[:, v] = (j[:, None] // (2 * b) == j[None, :] // (2 * b)) & (j[:, None] % (2 * b) < b) & (j[None, :] % (2 * b) >= b)
    put("lvl", np.tile(lvl, (2, 1, 1)))
    put("rst", np.tile((np.arange(T) % 64 != 0) * 1.0, (128, 1)))
    put("iota", np.tile(np.arange(8), (128, 1)) * 1.0)
    return C


def col(a):
    return a.reshape(-1, 128).T


def params(i):
    P = {}
    for l in range(2):
        P[f"nm{l}"], P[f"nf{l}"], P[f"mu{l}"] = col(i["norm_mix"][l]), col(i["norm_ffn"][l]), col(i["rw_mu"][l])
        for k, n in (("w0", "rw_w0"), ("a0", "rw_a0"), ("kk", "rw_k_k"), ("ka", "rw_k_a"), ("rk", "rw_r_k"),
                     ("lw", "rw_ln_w"), ("lb", "rw_ln_b"), ("gn", "ret_gn"), ("cb", "conv_b"), ("cw", "conv_ln_w"),
                     ("cl", "conv_ln_b")):
            P[f"{k}{l}"] = col(i[n][l].reshape(-1))
        P[f"sq{l}"], P[f"sk{l}"] = col(np.tile(i["sb_q_norm"][l], 2)), col(np.tile(i["sb_k_norm"][l], 2))
        P[f"dw{l}"] = i["conv_dw"][l].reshape(31, 2, 128).transpose(2, 1, 0).reshape(128, 62)
    P["rt"] = i["router"][0].reshape(8, 128, 8).transpose(1, 0, 2).reshape(128, 64)
    P["en"], P["on"] = col(i["even_norm_w_2"][0]), col(i["odd_norm_w_2"][0])
    P["ecw"] = i["even_conv_w_2"][0].reshape(16, 128, 4).transpose(1, 0, 2).reshape(128, 64)
    P["ecb"], P["esn"] = col(i["even_conv_b_2"][0]), col(i["even_ssd_norm_w_2"][0])
    P["edt"], P["eal"] = i["even_dt_bias_2"][0].reshape(16, 1), i["even_a_log_2"][0].reshape(16, 1)
    P["eds"] = col(np.repeat(i["even_d_skip_2"][0], 64))
    for k, n in (("eqn", "even_q_norm_2"), ("ekn", "even_k_norm_2"), ("oqn", "odd_q_norm_2"), ("okn", "odd_k_norm_2")):
        P[k] = col(np.tile(i[n][0], 2))
    off, n = offsets(PARAM_COLS)
    out = np.zeros((128, n), np.float32)
    for k, (o, w) in off.items():
        out[:P[k].shape[0], o:o + w] = P[k]
    return out


class Op:

    def __init__(self, eng, fn, after, sem=None, val=0):
        self.eng, self.fn, self.after, self.sem, self.val = eng, fn, after, sem, val
        self.count = 0
        self.signals = sem is not None


def flat(a):
    if a is None:
        return []
    return [o for x in a for o in flat(x)] if isinstance(a, (list, tuple)) else [a]


class Stream:

    def __init__(self, engines=()):
        self.prev = {E: E.ops[-1] for E in engines if E.ops}
        self.fence = {}


class Engine:

    def __init__(self, name, done, chained, log, cur):
        self.name, self.done, self.chained, self.ops, self.log, self.cur = name, done, chained, [], log, cur

    def __call__(self, fn, *after):
        st = self.cur[0]
        after = flat(after) + flat(st.fence.pop(self, None))
        if self.chained and self in st.prev:
            after = after + [st.prev[self]]
        op = self.insert(fn, *after)
        st.prev[self] = op
        return op

    def insert(self, fn, *after):
        op = Op(self, fn, flat(after))
        self.ops.append(op)
        self.log.append(op)
        return op

    def run(self, e):
        seen = {}
        for op in self.ops:
            need = {}
            for o in op.after:
                k, v = (o.sem, o.val) if o.sem is not None else (o.eng.done, o.count)
                need[k.name] = max(need.get(k.name, (0, None))[0], v), k
            for name, (v, k) in need.items():
                if v > seen.get(name, 0):
                    seen[name] = v
                    e.wait_ge(k, v)
            ins = op.fn(e)
            if op.sem is not None:
                ins.then_inc(op.sem, 16)
            elif op.signals:
                ins.then_inc(self.done, 1)


def number(engines):
    for E in engines:
        for op in E.ops:
            for o in op.after:
                if o.sem is None:
                    o.signals = True
    for E in engines:
        n = 0
        for op in E.ops:
            if op.sem is None and op.signals:
                n += 1
                op.count = n


class Bank:
    def __init__(self, t):
        self.t, self.free = t, []


class Ring:
    def __init__(self, items):
        self.items, self.n = items, 0

    def __call__(self):
        self.n += 1
        return self.items[(self.n - 1) % len(self.items)]


def build(nc, w, cst, par, xT, outT):
    ctx = ExitStack()
    with ctx:
        def sb(name, n, p=128, dt=F):
            return ctx.enter_context(nc.sbuf_tensor("s_" + name, [p, n], dt))

        def sem(name):
            return ctx.enter_context(nc.semaphore(name))

        where = {k: (g, o, n) for g, cols_ in CONSTS.items() for k, (o, n) in offsets(cols_)[0].items()}
        poff, pn = offsets(PARAM_COLS)
        CT = {"c0": sb("c0", offsets(CONSTS["c0"])[1])}
        CT["c1"] = CT["c2"] = sb("c1", offsets(CONSTS["c1"])[1])
        P_ = sb("par", pn)
        X_, ring_ = sb("X", 2048), sb("ring", RAW * SLOT)
        Hh_, Hl_, wh_, wl_ = (sb(k, n, dt=R) for k, n in (("Hh", 2048), ("Hl", 2048), ("wh", PARTS * SLOT), ("wl", PARTS * SLOT)))
        R_ = sb("roots", 336)
        base = nc.sbuf_base
        A_ = sb("arena", ARENA)
        Z_ = nc.alloc_sbuf_tensor_at("s_arena_r", [128, ARENA], R, offset=base)
        banks = [Bank(ctx.enter_context(nc.psum_tensor(f"b{i}", [128, 512], F))) for i in range(8)]
        log, cur = [], [Stream()]
        PE, V, A, G, SP = (Engine(n, sem("done_" + n), n in "VAG", log, cur) for n in ("PE", "V", "A", "G", "SP"))
        engines = [PE, V, A, G, SP]

        def c(k, p=128, p0=0):
            g, o, n = where[k]
            return CT[g][p0:p0 + p, o:o + n]

        def pc(k, j=0, p0=0, p1=128):
            o, n = poff[k]
            return P_[p0:p1, o + j:o + j + 1]

        X = X_[:, :].rearrange("p (t n) -> p t n", n=T)
        H = tuple(h[:, :].rearrange("p (t n) -> p t n", n=T) for h in (Hh_, Hl_))

        dma_sems = {}

        def dma(eng, key, fn, *after):
            if key not in dma_sems:
                dma_sems[key] = [sem("dma_" + key), 0]
            s, n = dma_sems[key]
            dma_sems[key][1] = n + 16
            op = eng.insert(fn, after)
            op.sem, op.val, op.signals = s, n + 16, True
            return op

        t_par = dma(SP, "par", lambda e: e.dma_start(P_[:, :], par))
        t_cst = dma(SP, "c0", lambda e: e.dma_start(CT["c0"][:, :], cst["c0"]))
        t_x = dma(SP, "x", lambda e: e.dma_start(X, xT.rearrange("(t p) n -> p t n", p=128)))

        t_c1 = dma(SP, "c1", lambda e: e.dma_start(CT["c1"][:, :], cst["c1"]))

        class Slot:
            def __init__(self, i):
                self.i, self.free = i, []
        raws, parts = Ring([Slot(i) for i in range(RAW)]), Ring([Slot(i) for i in range(PARTS)])
        marks = []

        def load(src):
            k, n = src.shape
            kt = k // 128
            s, q = raws(), parts()
            raw = ring_[:, s.i * SLOT:s.i * SLOT + kt * n]
            t = dma(SP, f"w{s.i}", lambda e: e.dma_start(raw.rearrange("p (k n) -> p k n", k=kt), src.rearrange("(k p) n -> p k n", p=128)), s.free)
            hi, lo = (z[:, q.i * SLOT:q.i * SLOT + kt * n] for z in (wh_, wl_))
            marks.append({E: E.insert(None) for E in (Aq_, V_, G_)})
            N = len(marks) - 1
            early.append((N, raw, hi, lo, t, q.free, s))
            c_ = [Op(None, None, []), Op(None, None, [])]
            early[-1] += (c_,)
            q.free, s.free = [], [c_[1]]
            return q, tuple(z.rearrange("p (k n) -> p k n", k=kt) for z in (hi, lo)), c_

        early = []

        def place_splits():
            jobs = {}
            for N, raw, hi, lo, t, free, s_, c_ in early:
                m = marks[max(0, N - AHEAD)]
                E = G_ if N % 3 == 1 else V_
                c_[0].eng, c_[0].fn, c_[0].after = Aq_, (lambda e, hi=hi, raw=raw: e.activation(hi, raw, ACT.Copy)), flat([t, free])
                c_[1].eng, c_[1].after = E, flat([t, free, c_[0]])
                c_[1].fn = lambda e, hi=hi, raw=raw, lo=lo: e.tensor_tensor(lo, raw, hi.bitcast(F), ALU.subtract)
                jobs.setdefault(id(m[Aq_]), []).append(c_[0])
                jobs.setdefault(id(m[E]), []).append(c_[1])
            for E in (Aq_, V_, G_):
                E.ops = [o for op in E.ops for o in (jobs.get(id(op), []) if op.fn is None else [op])]
            for o, nxt in zip(G_.ops, G_.ops[1:]):
                nxt.after = nxt.after + [o]

        def pairs(W, X_):
            return ((W[0], X_[0]), (W[0], X_[1]), (W[1], X_[0]))

        def mm3(out, W, X_, start):
            return [(out, a_, b_, start and z == 0) for z, (a_, b_) in enumerate(pairs(W, X_))]

        def cut(P2, f):
            return tuple(f(z) for z in P2)

        def split(P2, v, *af, E=None):
            t = act(P2[0], v, ACT.Copy, af)
            return tt(P2[1], v, P2[0].bitcast(F), SUB, t, E=E)

        def tt(out, a, b, op, *af, E=None):
            return (E or V)(lambda e: e.tensor_tensor(out, a, b, op), *af)

        def ts(out, a, s1, s2, o0, o1=None, *af, E=None):
            if o1 is None:
                return (E or V)(lambda e: e.tensor_scalar(out, a, s1, None, o0), *af)
            return (E or V)(lambda e: e.tensor_scalar(out, a, s1, s2, o0, o1), *af)

        def stt(out, a, s, b, o0, o1, *af):
            return V(lambda e: e.scalar_tensor_tensor(out=out, in0=a, scalar=s, in1=b, op0=o0, op1=o1), *af)

        def cp(out, a, *af):
            return V(lambda e: e.tensor_copy(out, a), *af)

        def act(out, a, f, *af, bias=0.0, scale=1.0, acc=None):
            kw = dict(bias=bias, scale=scale)
            if acc is not None:
                kw["accum_out"] = acc
            return A(lambda e: e.activation(out, a, f, **kw), *af)

        def acp(out, a, *af, scale=1.0):
            return A(lambda e: e.activation(out, a, ACT.Copy, scale=scale), *af)

        def root(x, y, a_, t, scale=1.0):
            V(lambda e: e.tensor_scalar(y.bitcast(I32), x.bitcast(I32), 1, None, ALU.logical_shift_right), t)
            V(lambda e: e.tensor_scalar(y.bitcast(I32), y.bitcast(I32), -1.0, 1597463007.0, MUL, ADD))
            for i in range(3):
                stt(a_, y, -0.5, y, MUL, MUL)
                tt(a_, a_, x, MUL)
                t = stt(y, a_, 1.5, y, ADD, MUL)
            return t if scale == 1.0 else ts(y, y, scale, None, MUL)

        def sums(cols_, tiles, *af):
            return mm([(cols_[:, i, j, :], s_[:, 128 * i:128 * i + 128], c("blk")[:, 0:65:64], True)
                       for i in range(2) for j, s_ in enumerate(tiles)], af)

        def spread(b, rs, js, *af):
            return mm([(b.t[64 * h:64 * h + 64, T * q + 128 * i:T * q + 128 * i + 128], rs[:, i, j, h:h + 1].broadcast_to([128, 64]), ident, True)
                       for q, j in enumerate(js) for i in range(2) for h in range(2)], b.free, af)

        def factors(b, rs, n, wide, eps, t, scale=1.0, floor=None):
            r, x, a_ = (z[:, 0:4 * n] for z in rs)
            if floor is None:
                t = ts(x, b.t[:, 0:4 * n], 1.0 / wide, eps, MUL, ADD, t)
            else:
                t = ts(x, b.t[:, 0:4 * n], floor, None, MAX, None, t)
            b.free = [t]
            t = root(x, r, a_, t, scale)
            return r.rearrange("p (i j h) -> p i j h", i=2, h=2), t

        def table(b, n):
            return b.t[:, 0:4 * n].rearrange("p (i j h) -> p i j h", i=2, h=2)

        def half_tanh(out, x, *af, bias=0.0):
            return act(out, x, ACT.Tanh, *af, bias=bias, scale=0.5)

        def one_plus(out, th, x, *af):
            return stt(out, th, 1.0, x, ADD, MUL, *af)

        def recip(out, a, *af):
            return V(lambda e: e.reciprocal(out, a), *af)

        def mset(out, v, *af):
            return G(lambda e: e.memset(out, v), *af)

        def mm(items, *af):
            items = list(items)

            def f(e):
                for o, l, r, st in items:
                    x = e.matmul(o, l, r, start=st, stop=True, skip_group_check=True)
                return x
            return PE(f, *af)

        def tr(items, *af):
            items = list(items)

            def f(e):
                for o, i_, idn in items:
                    x = e.transpose(o, i_, idn)
                return x
            return PE(f, *af)

        MUL, ADD, SUB, MAX, MIN, POW = ALU.mult, ALU.add, ALU.subtract, ALU.max, ALU.min, ALU.pow
        ident = c("id")
        last = lambda: [E.ops[-1] for E in (PE, V, A, G) if E.ops]

        class Arena:
            def __init__(self, lo, hi):
                self.lo, self.hi, self.at = lo, hi, lo

            def __call__(self, *shape, p=128, dt=F):
                n = int(np.prod(shape))
                assert self.at + n <= self.hi, ("arena", self.at + n, self.hi)
                v = (A_ if dt is F else Z_)[0:p, self.at:self.at + n]
                self.at += n
                if len(shape) == 2:
                    v = v.rearrange("p (a b) -> p a b", a=shape[0])
                if len(shape) == 3:
                    v = v.rearrange("p (a b c) -> p a b c", a=shape[0], b=shape[1])
                top[0] = max(top[0], self.at)
                if len(shape) == 4:
                    v = v.rearrange("p (a b c d) -> p a b c d", a=shape[0], b=shape[1], c=shape[2])
                return v

        top = [0]

        def two_parts(ar, *shape):
            return ar(*shape, dt=R), ar(*shape, dt=R)

        PE_, V_, Aq_, G_ = PE, V, A, G
        last = lambda: [E.ops[-1] for E in (PE_, V_, Aq_, G_) if E.ops]

        def barrier():
            for E in (PE_, V_, Aq_, G_):
                cur[0].fence[E] = last()

        def run(*gens):
            parent = cur[0]
            gens = [(*(g if isinstance(g, tuple) else (g, 1)), Stream(engines[:4])) for g in gens]
            for g in gens:
                g[2].fence.update(parent.fence)
            parent.fence.clear()
            while gens:
                base = {E: len(E.ops) for E in engines}
                seqs = []
                for g in list(gens):
                    cur[0], n0 = g[2], len(log)
                    for _ in range(g[1]):
                        try:
                            next(g[0])
                        except StopIteration:
                            gens.remove(g)
                            break
                    seqs.append(log[n0:])
                left, order = {id(o) for s_ in seqs for o in s_}, []
                while left:
                    for s_ in seqs:
                        if s_ and not any(id(o) in left for o in s_[0].after):
                            o = s_.pop(0)
                            left.remove(id(o))
                            order.append(o)
                for E in engines:
                    E.ops[base[E]:] = [o for o in order if o.eng is E]
            cur[0] = parent
            parent.prev = {E: E.ops[-1] for E in engines[:4] if E.ops}

        def two(b):
            return b.t[:, :].rearrange("p (t n) -> p t n", t=2)

        def proj(src, rhs, nk, bring, evac, t_rhs):
            f0 = 0
            for s_ in src:
                s, wv, tw = load(s_)
                n = s_.shape[1]
                for j in range(0, n, 256):
                    b = bring()
                    m = min(256, n - j)
                    items = []
                    for i in range(0, m, 128):
                        for k in range(nk):
                            items += mm3(b.t[:, 2 * i:2 * i + 256], cut(wv, lambda z: z[:, k, j + i:j + i + 128]),
                                         cut(rhs, lambda z: z[:, k, :]), k == 0)
                    t = mm(items, tw, t_rhs, b.free)
                    s.free.append(t)
                    b.free = evac(b, f0, (m + 127) // 128, t)
                    f0 += (m + 127) // 128
                    yield

        def cols(W, c0, c1, step=256):
            return [W[:, i:min(i + step, c1)] for i in range(c0, c1, step)]

        def to_sbuf(dst, E="A"):
            def evac(b, f0, nt, t):
                o = dst[:, f0:f0 + nt, :]
                i = two(b)[:, 0:nt, :]
                return [acp(o, i, t)] if E == "A" else [cp(o, i, t)]
            return evac

        def proj_tok(src, bring, dst, t_rhs):
            n0 = 0
            for s_ in src:
                s, wv, tw = load(s_)
                n = s_.shape[1]
                for i in range(2):
                    b = bring()
                    t = mm([z for k in range(8) for z in mm3(b.t[:, 0:n], cut(H, lambda z: z[:, k, 128 * i:128 * i + 128]),
                                                             cut(wv, lambda z: z[:, k, :]), k == 0)], tw, t_rhs, b.free)
                    b.free = [acp(dst[:, i, n0:n0 + n], b.t[:, 0:n], t)]
                s.free = [t]
                yield
                n0 += n

        rt_ = [R_[:, 96 * j:96 * j + 96] for j in range(3)]
        rt2 = [R_[:, 288 + 8 * j:288 + 8 * j + 8] for j in range(3)]
        rt3 = [R_[:, 312 + 8 * j:312 + 8 * j + 8] for j in range(3)]

        def all_rows(b, tiles, src, t, n, eps, b2):
            x, r, a_ = (z[:, 0:2] for z in rt2)
            t = mm([(b.t[:, i:i + 1], src[:, k, 128 * i:128 * i + 128], c("ones")[:, 0:1], k == tiles[0])
                    for i in range(2) for k in tiles], t, b.free, t_cst)
            t = ts(x, b.t[:, 0:2], 1.0 / n, eps, MUL, ADD, t, t_par)
            b.free = [t]
            t = root(x, r, a_, t)
            return mm([(b2.t[:, 128 * i:128 * i + 128], r[:, i:i + 1].broadcast_to([128, 128]), ident, True) for i in range(2)],
                      t, b2.free)

        def norm(key, tmp, bank, *af):
            t = act(tmp, X, ACT.Square, af, t_x, t_par)
            t = all_rows(bank, range(8), tmp, t, DM, EPS, bank)
            for k in range(8):
                t = stt(tmp[:, k, :], X[:, k, :], pc(key, k), bank.t[:, 0:T], MUL, MUL, t)
            bank.free = [t]
            for k in range(0, 8, 4):
                t2 = split(cut(H, lambda z: z[:, k:k + 4, :]), tmp[:, k:k + 4, :], t, af)
            return t2

        def bsum(bank, src, n, lhs, *af):
            return mm([(bank.t[:, T * i:T * i + T], lhs, src[:, i, :], True) for i in range(n)], bank.free, af)

        def layernorm(y, bring, tmp, eps, across=False, tabs=None):
            b = bring()
            if across:
                f = lambda s_: [(b.t[:, T * i:T * i + T], c("ones"), s_[:, j, :], j == 0) for i in range(2) for j in range(2)]
                n = 256.0
            else:
                f = lambda s_: [(b.t[:, T * i:T * i + T], c("blk"), s_[:, i, :], True) for i in range(2)]
                n = 64.0
            t = mm(f(y), V_.ops[-1], Aq_.ops[-1], b.free)
            yield
            t = stt(y, two(b), -1.0 / n, y, MUL, ADD, t)
            b.free = [t]
            t = tt(tmp, y, y, MUL)
            b, b2 = bring(), bring()
            if across:
                t = all_rows(b, range(2), tmp, t, 256, eps, b2)
                yield
                f_ = b2.t[:, 0:T].unsqueeze(1).broadcast_to([128, 2, T])
            else:
                t = sums(table(b, 2), [tmp[:, i, :] for i in range(2)], t, b.free)
                yield
                r, t = factors(b, tabs, 2, 64, eps, t)
                t = spread(b2, r, (0, 1), t)
                yield
                f_ = two(b2)
            t = tt(y, y, f_, MUL, t)
            b2.free = [t]

        def sigm(x, out, *af):
            t = half_tanh(out, x, *af)
            return ts(out, out, 0.5, 0.5, MUL, ADD, t)

        def rwkv(l, pz, lora, BT, ar, bring):
            p = ar(8, T)
            ar.at -= 8 * T
            Gm = ar(2, 4, 256)
            Ym = ar(2, 4, 64)
            AR = ar(2, 4, 2, 64)
            at = bz_at = ar.at
            d = ar(8, T)
            ar.at = at
            bz, kz = ar(2, 2, T), ar(2, 2, T)
            t = tt(d, pz[:, :, 0:T], pz[:, :, 1:T + 1], SUB, last())
            for i in range(8):
                t = stt(p[:, i, :], d[:, i, :], pc(f"mu{l}", i), pz[:, i, 1:T + 1], MUL, ADD)
            r, k, v = p[:, 0:2, :], p[:, 2:4, :], p[:, 4:6, :]
            t = act(p[0:64, 6, :], p[0:64, 6, :], ACT.Tanh, t)
            b, b2 = bring(), bring()
            t_l = lora["t"]
            t1 = mm([(b.t[:, T * i:T * i + T], lora["w"][:, 128 * i:128 * i + 128], p[:, 6, :], True) for i in range(2)], t, b.free, t_l)
            t2 = mm([(b2.t[:, T * i:T * i + T], lora["a"][:, 128 * i:128 * i + 128], p[:, 6, :], True) for i in range(2)], b2.free)
            yield
            nb = ar(4)
            t = ts(nb[:, 0:2], P_[:, poff[f"w0{l}"][0]:poff[f"w0{l}"][0] + 2], 0.5, None, MUL)
            t = ts(nb[:, 2:4], P_[:, poff[f"a0{l}"][0]:poff[f"a0{l}"][0] + 2], 0.5, None, MUL)
            sig, aa, cum, kk, tmp, tm2, gg = (ar(2, T) for _ in range(7))
            for i in range(2):
                tb = half_tanh(sig[:, i, :], two(b)[:, i, :], t1, t, bias=nb[:, i:i + 1])
            b.free = [tb]
            for i in range(2):
                tb2 = half_tanh(aa[:, i, :], two(b2)[:, i, :], t2, t, bias=nb[:, 2 + i:3 + i])
            b2.free = [tb2]
            ts(sig, sig, 0.5, 0.5, MUL, ADD, tb)
            ts(aa, aa, 0.5, 0.5, MUL, ADD, tb2)
            t = sigm(p[:, 7, :], tmp[:, 0, :])
            b = bring()
            tg = mm([(b.t[:, T * i:T * i + T], lora["g"][:, 128 * i:128 * i + 128], tmp[:, 0, :], True) for i in range(2)], t, b.free)
            b.free = [acp(gg, two(b), tg)]
            yield
            for i in range(2):
                t = V(lambda e, i=i: e.tensor_tensor_scan(cum[:, i, :], c("rst"), sig[:, i, :], 0.0, MUL, ADD))
            Pp, Pi, Pm = ar(2, T), ar(2, T), ar(2, T)
            t1 = act(Pp, cum, ACT.Exp, t, scale=-RWS)
            t2 = act(Pi, cum, ACT.Exp, scale=RWS)
            t = tt(cum, cum, sig, SUB, t2)
            t3 = act(Pm, cum, ACT.Exp, t, scale=-RWS)
            for i in range(2):
                ts(kk[:, i, :], k[:, i, :], pc(f"kk{l}", i), None, MUL)
            t = tt(tmp, kk, kk, MUL, tg)
            b = bring()
            t = sums(table(b, 2), [tmp[:, i, :] for i in range(2)], t, b.free)
            yield
            r_, t = factors(b, rt3, 2, 1, 0, t, floor=1e-24)
            b = bring()
            t = spread(b, r_, (0, 1), t)
            yield
            t = tt(kk, kk, two(b), MUL, t)
            b.free = [t]
            om = ar(2)
            ts(om, P_[:, poff[f"ka{l}"][0]:poff[f"ka{l}"][0] + 2], -1.0, 1.0, MUL, ADD)
            for i in range(2):
                ts(tmp[:, i, :], aa[:, i, :], pc(f"ka{l}", i), om[:, i:i + 1], MUL, ADD)
            tt(k, k, tmp, MUL)
            ch = lambda a_: a_.rearrange("p t (c n) -> p t c n", c=4)
            for i in range(2):
                tt(AR[:, i, :, 0, :], ch(kk)[:, i], ch(Pm)[:, i], MUL, t3)
                t_ar = tt(AR[:, i, :, 1, :], ch(r)[:, i], ch(Pp)[:, i], MUL, t1)
            be, ka = sig, aa
            mset(bz, 0.0, t)
            tz = mset(kz, 0.0)
            tt(be, kk, aa, MUL)
            tt(be, be, Pi, MUL)
            t = tt(ka, k, Pi, MUL)
            for s_, z in ((be, bz), (ka, kz)):
                for q in range(2):
                    tzz = acp(z[64 * q:64 * q + 64, q, :, :], s_[64 * q:64 * q + 64, :, :], t, tz)
            yield
            for i in range(2):
                t_b = stt(tmp[:, i, :], r[:, i, :], pc(f"rk{l}", i), k[:, i, :], MUL, MUL)
            bon = tm2
            b = bring()
            t_b = bsum(b, tmp, 2, c("blk"), t_b)
            pzf = pz.rearrange("p a b -> p (a b)")
            tok = [pzf[:, 512 * j:512 * j + 512].rearrange("p (a b) -> p a b", a=2) for j in range(3)]
            b.free = [tt(bon, two(b), v, MUL, t_b)]
            for s_, dst in zip((v, be, ka), tok):
                b = bring()
                t = tr([(b.t[:, 256 * j + 128 * i:256 * j + 128 * i + 128], s_[:, i, 128 * j:128 * j + 128], ident)
                        for j in range(2) for i in range(2)], t_b, b.free, V_.ops[-1])
                t_tok = acp(dst, two(b), t)
                b.free = [t_tok]
                yield
            vt, bt, kt = tok
            for q in range(4):
                o = 64 * (q % 2)
                rwm = c("rwm", 64, o).unsqueeze(1).broadcast_to([64, 2, 256])
                for h2 in range(2):
                    b = bring()
                    items = []
                    for hh in range(2):
                        h = 2 * h2 + hh
                        for s_, z in ((0, bz), (1, kz)):
                            a0 = 256 * hh + 128 * s_
                            items.append((b.t[o:o + 64, a0:a0 + 128], z[:, h % 2, h // 2, 64 * q:64 * q + 64],
                                          AR[:, h // 2, q, :, :], True))
                    t = mm(items, tzz, t_ar, b.free)
                    t = tt(Gm[o:o + 64, q // 2, 2 * h2:2 * h2 + 2, :], b.t[o:o + 64, :].rearrange("p (a n) -> p a n", a=2), rwm, MUL, t)
                    b.free = [t]
                    yield
            m3 = lambda a_: a_.rearrange("p a b c -> p (a b) c")
            h8 = lambda a_: a_.rearrange("p a b -> p (a b)").rearrange("p (a b) -> p a b", a=8)
            Xm, Tm, Am = h8(sig), h8(Pi), h8(Pm)
            for hf in range(2):
                o = 64 * hf
                hs = slice(o, o + 64)
                b3 = lambda b_: b_.t[hs, :].rearrange("p (a n) -> p a n", a=8)
                eye = ident[hs, o:o + 64].unsqueeze(1).broadcast_to([64, 8, 64])
                Yh, Xh, Th, Ah = m3(Ym)[hs], Xm[hs], Tm[hs], Am[hs]
                cp(Yh, eye)
                t_i = cp(Xh, eye)
                for lv in range(6):
                    msk = c("lvl", 64, o)[:, 64 * lv:64 * lv + 64].unsqueeze(1).broadcast_to([64, 8, 64])
                    t_a = tt(Ah, m3(Gm)[hs, :, 0:64], msk, MUL, t_i, E=G)
                    b = bring()
                    t = mm([(b.t[hs, 64 * j:64 * j + 64], Ah[:, j, :], Xh[:, j, :], True) for j in range(8)], t_a, t_i, b.free)
                    yield
                    t = acp(Th, b3(b), t)
                    b.free = [t]
                    bx, by = bring(), bring()
                    tx = mm([(bx.t[hs, 64 * j:64 * j + 64], Yh[:, j, :], Th[:, j, :], True) for j in range(8)], t, bx.free)
                    ty = mm([(by.t[hs, 64 * j:64 * j + 64], Th[:, j, :], Yh[:, j, :], True) for j in range(8)], by.free)
                    yield
                    bx.free = [tt(Xh, Xh, b3(bx), SUB, tx, ty)]
                    t_i = tt(Yh, Yh, b3(by), SUB, ty)
                    by.free = [t_i]
            S = ar(2, 128)
            y = cum
            t_s = None
            for q in range(4):
                o, j = 64 * (q % 2), q // 2
                hs = slice(o, o + 64)
                W, U = tmp[hs, 0, :], tmp[hs, 1, :]
                g_ = lambda h, k_: Gm[hs, j, h, 64 * k_:64 * k_ + 64]
                b = bring()
                items = []
                for i in range(2):
                    if q:
                        items.append((b.t[hs, 128 * i:128 * i + 128], AR[:, i, q, 0, :], S[:, i, :], True))
                b2 = bring()
                t2 = mm([(b2.t[hs, 64 * h:64 * h + 64], g_(h, 2), vt[hs, j, 64 * h:64 * h + 64], True) for h in range(4)], t_tok, t_i, V_.ops[-1], b2.free)
                if q:
                    t = mm(items, t_s, b.free)
                yield
                t = acp(W, b2.t[hs, 0:256], t2, V_.ops[-1], PE_.ops[-1], scale=-1.0)
                b2.free = [t]
                if q:
                    t = tt(W, W, b.t[hs, 0:256], SUB, t, t_s, PE_.ops[-1])
                    b.free = [t]
                b = bring()
                t = mm([(b.t[hs, 64 * h:64 * h + 64], Ym[hs, j, h, :], W[:, 64 * h:64 * h + 64], True) for h in range(4)], t, b.free)
                yield
                t_u = acp(U, b.t[hs, 0:256], t)
                b.free = [t_u]
                b = bring()
                if q:
                    b2 = bring()
                    t2 = mm([(b2.t[:, 64 * i:64 * i + 64], S[:, i, :], AR[:, i, q, 1, :], True) for i in range(2)], b2.free, t_s)
                items = []
                for h in range(4):
                    po = b.t[64 * (h % 2):64 * (h % 2) + 64, 64 * (h // 2):64 * (h // 2) + 64]
                    items.append((po, U[:, 64 * h:64 * h + 64], g_(h, 1), True))
                    items.append((po, vt[hs, j, 64 * h:64 * h + 64], g_(h, 3), False))
                t = mm(items, t_u, b.free)
                yo = y[:, :, 64 * q:64 * q + 64]
                pv = lambda b_: b_.t[:, 0:128].rearrange("p (t n) -> p t n", t=2)
                b.free = [acp(yo, pv(b), t)]
                t_y = b.free
                if q < 3:
                    b = bring()
                    items = []
                    for i in range(2):
                        po = b.t[:, 128 * i:128 * i + 128]
                        items.append((po, bt[hs, j, 128 * i:128 * i + 128], U[:, 128 * i:128 * i + 128], True))
                        items.append((po, kt[hs, j, 128 * i:128 * i + 128], vt[hs, j, 128 * i:128 * i + 128], False))
                    t = mm(items, b.free)
                    yield
                    ps = b.t[:, 0:256].rearrange("p (t n) -> p t n", t=2)
                    if q:
                        t = tt(S, S, ps, ADD, t)
                        ps = S
                    for i in range(2):
                        t = stt(S[:, i, :], ps[:, i, :], Pp[:, i, 64 * q + 63:64 * q + 64], c("blk"), MUL, MUL, t)
                    t_s = t
                    b.free = [t]
                if q:
                    b2.free = [tt(yo, yo, pv(b2), ADD, t2, t_y)]
            yield from layernorm(y, bring, tmp, 64e-5, tabs=rt3)
            for i in range(2):
                ts(y[:, i, :], y[:, i, :], pc(f"lw{l}", i), pc(f"lb{l}", i), MUL, ADD)
            tt(y, y, bon, ADD)
            BT["t"] = tt(y, y, gg, MUL)
            BT["v"] = y
            BT["p"] = tuple(Z_[:, bz_at + 512 * j:bz_at + 512 * j + 512].rearrange("p (t n) -> p t n", n=T) for j in range(2))

        def kq(b, kzp, par_, i, q):
            return [(b.t[:, 0:256], kzp[:, par_, i, 0:128], q[:, i, :], True),
                    (b.t[:, 256:384], kzp[:, par_, i, 128:256], q[:, i, 128:256], False)]

        def av(b, h, v, at):
            o = b.t[64 * (h % 2):64 * (h % 2) + 64, :]
            return [(o[:, 0:256], v[:, 0, 64 * h:64 * h + 64], at[:, 0:256], True),
                    (o[:, 128:256], v[:, 1, 64 * h:64 * h + 64], at[:, 256:384], False)]

        def stick(l, qk, v, BT, ar, bring):
            tmp, kz, q = ar(4, T), ar(2, 2, T), ar(2, T)
            tz = mset(kz, 0.0)
            t = tt(tmp, qk, qk, MUL, last())
            b = bring()
            t = sums(table(b, 4), [tmp[:, i, :] for i in range(4)], t, b.free)
            yield
            r_, t = factors(b, rt_, 4, 64, EPS, t)
            bq, bk = bring(), bring()
            t1 = spread(bq, r_, (0, 1), t)
            t2 = spread(bk, r_, (2, 3))
            yield
            for i in range(2):
                t = stt(q[:, i, :], qk[:, i, :], pc(f"sq{l}"), two(bq)[:, i, :], MUL, MUL, t1)
            bq.free = [t]
            ts(q, q, 0.125, None, MUL)
            for i in range(2):
                for z in range(2):
                    h = slice(64 * z, 64 * z + 64)
                    t_k = stt(kz[h, z, i, :], qk[h, 2 + i, :], pc(f"sk{l}", 0, 64 * z, 64 * z + 64), two(bk)[h, i, :], MUL, MUL, tz, t2)
            bk.free = [t_k]
            u = [tmp.rearrange("p a b -> p (a b)")[:, 0:384], tmp.rearrange("p a b -> p (a b)")[:, 512:896]]
            w_ = [ar(384), ar(384)]
            ends = [None, None]
            for h in range(4):
                m = h % 2
                if m == 0:
                    bo = bring()
                b = bring()
                t = mm(kq(b, kz, m, h // 2, q), t_k, b.free)
                yield
                z = b.t[:, 0:384]
                act(u[m], z, ACT.Abs, t, t_k, ends[m])
                act(u[m], u[m], ACT.Exp, scale=-1.0)
                t = act(u[m], u[m], ACT.Ln, bias=1.0)
                t = stt(u[m], z, 0.0, u[m], MAX, ADD, t)
                for o in (0, 256):
                    t = tt(u[m][:, o:o + 128], u[m][:, o:o + 128], c("sb01"), MUL)
                t = mm([(b.t[:, 0:256], c("rneg"), u[m][:, 0:256], False),
                        (b.t[:, 256:384], c("rneg"), u[m][:, 256:384], False),
                        (b.t[:, 128:256], c("nones"), u[m][:, 256:384], False)], t)
                yield
                t = tt(w_[m], z, c("sbadd"), ADD, t, ends[m])
                b.free = [t]
                t = act(w_[m], w_[m], ACT.Exp, t)
                t = mm(av(bo, h, v, w_[m]), t, bo.free)
                ends[m] = t
                if m == 1:
                    bo.free = [acp(BT["v"][:, h // 2, :], bo.t[:, 0:256], t)]
                    BT["t"] = bo.free[0]
                yield

        def rotate(src, n, perm, cos, sin, bring, tmp, tm2, dst, *af):
            for i in range(0, n, 2):
                b = bring()
                s_ = src[:, i:i + 2, :]
                t = mm([(b.t[:, T * j:T * j + T], c(perm), s_[:, j, :], True) for j in range(2)], b.free, af)
                bc = lambda k_: c(k_).unsqueeze(1).broadcast_to([128, 2, T])
                tt(tmp, s_, bc(cos), MUL, af)
                t = tt(tm2, two(b), bc(sin), MUL, t)
                b.free = [t]
                dst(i, tmp, tm2)
                yield

        def retention(l, qk, g, v, BT, ar, bring):
            tmp, tm2, kz, q = ar(2, T), ar(2, T), ar(2, 2, T), ar(2, T)
            tz = mset(kz, 0.0)
            tok = {}

            def dst(i, a_, b_):
                if i == 0:
                    tok["q"] = tt(q, a_, b_, ADD)
                else:
                    for z in range(2):
                        h = slice(64 * z, 64 * z + 64)
                        tok["k"] = tt(kz[h, z, :, :], a_[h], b_[h], ADD, tz)
            yield from rotate(qk, 4, "pr", "cr", "sr", bring, tmp, tm2, dst, last())
            y = qk[:, 0:2, :]
            u = [a_.rearrange("p a b -> p (a b)")[:, 0:384] for a_ in (tmp, tm2)]
            ends = [None, None]
            for h in range(4):
                m = h % 2
                if m == 0:
                    bo = bring()
                b = bring()
                t = mm(kq(b, kz, m, h // 2, q), tok["k"], tok["q"], b.free)
                yield
                d = c("dec")[:, T * h:T * h + T]
                t1 = tt(u[m][:, 0:256], b.t[:, 0:256], d, MUL, t, ends[m])
                t = tt(u[m][:, 256:384], b.t[:, 256:384], d[:, 0:128], MUL)
                b.free = [t]
                t = mm(av(bo, h, v, u[m]), t, bo.free)
                ends[m] = t
                if m == 1:
                    bo.free = [acp(y[:, h // 2, :], bo.t[:, 0:256], t)]
                yield
            yield from layernorm(y, bring, tmp, 1e-5, tabs=rt_)
            for i in range(2):
                ts(y[:, i, :], y[:, i, :], pc(f"gn{l}", i), None, MUL)
            t = half_tanh(tmp, g, V_.ops[-1])
            one_plus(tmp, tmp, g, t)
            BT["t"] = stt(BT["v"], y, 0.5, tmp, MUL, MUL)

        def conformer(l, ab, BT, ar, bring):
            up, acc, e_ = ar(2, 286), ar(2, T), ar(2, T)
            tz = mset(up[:, :, 0:30], 0.0)
            t = sigm(ab[:, 2:4, :], e_, last())
            t = tt(up[:, :, 30:286], ab[:, 0:2, :], e_, MUL, tz)
            o = poff[f"dw{l}"][0]
            for i in range(2):
                ts(acc[:, i, :], up[:, i, 0:T], P_[:, o + 31 * i:o + 31 * i + 1], pc(f"cb{l}", i), MUL, ADD)
            for j in range(1, 31):
                for i in range(2):
                    stt(acc[:, i, :], up[:, i, j:j + T], P_[:, o + 31 * i + j:o + 31 * i + j + 1], acc[:, i, :], MUL, ADD)
                if j % 8 == 0:
                    yield
            yield from layernorm(acc, bring, e_, 1e-5, across=True)
            for i in range(2):
                t = ts(acc[:, i, :], acc[:, i, :], pc(f"cw{l}", i), pc(f"cl{l}", i), MUL, ADD)
            t = half_tanh(e_, acc, t)
            one_plus(e_, e_, acc, t)
            BT["t"] = ts(BT["v"], e_, 0.5, None, MUL)

        def merge(l, i, BT, M, e_, bring, first, MP=None):
            BP = BT["p"]
            tB_ = split(BP, BT["v"], BT["t"])
            for u in range(4):
                s, wv, tw = load(w["w_gate"][l, i][:, 256 * u:256 * u + 256])
                sB, wB, tB = load(w["w_branch"][l, i][:, 256 * u:256 * u + 256])
                f0 = 2 * u
                if f0 >= 0:
                    b, b2 = bring(), bring()
                    t = mm([z for q in range(2) for k in range(8) for z in
                            mm3(b.t[:, T * q:T * q + T], cut(wv, lambda z: z[:, k, 128 * q:128 * q + 128]), cut(H, lambda z: z[:, k, :]), k == 0)],
                           tw, b.free)
                    s.free = [t]
                    t2 = mm([z for q in range(2) for k in range(2) for z in
                             mm3(b2.t[:, T * q:T * q + T], cut(wB, lambda z: z[:, k, 128 * q:128 * q + 128]), cut(BP, lambda z: z[:, k, :]), k == 0)],
                            tB, tB_, b2.free)
                    sB.free = [t2]
                    e = e_()
                    t = half_tanh(e["v"], two(b), t, e["t"])
                    b.free = [t]
                    tm = one_plus(e["v"], e["v"], two(b2), t, t2)
                    b2.free = [tm]
                    Mo = M[:, f0:f0 + 2, :]
                    if first:
                        tm = ts(Mo, e["v"], 0.5, None, MUL)
                    else:
                        tm = stt(Mo, e["v"], 0.5, Mo, MUL, ADD)
                    if MP is not None:
                        tm = split(cut(MP, lambda z: z[:, f0:f0 + 2, :]), Mo, tm)
                    e["t"] = tm
                    yield

        def residual(b, f0, nt, t):
            return [tt(X[:, f0:f0 + nt, :], X[:, f0:f0 + nt, :], two(b)[:, 0:nt, :], ADD, t)]

        def mix_block(l):
            barrier()
            ar = Arena(0, ARENA)
            pz = ar(8, T + 1)
            M = ar(8, T)
            es = Ring([dict(v=ar(2, T), t=None) for _ in range(2)])
            BT = [dict(), dict(v=ar(2, T), t=None)]
            sub = Arena(ar.at, ar.at + 4864)
            rw_ar = Arena(sub.hi, ARENA)
            BT[1]["p"] = two_parts(Arena(sub.lo, sub.hi), 2, T)
            MP = two_parts(Arena(sub.lo, sub.hi), 8, T)
            la = Arena(sub.hi + 8 * T + 512, ARENA)
            lora = {k: la(256) for k in "wag"}
            zt = [mset(pz[:, :, 0:1], 0.0), mset(lora["w"][64:128, :], 0.0), mset(lora["a"][0:64, :], 0.0)]
            t1 = dma(Aq_, "l0", lambda e: e.dma_start(lora["w"][0:64, :], w["rw_w2"][l]), zt)
            t2 = dma(Aq_, "l1", lambda e: e.dma_start(lora["a"][64:128, :], w["rw_a2"][l]), zt)
            t3 = dma(Aq_, "l2", lambda e: e.dma_start(lora["g"], w["rw_g2"][l]), zt)
            lora["t"] = [t1, t2, t3]
            t_h = norm(f"nm{l}", M, banks[0], t_x, t_par, zt, t_c1)
            W = w["w_in"][l]
            bulk, small = Ring(banks[0:4]), Ring(banks[4:8])

            def ev(b, f0, nt, t):
                return [acp(pz[:, f0:f0 + nt, 1:T + 1], two(b)[:, 0:nt, :], t)]
            for _ in proj(cols(W, 0, 1024), H, 8, bulk, ev, t_h):
                pass

            def others():
                sub.at = sub.lo
                qk, v = sub(4, T), sub(2, T)
                yield from proj(cols(W, 1024, 1536), H, 8, bulk, to_sbuf(qk), t_h)
                yield from proj_tok([W[:, 1536:1792]], bulk, v, t_h)
                yield from stick(l, qk, v, BT[1], sub, bulk)
                yield from merge(l, 1, BT[1], M, es, bulk, True)
                sub.at = sub.lo
                qk, v, g = sub(4, T), sub(2, T), sub(2, T)
                barrier()
                yield from proj(cols(W, 1792, 2304), H, 8, bulk, to_sbuf(qk), t_h)
                yield from proj_tok([W[:, 2304:2560]], bulk, v, t_h)
                yield from proj([W[:, 2560:2816]], H, 8, bulk, to_sbuf(g), t_h)
                yield from retention(l, qk, g, v, BT[1], sub, bulk)
                yield from merge(l, 2, BT[1], M, es, bulk, False)
                sub.at = sub.lo
                ab = sub(4, T)
                barrier()
                yield from proj(cols(W, 2816, 3328), H, 8, bulk, to_sbuf(ab), t_h)
                yield from conformer(l, ab, BT[1], sub, bulk)
                yield from merge(l, 3, BT[1], M, es, bulk, False)

            run(others(), rwkv(l, pz, lora, BT[0], rw_ar, small))
            for _ in merge(l, 0, BT[0], M, es, bulk, False, MP):
                pass
            for _ in proj(cols(w["w_out"][l], 0, 1024), MP, 8, bulk, residual, last()):
                pass

        def swiglu(w1, w3, hid, nt, bring, es, t_h, gate=None, free=None):
            n = nt * 128
            t = None
            for c0 in range(0, n, 256):
                c1 = min(c0 + 256, n)
                s1, v1, t1 = load(w1[:, c0:c1])
                s3, v3, t3 = load(w3[:, c0:c1])
                m = (c1 - c0) // 128
                b, b2 = bring(), bring()
                ts_ = []
                for (bb, vv, tw, ss) in ((b, v1, t1, s1), (b2, v3, t3, s3)):
                    t = mm([z for q in range(m) for k in range(8) for z in
                            mm3(bb.t[:, T * q:T * q + T], cut(vv, lambda z: z[:, k, 128 * q:128 * q + 128]), cut(H, lambda z: z[:, k, :]), k == 0)],
                           tw, t_h, bb.free)
                    ss.free = [t]
                    ts_.append(t)
                e = es()
                ev = e["v"][:, 0:m, :]
                t = half_tanh(ev, two(b)[:, 0:m, :], ts_[0], e["t"])
                t = one_plus(ev, ev, two(b)[:, 0:m, :], t)
                b.free = [t]
                f0 = c0 // 128
                t = stt(ev, ev, 0.5, two(b2)[:, 0:m, :], MUL, MUL, ts_[1])
                b2.free = [t]
                if gate is not None:
                    t = tt(ev, ev, gate.unsqueeze(1).broadcast_to([128, m, T]), MUL)
                t = split(cut(hid, lambda z: z[:, f0:f0 + m, :]), ev, t, free)
                e["t"] = t
                yield t

        def down(w2, hid, nt, acc, first, t_hid):
            for k0 in range(0, nt, 2):
                k1 = min(nt, k0 + 2)
                s, wv, tw = load(w2[128 * k0:128 * k1, :])
                items = []
                for k in range(k0, k1):
                    for d in range(8):
                        items += mm3(acc[d // 2].t[:, T * (d % 2):T * (d % 2) + T], cut(wv, lambda z: z[:, k - k0, 128 * d:128 * d + 128]),
                                     cut(hid, lambda z: z[:, k, :]), first and k == 0 and d % 2 == 0)
                t = mm(items, tw, t_hid[k0 // 2], [b.free for b in acc] if first and k0 == 0 else None)
                s.free = [t]
                yield t

        def add_acc(acc, t):
            for j in range(4):
                acc[j].free = [tt(X[:, 2 * j:2 * j + 2, :], X[:, 2 * j:2 * j + 2, :], two(acc[j]), ADD, t)]

        def ffn(l):
            barrier()
            ar = Arena(0, ARENA)
            tmp = ar(8, T)
            t_h = norm(f"nf{l}", tmp, banks[0], last())
            hid = two_parts(ar, 22, T)
            es = Ring([dict(v=ar(2, T), t=None) for _ in range(2)])
            ts_ = []
            dn = down(w["ffn_w2"][0], hid, 22, banks[4:8], True, ts_)
            for n, t in enumerate(swiglu(w["ffn_w1"][0], w["ffn_w3"][0], hid, 22, Ring(banks[0:4]), es, t_h)):
                ts_.append(t)
                if n > 0:
                    next(dn)
            for t in dn:
                pass
            add_acc(banks[4:8], t)

        def moe(l):
            barrier()
            ar = Arena(0, ARENA)
            tmp = ar(8, T)
            t_h = norm(f"nf{l}", tmp, banks[0], last())
            b = banks[0]
            o = poff["rt"][0]
            rtp = two_parts(ar, 64)
            t = split(rtp, P_[:, o:o + 64])
            t = mm([z for i in range(2) for k in range(8) for z in
                    mm3(b.t[:, 8 * i:8 * i + 8], cut(H, lambda z: z[:, k, 128 * i:128 * i + 128]), cut(rtp, lambda z: z[:, 8 * k:8 * k + 8]), k == 0)],
                   t_h, t, b.free)
            lg, mx, gt, e1 = ar(2, 8), ar(2, 8), ar(2, 8), ar(2, 8)
            idx = ar(2, 8).bitcast(U32)
            fx, gs = ar(2, 8), ar(2, 8)
            t = cp(lg, b.t[:, 0:16].rearrange("p (i e) -> p i e", i=2), t)
            b.free = [t]
            for i in range(2):
                V(lambda e, i=i: e.max(mx[:, i, :], lg[:, i, :]))
                V(lambda e, i=i: e.max_index(idx[:, i, :], mx[:, i, :], lg[:, i, :]))
                cp(fx[:, i, :], idx[:, i, :])
                t = tt(gs[:, i, 0:1], mx[:, i, 1:2], mx[:, i, 0:1], SUB)
                t = act(gs[:, i, 0:1], gs[:, i, 0:1], ACT.Exp, t)
                ts(gs[:, i, 1:2], gs[:, i, 0:1], 1.0, None, ADD, None, t)
                recip(gs[:, i, 1:2], gs[:, i, 1:2])
                tt(gs[:, i, 2:3], gs[:, i, 0:1], gs[:, i, 1:2], MUL)
                ts(gt[:, i, :], c("iota"), fx[:, i, 0:1], gs[:, i, 1:2], ALU.is_equal, MUL)
                ts(e1[:, i, :], c("iota"), fx[:, i, 1:2], gs[:, i, 2:3], ALU.is_equal, MUL)
                t = tt(gt[:, i, :], gt[:, i, :], e1[:, i, :], ADD)
            gT = ar(T, p=8)
            b = banks[1]
            t = tr([(b.t[0:8, 128 * i:128 * i + 128], gt[:, i, :], ident) for i in range(2)], t, b.free)
            t_g = acp(gT, b.t[0:8, 0:T], t)
            b.free = [t_g]
            hids = [two_parts(ar, 11, T) for _ in range(2)]
            gbs = [ar(T) for _ in range(2)]
            es = Ring([dict(v=ar(2, T), t=None) for _ in range(2)])
            bring = Ring(banks[0:4])
            t_d = [None, None]
            pend = iter(())
            for x in range(8):
                b = bring()
                t = mm([(b.t[:, 0:T], ident[0:8, x:x + 1].broadcast_to([8, 128]), gT, True)], t_g, b.free)
                gb = gbs[x % 2]
                t = acp(gb, b.t[:, 0:T], t, V_.ops[-1])
                b.free = [t]
                ts_ = []
                for t in swiglu(w["moe_w1"][0, x], w["moe_w3"][0, x], hids[x % 2], 11, bring, es, [t_h, t], gb, t_d[x % 2]):
                    ts_.append(t)
                    for t_d[(x - 1) % 2] in pend:
                        break
                for t_d[(x - 1) % 2] in pend:
                    pass
                pend = down(w["moe_w2"][0, x], hids[x % 2], 11, banks[4:8], x == 0, ts_)
            for t in pend:
                pass
            add_acc(banks[4:8], t)

        def attend(cases, e, bring, lag):
            for _ in range(lag):
                yield
            for (ready, qs, fq, keys, vals, o_dst) in cases:
                while ready() is None:
                    yield
                at, b, bs, spans = 0, None, [], []
                for k_, mk in keys:
                    n = k_.shape[1]
                    if b is None or at + n > 512:
                        b, at = bring(), 0
                        bs.append(b)
                    spans.append((b, at, n, mk))
                    at += n
                tok = [mm([(b.t[:, s_[1]:s_[1] + s_[2]], qs[j], k_, True) for j, (s_, (k_, _)) in enumerate(zip(spans, keys)) if s_[0] is b],
                          ready(), b.free) for b in bs]
                yield
                pos = 0
                for f_, (b, a0, n, mk) in zip(fq, spans):
                    t = stt(e["v"][:, pos:pos + n], b.t[:, a0:a0 + n], f_, mk, MUL, ADD, tok, e["t"])
                    b.free = [t]
                    pos += n
                V(lambda en, e=e, pos=pos: en.tensor_reduce(e["m"][:, 0:1], e["v"][:, 0:pos], AX.X, MAX))
                t = ts(e["m"][:, 1:2], e["m"][:, 0:1], -1.0, None, MUL)
                t = act(e["v"][:, 0:pos], e["v"][:, 0:pos], ACT.Exp, t, bias=e["m"][:, 1:2], acc=e["m"][:, 2:3])
                yield
                t_r = recip(e["m"][:, 3:4], e["m"][:, 2:3], t)
                blk = pos // 128
                pt = []
                for j0 in range(0, blk, 4):
                    j1 = min(blk, j0 + 4)
                    b = bring()
                    tp = tr([(b.t[:, 128 * (j - j0):128 * (j - j0) + 128], e["v"][:, 128 * j:128 * j + 128], ident) for j in range(j0, j1)], t, b.free)
                    pt.append(acp(e["p"][:, 128 * j0:128 * j1], b.t[:, 0:128 * (j1 - j0)], tp, e["t"]))
                    b.free = [pt[-1]]
                yield
                bo = bring()
                to = mm([(bo.t[:, 0:64], e["p"][:, 128 * j:128 * j + 128], vals[j], j == 0) for j in range(blk)], pt, bo.free)
                t = ts(o_dst, bo.t[:, 0:64], e["m"][:, 3:4], None, MUL, None, to, t_r)
                bo.free = [t]
                e["t"] = t
                yield

        class QK:

            def __init__(self, raw, n, b, sq, free):
                self.raw, self.n, self.b, self.sq, self.todo, self.k, self.t = raw, n, b, sq, [], 0, [free, b.free]

            def evac(self, b, f0, nt, t):
                m = self.k % 2
                self.k += 1
                t1 = acp(self.raw[:, f0:f0 + nt, :], two(b)[:, 0:nt, :], t)
                t2 = act(self.sq[m][:, 0:nt, :], two(b)[:, 0:nt, :], ACT.Square, t, self.t)
                self.flush()
                self.todo = [(f0 + i, self.sq[m][:, i, :], t2) for i in range(nt)]
                return [t2]

            def flush(self):
                for j, s_, t in self.todo:
                    self.t = mm([(table(self.b, self.n)[:, i, j, :], s_[:, 128 * i:128 * i + 128], c("blk")[:, 0:65:64], True)
                                 for i in range(2)], t, self.t)
                self.todo = []

            def factors(self):
                self.flush()
                r, t = factors(self.b, rt_, self.n, 64, EPS, self.t)
                t = ts(r[:, :, 0:self.n // 2, :], r[:, :, 0:self.n // 2, :], 0.125, None, MUL)
                return r, t

        def qk_ready(raw, tiles, ready, rs, t_rs, tmps, bring):
            for n, (j, key, is_k, name) in enumerate(tiles):
                tmp, tm2, un = (tmps[3 * (n % 2) + z][:, 0, :] for z in range(3))
                b = bring()
                if is_k:
                    t = spread(b, rs, [j], t_rs)
                    t = stt(un, raw[:, j, :], pc(key), b.t[:, 0:T], MUL, MUL, t)
                else:
                    t = ts(un, raw[:, j, :], pc(key), None, MUL, None, t_rs)
                t2 = mm([(b.t[:, T:2 * T], c("pp"), un, True)], t, b.free)
                tp = tt(tmp, un, c("cp"), MUL, t, E=G)
                t = tt(tm2, b.t[:, T:2 * T], c("sp"), MUL, t2)
                b.free = [t]
                t = tt(raw[:, j, :], tmp, tm2, ADD, tp)
                if name is not None:
                    ready[name] = t
                yield

        def softplus(x, a_, b_):
            t = act(a_, x, ACT.Abs, V_.ops[-1])
            act(a_, a_, ACT.Exp, scale=-1.0)
            t = act(a_, a_, ACT.Ln, bias=1.0)
            return stt(x, x, 0.0, a_, MAX, ADD, t)

        t_c2 = []

        def second_consts():
            t_c2.append(dma(Aq_, "c2", lambda e: e.dma_start(CT["c2"][:, 0:offsets(CONSTS["c2"])[1]], cst["c2"]), t_c1, last()))

        def even():
            barrier()
            W = w["even_w_in_2"][0]
            ar = Arena(0, ARENA)
            xbc, zs = ar(16, T), ar(8, T)
            t_h = norm("en", zs, banks[0], last(), t_c2)
            dtT, dtm, cs = ar(T, p=16), ar(T, p=16), ar(T, p=16)
            tokd, nA = ar(2, 2, 16), ar(1, p=16)
            at = ar.at
            xd, cbm = ar(2, 1024), ar(384)
            us = [ar(384), ar(384)]
            second = Arena(8 * T, ar.at)
            raw_at = ar.at
            raw, v, g_, oT = ar(24, T), ar(2, 1536), ar(4, T), ar(4, T)
            pa = Arena(at, at + 2048)
            pad = Ring([dict(v=pa(2, T + 3), t=None) for _ in range(2)])
            acc = pa(2, T)
            tz = [mset(p_["v"][:, :, 0:3], 0.0) for p_ in pad.items]
            cw, cbi = ar(16, 4), ar(16)
            t_cw = ts(cw, P_[:, poff["ecw"][0]:poff["ecw"][0] + 64].rearrange("p (a b) -> p a b", a=16), 0.5, None, MUL, None, t_par)
            ts(cbi, P_[:, poff["ecb"][0]:poff["ecb"][0] + 16], 0.5, None, MUL)
            bulk = Ring(banks[0:8])

            def ev(b, f0, nt, t):
                p_ = pad()
                t = acp(p_["v"][:, 0:nt, 3:T + 3], two(b)[:, 0:nt, :], t, tz, p_["t"])
                for i in range(nt):
                    f = f0 + i
                    ts(acc[:, i, :], p_["v"][:, i, 0:T], cw[:, f, 0:1], cbi[:, f:f + 1], MUL, ADD, t)
                    for j in range(1, 4):
                        u = stt(acc[:, i, :], p_["v"][:, i, j:j + T], cw[:, f, j:j + 1], acc[:, i, :], MUL, ADD)
                p_["t"] = u
                xo = xbc[:, f0:f0 + nt, :]
                u = act(xo, acc[:, 0:nt, :], ACT.Tanh, u)
                one_plus(xo, xo, acc[:, 0:nt, :], u)
                return [t]
            for _ in proj(cols(W, 1024, 3072), H, 8, bulk, ev, t_h):
                pass

            def evd(b, f0, nt, t):
                return [acp(dtT, b.t[0:16, 0:T], t)]
            for _ in proj([W[:, 3072:3200]], H, 8, bulk, evd, t_h):
                pass
            for _ in proj(cols(W, 0, 1024), H, 8, bulk, to_sbuf(zs), t_h):
                pass

            def ssd(bring):
                t = ts(dtT, dtT, pc("edt", 0, 0, 16), None, ADD, None, Aq_.ops[-1])
                softplus(dtT, dtm, None)
                t = act(nA, pc("eal", 0, 0, 16), ACT.Exp)
                ts(nA, nA, -1.0, None, MUL, None, t)
                ts(dtm, dtT, nA, None, MUL)
                t = V(lambda e: e.tensor_tensor_scan(cs, c("ones", 16)[:, 0:1].broadcast_to([16, T]), dtm, 0.0, MUL, ADD))
                yield
                b = bring()
                t = tr([(b.t[:, 16 * (2 * s_ + i):16 * (2 * s_ + i) + 16], src[:, 128 * i:128 * i + 128], ident[0:16, 0:16])
                        for s_, src in enumerate((dtT, cs)) for i in range(2)], t, b.free)
                t_dt = cp(tokd, b.t[:, 0:64].rearrange("p (s i h) -> p s i h", s=2, i=2), t)
                b.free = [t_dt]
                yield
                for i in range(2):
                    for f0 in (0, 4):
                        b = bring()
                        t = tr([(b.t[:, 128 * j:128 * j + 128], xbc[:, f0 + j, 128 * i:128 * i + 128], ident) for j in range(4)], V_.ops[-1], b.free)
                        t = tt(xd[:, i, 128 * f0:128 * f0 + 512].rearrange("p (h n) -> p h n", n=64),
                               b.t[:, :].rearrange("p (h n) -> p h n", n=64),
                               tokd[:, 0, i, 2 * f0:2 * f0 + 8].unsqueeze(2).broadcast_to([128, 8, 64]), MUL, t)
                        b.free = [t]
                        yield
                t_xd = t
                mask = c("ssd")
                ends = [None, None]
                for g in range(4):
                    Bt, Ct = xbc[:, 8 + g, :], xbc[:, 12 + g, :]
                    b = bring()
                    t = mm([(b.t[:, 0:256], Bt[:, 0:128], Ct, True), (b.t[:, 256:384], Bt[:, 128:256], Ct[:, 128:256], True)], t_xd, b.free)
                    tt(cbm[:, 0:256], b.t[:, 0:256], mask, MUL, t)
                    t = tt(cbm[:, 256:384], b.t[:, 256:384], mask[:, 0:128], MUL)
                    b.free = [t]
                    for hh in range(4):
                        h = 4 * g + hh
                        m = h % 2
                        b = bring()
                        t = mm([(b.t[:, 0:T], ident[0:16, h:h + 1].broadcast_to([16, 128]), cs, True)], t_dt, b.free)
                        u = us[m]
                        ts(u[:, 0:256], b.t[:, 0:256], tokd[:, 1, 0, h:h + 1], 0.0, SUB, MIN, t, ends[m])
                        t = ts(u[:, 256:384], b.t[:, 128:256], tokd[:, 1, 1, h:h + 1], 0.0, SUB, MIN)
                        b.free = [t]
                        t = act(u, u, ACT.Exp, t)
                        t_u = tt(u, u, cbm, MUL, t)
                        yield
                        if m == 0:
                            bo = bring()
                        o = bo.t[64 * m:64 * m + 64, :]
                        t = mm([(o[:, 0:256], xd[:, 0, 64 * h:64 * h + 64], u[:, 0:256], True),
                                (o[:, 128:256], xd[:, 1, 64 * h:64 * h + 64], u[:, 256:384], False)], t_u, bo.free, t_xd)
                        ends[m] = t
                        if m == 1:
                            f = h // 2
                            t = stt(xbc[:, f, :], xbc[:, f, :], pc("eds", f), bo.t[:, 0:T], MUL, ADD, t)
                            bo.free = [t]
                y = xbc[:, 0:8, :]
                t = half_tanh(xbc[:, 8:16, :], zs, t)
                one_plus(zs, xbc[:, 8:16, :], zs, t)
                yield
                stt(y, y, 0.5, zs, MUL, MUL)
                t = tt(zs, y, y, MUL)
                for g in range(4):
                    b, b2 = bring(), bring()
                    t2 = all_rows(b, range(2 * g, 2 * g + 2), zs, t, 256, EPS, b2)
                    for j in range(2):
                        f = 2 * g + j
                        u = stt(y[:, f, :], y[:, f, :], pc("esn", f), b2.t[:, 0:T], MUL, MUL, t2)
                    b2.free = [u]
                    yield

            fac = []

            def dil_proj():
                b_ = Ring(banks[4:7])
                q_ = QK(raw, 24, banks[7], [oT[:, 0:2, :], oT[:, 2:4, :]], [])
                yield from proj(cols(W, 3088, 6160), H, 8, b_, q_.evac, t_h)
                fac.append(q_.factors())
                yield from proj_tok(cols(W, 6160, 7696), b_, v, t_h)
                yield from proj(cols(W, 7696, 8208), H, 8, b_, to_sbuf(g_), t_h)
            run(dil_proj(), ssd(Ring(banks[0:4])))
            barrier()
            o_tok = second(2, 512)
            tmps = [second(1, T) for _ in range(6)]
            es = [dict(v=second(768), p=second(768), m=second(4), t=None) for _ in range(3)]
            dm = c("dil").rearrange("p (g n) -> p g n", g=3)
            bk = Ring(banks[6:8])
            rs, t_rs = fac[0]
            tiles, ready = [], {}
            for hp in range(4):
                tiles += [(4 * g + hp, "eqn", False, None) for g in range(3)]
                tiles += [(12 + 4 * g + hp, "ekn", True, hp if g == 2 else None) for g in range(3)]
            cases = []
            for hp in range(4):
                for hh in range(2):
                    h, r = 2 * hp + hh, slice(64 * hh, 64 * hh + 64)
                    for i in range(2):
                        n = 128 * (i + 1)
                        cases.append((lambda hp=hp: ready.get(hp), [raw[r, 4 * g + hp, 128 * i:128 * i + 128] for g in range(3)],
                                      [rs[:, i, 4 * g + hp, hh:hh + 1] for g in range(3)],
                                      [(raw[r, 12 + 4 * g + hp, 0:n], dm[:, g, 256 - n:256]) for g in range(3)],
                                      [v[:, j, 64 * (8 * g + h):64 * (8 * g + h) + 64] for g in range(3) for j in range(i + 1)],
                                      o_tok[:, i, 64 * h:64 * h + 64]))
            it = iter(cases)
            run((qk_ready(raw, tiles, ready, rs, t_rs, tmps, bk), 2), *(attend(it, es[z], Ring(banks[2 * z:2 * z + 2]), z) for z in range(3)))
            for i in range(2):
                b = bk()
                t = tr([(b.t[:, 128 * j:128 * j + 128], o_tok[:, i, 128 * j:128 * j + 128], ident) for j in range(4)], V_.ops[-1], b.free)
                t = acp(oT[:, :, 128 * i:128 * i + 128], b.t[:, :].rearrange("p (j n) -> p j n", j=4), t)
                b.free = [t]
            th = tmps_gate(v, 4)
            t2 = half_tanh(th, g_)
            one_plus(th, th, g_, t2)
            t = stt(oT, oT, 0.5, th, MUL, MUL)
            out_proj(w["even_w_out_2"][0], [xbc[:, k:k + 2, :] for k in range(0, 8, 2)] + [oT[:, 0:2, :], oT[:, 2:4, :]],
                     two_parts(Arena(raw_at, ARENA), 12, T), 12, t)

        def tmps_gate(v, n):
            return v.rearrange("p a b -> p (a b)")[:, 0:n * T].rearrange("p (t n) -> p t n", n=T)

        def out_proj(W, src, parts_, nt, t):
            ts_ = [split(cut(parts_, lambda z: z[:, 2 * k:2 * k + 2, :]), s_, t) for k, s_ in enumerate(src)]
            for t in down(W, parts_, nt, banks[4:8], True, ts_):
                pass
            add_acc(banks[4:8], t)

        def odd():
            barrier()
            W = w["odd_w_in_2"][0]
            ar = Arena(0, ARENA)
            raw = ar(16, T)
            t_h = norm("on", raw[:, 0:8, :], banks[0], last(), t_c2)
            bulk = Ring(banks[0:8])
            v, g_, oT = ar(2, 1024), ar(8, T), ar(8, T)
            q_ = QK(raw, 16, banks[7], [oT[:, 0:2, :], oT[:, 2:4, :]], [])
            bulk = Ring(banks[0:7])
            for _ in proj(cols(W, 0, 2048), H, 8, bulk, q_.evac, t_h):
                pass
            rs, t_rs = q_.factors()
            for _ in proj_tok(cols(W, 2048, 3072), bulk, v, t_h):
                pass
            o_tok = ar(2, 1024)
            tmps = [ar(1, T) for _ in range(6)]
            causal = ar(256)
            mset(causal[:, 0:128], 0.0)
            tz = cp(causal[:, 128:256], c("dil")[:, 128:256], G_.ops[-1])
            es = [dict(v=ar(256), p=ar(256), m=ar(4), t=tz) for _ in range(4)]
            th = ar(8, T)
            bk = Ring(banks[4:6])
            tiles, ready = [], {}
            for hp in range(8):
                tiles += [(hp, "oqn", False, None), (8 + hp, "okn", True, hp)]
            cases = []
            for hp in range(8):
                for hh in range(2):
                    h, r = 2 * hp + hh, slice(64 * hh, 64 * hh + 64)
                    for i in range(2):
                        cases.append((lambda hp=hp: ready.get(hp), [raw[r, hp, 128 * i:128 * i + 128]], [rs[:, i, hp, hh:hh + 1]],
                                      [(raw[r, 8 + hp, 0:128 * i + 128], causal[:, 128 - 128 * i:256])],
                                      [v[:, j, 64 * h:64 * h + 64] for j in range(i + 1)],
                                      o_tok[:, i, 64 * h:64 * h + 64]))
            it = iter(cases)
            run((qk_ready(raw, tiles, ready, rs, t_rs, tmps, bk), 1), *(attend(it, es[z], Ring(banks[z:z + 1]), z) for z in range(4)),
                proj(cols(W, 3072, 4096, 128), H, 8, Ring(banks[6:8]), to_sbuf(g_), t_h))
            for i in range(2):
                for f0 in (0, 4):
                    b = bk()
                    t = tr([(b.t[:, 128 * j:128 * j + 128], o_tok[:, i, 128 * (f0 + j):128 * (f0 + j) + 128], ident) for j in range(4)],
                           V_.ops[-1], b.free)
                    t = acp(oT[:, f0:f0 + 4, 128 * i:128 * i + 128], b.t[:, :].rearrange("p (j n) -> p j n", j=4), t)
                    b.free = [t]
            t2 = half_tanh(th, g_)
            one_plus(th, th, g_, t2)
            t = stt(oT, oT, 0.5, th, MUL, MUL)
            out_proj(w["odd_w_out_2"][0], [oT[:, k:k + 2, :] for k in range(0, 8, 2)], two_parts(Arena(0, ARENA), 8, T), 8, t)

        mix_block(0)
        ffn(0)
        mix_block(1)
        second_consts()
        moe(1)
        even()
        odd()
        t_out = dma(SP, "out", lambda e: e.dma_start(outT.rearrange("(t p) n -> p t n", p=128), X), last())
        SP(lambda e: e.nop(), t_out)
        place_splits()
        number(engines)

        block = ctx.enter_context(nc.Block())
        for E, name in ((PE_, "tensor"), (V_, "vector"), (Aq_, "scalar"), (G_, "gpsimd"), (SP, "sync")):
            def body(e, E=E):
                E.run(e)
            {"tensor": block.tensor, "vector": block.vector, "scalar": block.scalar, "gpsimd": block.gpsimd,
             "sync": block.sync}[name](body)


_W = ["w_in", "rw_w2", "rw_a2", "rw_g2", "w_gate", "w_branch", "w_out", "ffn_w1", "ffn_w3", "ffn_w2", "moe_w1", "moe_w3",
      "moe_w2", "even_w_in_2", "even_w_out_2", "odd_w_in_2", "odd_w_out_2"]


def kernel(**inputs):
    import concourse.bacc as _bacc
    from concourse.bass_utils import run_bass_kernel_spmd as _run

    nc = _bacc.Bacc("TRN2", target_bir_lowering=False, num_devices=1)
    i = {k: np.asarray(v) for k, v in inputs.items()}
    arrays = {k: np.ascontiguousarray(i[k]) for k in _W}
    arrays.update(consts())
    arrays["par"] = params(i)
    arrays["xT"] = np.ascontiguousarray(i["x"][0].T)
    h = {k: nc.dram_tensor(k, a.shape, F, kind="ExternalInput").ap() for k, a in arrays.items()}
    outT = nc.dram_tensor("outT", (DM, T), F, kind="ExternalOutput").ap()
    build(nc, {k: h[k] for k in _W}, {k: h[k] for k in CONSTS}, h["par"], h["xT"], outT)
    r = _run(nc, [arrays], core_ids=[0])
    return np.ascontiguousarray(r.results[0]["outT"].T)[None]
```

```python
import concourse.bass as bass
from concourse import mybir
from contextlib import ExitStack
import numpy as np

F = mybir.dt.float32
U32 = mybir.dt.uint32
I32 = mybir.dt.int32
R = mybir.dt.float32r
ALU = mybir.AluOpType
ACT = mybir.ActivationFunctionType
AX = mybir.AxisListType

T = 256
DM = 1024
EPS = 1e-6
RWS = 0.606531
NEG = -1.0e30
RAW = 3
PARTS = 3
AHEAD = 2
SLOT = 2048
STEP = 8
ARENA = 24072

PARAM_COLS = []
for _l in range(2):
    PARAM_COLS += [(f"nm{_l}", 8), (f"nf{_l}", 8), (f"mu{_l}", 8), (f"w0{_l}", 2), (f"a0{_l}", 2), (f"kk{_l}", 2),
                   (f"ka{_l}", 2), (f"rk{_l}", 2), (f"lw{_l}", 2), (f"lb{_l}", 2), (f"sq{_l}", 1), (f"sk{_l}", 1),
                   (f"gn{_l}", 2), (f"dw{_l}", 62), (f"cb{_l}", 2), (f"cw{_l}", 2), (f"cl{_l}", 2)]
PARAM_COLS += [("rt", 64), ("en", 8), ("ecw", 64), ("ecb", 16), ("edt", 1), ("eal", 1), ("eds", 8), ("esn", 8),
               ("eqn", 1), ("ekn", 1), ("on", 8), ("oqn", 1), ("okn", 1)]
CONSTS = {
    "c0": [("id", 128), ("blk", 128), ("ones", 128), ("iota", 8)],
    "c1": [("nones", 128), ("pr", 128), ("cr", 256), ("sr", 256), ("dec", 1024), ("rneg", 128), ("sbadd", 384),
           ("sb01", 128), ("rwm", 256), ("lvl", 384), ("rst", 256)],
    "c2": [("pp", 128), ("cp", 256), ("sp", 256), ("dil", 768), ("ssd", 256)],
}


def offsets(cols):
    out, n = {}, 0
    for k, w in cols:
        out[k] = (n, w)
        n += w
    return out, n


def consts():
    C = {g: np.zeros((128, offsets(cols)[1]), np.float32) for g, cols in CONSTS.items()}
    where = {k: (g, o, w) for g, cols in CONSTS.items() for k, (o, w) in offsets(cols)[0].items()}

    def put(k, a):
        g, o, w = where[k]
        C[g][:a.shape[0], o:o + w] = a.reshape(a.shape[0], w)

    i = np.arange(128)
    put("id", np.eye(128))
    put("blk", (i[:, None] // 64 == i[None, :] // 64) * 1.0)
    put("ones", np.ones((128, 128)))
    put("nones", -np.ones((128, 128)))
    for key, half, width in (("pr", 32, 64), ("pp", 8, 16)):
        m = np.zeros((128, 128))
        for b in (0, 64):
            for j in range(half):
                m[b + j + half, b + j] = -1.0
                m[b + j, b + j + half] = 1.0
        put(key, m)
    t = np.arange(T, dtype=np.float32)
    inv = np.float32(10000.0) ** (-np.arange(0, 64, 2, dtype=np.float32) / np.float32(64))
    ang = (t[None, :] * inv[:, None]).astype(np.float32)
    put("cr", np.tile(np.cos(ang), (4, 1)))
    put("sr", np.tile(np.sin(ang), (4, 1)))
    inv = np.float32(500000.0) ** (-np.arange(8, dtype=np.float32) * np.float32(2.0) / np.float32(16))
    ang = (t[None, :] * inv[:, None]).astype(np.float32)
    c, s = np.ones((64, T)), np.zeros((64, T))
    c[0:16] = np.tile(np.cos(ang), (2, 1))
    s[0:16] = np.tile(np.sin(ang), (2, 1))
    put("cp", np.tile(c, (2, 1)))
    put("sp", np.tile(s, (2, 1)))
    dec = np.zeros((128, 4, T))
    rel = np.arange(T)[None, :] - i[:, None]
    for h in range(4):
        lg = np.log(1.0 - 2.0 ** (-5.0 - h))
        dec[:, h] = np.where(rel >= 0, np.exp(np.maximum(rel, 0) * lg), 0.0) * 0.125
    put("dec", dec)
    put("rneg", (i[:, None] >= i[None, :]) * -1.0)
    lt = i[:, None] < i[None, :]
    d = np.where(lt, 0.0, NEG)
    put("sbadd", np.concatenate([d, np.zeros((128, 128)), d], 1))
    put("sb01", lt * 1.0)
    dil = np.zeros((128, 3, 256))
    dist = i[:, None] + 128 - np.arange(256)[None, :]
    for g, (w, r) in enumerate(((128, 1), (512, 4), (2048, 16))):
        ok = (dist >= 0) & (dist <= w) & (dist % r == 0)
        dil[:, g] = np.where(ok, 0.0, NEG)
    put("dil", dil)
    put("ssd", (np.arange(256)[None, :] >= i[:, None]) * 1.0)
    j = np.arange(64)
    st, inc = (j[:, None] < j[None, :]) * 1.0, (j[:, None] <= j[None, :]) * 1.0
    put("rwm", np.tile(np.concatenate([st, inc, st, inc], 1), (2, 1)))
    lvl = np.zeros((64, 6, 64))
    for v in range(6):
        b = 1 << v
        lvl[:, v] = (j[:, None] // (2 * b) == j[None, :] // (2 * b)) & (j[:, None] % (2 * b) < b) & (j[None, :] % (2 * b) >= b)
    put("lvl", np.tile(lvl, (2, 1, 1)))
    put("rst", np.tile((np.arange(T) % 64 != 0) * 1.0, (128, 1)))
    put("iota", np.tile(np.arange(8), (128, 1)) * 1.0)
    return C


def col(a):
    return a.reshape(-1, 128).T


def params(i):
    P = {}
    for l in range(2):
        P[f"nm{l}"], P[f"nf{l}"], P[f"mu{l}"] = col(i["norm_mix"][l]), col(i["norm_ffn"][l]), col(i["rw_mu"][l])
        for k, n in (("w0", "rw_w0"), ("a0", "rw_a0"), ("kk", "rw_k_k"), ("ka", "rw_k_a"), ("rk", "rw_r_k"),
                     ("lw", "rw_ln_w"), ("lb", "rw_ln_b"), ("gn", "ret_gn"), ("cb", "conv_b"), ("cw", "conv_ln_w"),
                     ("cl", "conv_ln_b")):
            P[f"{k}{l}"] = col(i[n][l].reshape(-1))
        P[f"sq{l}"], P[f"sk{l}"] = col(np.tile(i["sb_q_norm"][l], 2)), col(np.tile(i["sb_k_norm"][l], 2))
        P[f"dw{l}"] = i["conv_dw"][l].reshape(31, 2, 128).transpose(2, 1, 0).reshape(128, 62)
    P["rt"] = i["router"][0].reshape(8, 128, 8).transpose(1, 0, 2).reshape(128, 64)
    P["en"], P["on"] = col(i["even_norm_w_2"][0]), col(i["odd_norm_w_2"][0])
    P["ecw"] = i["even_conv_w_2"][0].reshape(16, 128, 4).transpose(1, 0, 2).reshape(128, 64)
    P["ecb"], P["esn"] = col(i["even_conv_b_2"][0]), col(i["even_ssd_norm_w_2"][0])
    P["edt"], P["eal"] = i["even_dt_bias_2"][0].reshape(16, 1), i["even_a_log_2"][0].reshape(16, 1)
    P["eds"] = col(np.repeat(i["even_d_skip_2"][0], 64))
    for k, n in (("eqn", "even_q_norm_2"), ("ekn", "even_k_norm_2"), ("oqn", "odd_q_norm_2"), ("okn", "odd_k_norm_2")):
        P[k] = col(np.tile(i[n][0], 2))
    off, n = offsets(PARAM_COLS)
    out = np.zeros((128, n), np.float32)
    for k, (o, w) in off.items():
        out[:P[k].shape[0], o:o + w] = P[k]
    return out


class Op:

    def __init__(self, eng, fn, after, sem=None, val=0):
        self.eng, self.fn, self.after, self.sem, self.val = eng, fn, after, sem, val
        self.count = 0
        self.cost = self.end = 0.0
        self.signals = sem is not None


def flat(a):
    if a is None:
        return []
    return [o for x in a for o in flat(x)] if isinstance(a, (list, tuple)) else [a]


class Stream:

    def __init__(self, prev=(), gen=None, ahead=0.0):
        self.prev, self.fence, self.gen, self.ahead, self.todo = dict(prev), {}, gen, ahead, []


class Engine:

    def __init__(self, name, done, chained, log, cur):
        self.name, self.done, self.chained, self.ops, self.log, self.cur = name, done, chained, [], log, cur

    def __call__(self, fn, *after):
        st = self.cur[0]
        after = flat(after) + flat(st.fence.pop(self, None))
        if self.chained and self in st.prev:
            after = after + [st.prev[self]]
        op = self.insert(fn, *after)
        st.prev[self] = op
        return op

    def insert(self, fn, *after):
        op = Op(self, fn, flat(after))
        self.ops.append(op)
        self.log.append(op)
        return op

    def run(self, e):
        seen = {}
        for op in self.ops:
            need = {}
            for o in op.after:
                k, v = (o.sem, o.val) if o.sem is not None else (o.eng.done, o.count)
                need[k.name] = max(need.get(k.name, (0, None))[0], v), k
            for name, (v, k) in need.items():
                if v > seen.get(name, 0):
                    seen[name] = v
                    e.wait_ge(k, v)
            ins = op.fn(e)
            if op.sem is not None:
                ins.then_inc(op.sem, 16)
            elif op.signals:
                ins.then_inc(self.done, 1)


def number(engines):
    for E in engines:
        for op in E.ops:
            for o in op.after:
                if o.sem is None:
                    o.signals = True
    for E in engines:
        n = 0
        for op in E.ops:
            if op.sem is None and op.signals:
                n += 1
                op.count = n


class Bank:
    def __init__(self, t):
        self.t, self.free = t, []


class Ring:
    def __init__(self, items):
        self.items, self.n = items, 0

    def __call__(self):
        self.n += 1
        return self.items[(self.n - 1) % len(self.items)]


def build(nc, w, cst, par, xT, outT):
    ctx = ExitStack()
    with ctx:
        def sb(name, n, p=128, dt=F):
            return ctx.enter_context(nc.sbuf_tensor("s_" + name, [p, n], dt))

        def sem(name):
            return ctx.enter_context(nc.semaphore(name))

        where = {k: (g, o, n) for g, cols_ in CONSTS.items() for k, (o, n) in offsets(cols_)[0].items()}
        poff, pn = offsets(PARAM_COLS)
        CT = {"c0": sb("c0", offsets(CONSTS["c0"])[1])}
        CT["c1"] = CT["c2"] = sb("c1", offsets(CONSTS["c1"])[1])
        P_ = sb("par", pn)
        X_, ring_ = sb("X", 2048), sb("ring", RAW * SLOT)
        h_at = nc.sbuf_base
        Hh_, Hl_, wh_, wl_ = (sb(k, n, dt=R) for k, n in (("Hh", 2048), ("Hl", 2048), ("wh", PARTS * SLOT), ("wl", PARTS * SLOT)))
        R_ = sb("roots", 336)
        S_ = nc.alloc_sbuf_tensor_at("s_squares", [128, 2048], F, offset=h_at)
        base = nc.sbuf_base
        A_ = sb("arena", ARENA)
        Z_ = nc.alloc_sbuf_tensor_at("s_arena_r", [128, ARENA], R, offset=base)
        banks = [Bank(ctx.enter_context(nc.psum_tensor(f"b{i}", [128, 512], F))) for i in range(8)]
        log, cur = [], [Stream()]
        PE, V, A, G, SP = (Engine(n, sem("done_" + n), n in "VAG", log, cur) for n in ("PE", "V", "A", "G", "SP"))
        engines = [PE, V, A, G, SP]

        def c(k, p=128, p0=0):
            g, o, n = where[k]
            return CT[g][p0:p0 + p, o:o + n]

        def pc(k, j=0, p0=0, p1=128):
            o, n = poff[k]
            return P_[p0:p1, o + j:o + j + 1]

        X = X_[:, :].rearrange("p (t n) -> p t n", n=T)
        SQ = S_[:, :].rearrange("p (t n) -> p t n", n=T)
        H = tuple(h[:, :].rearrange("p (t n) -> p t n", n=T) for h in (Hh_, Hl_))

        dma_sems = {}

        def dma(eng, key, fn, *after):
            if key not in dma_sems:
                dma_sems[key] = [sem("dma_" + key), 0]
            s, n = dma_sems[key]
            dma_sems[key][1] = n + 16
            op = eng.insert(fn, after)
            op.sem, op.val, op.signals = s, n + 16, True
            return op

        t_x = dma(SP, "x", lambda e: e.dma_start(X, xT.rearrange("(t p) n -> p t n", p=128)))
        t_cst = dma(SP, "c0", lambda e: e.dma_start(CT["c0"][:, :], cst["c0"]))
        t_par = dma(SP, "par", lambda e: e.dma_start(P_[:, :], par))
        t_c1 = []

        def first_consts():
            if not t_c1:
                t_c1.append(dma(SP, "c1", lambda e: e.dma_start(CT["c1"][:, :], cst["c1"])))

        class Slot:
            def __init__(self, i):
                self.i, self.free = i, []
        raws, parts = Ring([Slot(i) for i in range(RAW)]), Ring([Slot(i) for i in range(PARTS)])
        marks = []

        def load(src):
            k, n = src.shape
            kt = k // 128
            s, q = raws(), parts()
            raw = ring_[:, s.i * SLOT:s.i * SLOT + kt * n]
            t = dma(SP, f"w{s.i}", lambda e: e.dma_start(raw.rearrange("p (k n) -> p k n", k=kt), src.rearrange("(k p) n -> p k n", p=128)), s.free)
            hi, lo = (z[:, q.i * SLOT:q.i * SLOT + kt * n] for z in (wh_, wl_))
            marks.append({E: E.insert(None) for E in (Aq_, V_, G_)})
            N = len(marks) - 1
            early.append((N, raw, hi, lo, t, q.free, s))
            c_ = [Op(None, None, []), Op(None, None, [])]
            early[-1] += (c_,)
            q.free, s.free = [], [c_[1]]
            return q, tuple(z.rearrange("p (k n) -> p k n", k=kt) for z in (hi, lo)), c_

        early = []

        def place_splits():
            jobs = {}
            for N, raw, hi, lo, t, free, s_, c_ in early:
                m = marks[max(0, N - AHEAD)]
                E = G_ if N % 3 == 1 else V_
                c_[0].eng, c_[0].fn, c_[0].after = Aq_, (lambda e, hi=hi, raw=raw: e.activation(hi, raw, ACT.Copy)), flat([t, free])
                c_[1].eng, c_[1].after = E, flat([t, free, c_[0]])
                c_[1].fn = lambda e, hi=hi, raw=raw, lo=lo: e.tensor_tensor(lo, raw, hi.bitcast(F), ALU.subtract)
                jobs.setdefault(id(m[Aq_]), []).append(c_[0])
                jobs.setdefault(id(m[E]), []).append(c_[1])
            for E in (Aq_, V_, G_):
                E.ops = [o for op in E.ops for o in (jobs.get(id(op), []) if op.fn is None else [op])]
            for o, nxt in zip(G_.ops, G_.ops[1:]):
                nxt.after = nxt.after + [o]

        def pairs(W, X_):
            return ((W[0], X_[0]), (W[0], X_[1]), (W[1], X_[0]))

        def mm3(out, W, X_, start):
            return [(out, a_, b_, start and z == 0) for z, (a_, b_) in enumerate(pairs(W, X_))]

        def cut(P2, f):
            return tuple(f(z) for z in P2)

        def split(P2, v, *af, E=None):
            t = act(P2[0], v, ACT.Copy, af)
            return tt(P2[1], v, P2[0].bitcast(F), SUB, t, E=E)

        def cost(op, out, each=1.04e-3, fixed=0.06):
            op.cost = fixed + each * float(np.prod(out.shape[1:]))
            return op

        def tt(out, a, b, op, *af, E=None):
            return cost((E or V)(lambda e: e.tensor_tensor(out, a, b, op), *af), out, 2.1e-3 if E is G else 1.04e-3)

        def ts(out, a, s1, s2, o0, o1=None, *af, E=None):
            if o1 is None:
                return cost((E or V)(lambda e: e.tensor_scalar(out, a, s1, None, o0), *af), out)
            return cost((E or V)(lambda e: e.tensor_scalar(out, a, s1, s2, o0, o1), *af), out)

        def stt(out, a, s, b, o0, o1, *af):
            return cost(V(lambda e: e.scalar_tensor_tensor(out=out, in0=a, scalar=s, in1=b, op0=o0, op1=o1), *af), out)

        def cp(out, a, *af):
            return V(lambda e: e.tensor_copy(out, a), *af)

        def act(out, a, f, *af, bias=0.0, scale=1.0, acc=None):
            kw = dict(bias=bias, scale=scale)
            if acc is not None:
                kw["accum_out"] = acc
            return cost(A(lambda e: e.activation(out, a, f, **kw), *af), out, 0.83e-3, 0.2)

        def acp(out, a, *af, scale=1.0):
            return cost(A(lambda e: e.activation(out, a, ACT.Copy, scale=scale), *af), out, 0.83e-3, 0.2)

        def root(x, y, a_, t, scale=1.0):
            V(lambda e: e.tensor_scalar(y.bitcast(I32), x.bitcast(I32), 1, None, ALU.logical_shift_right), t)
            V(lambda e: e.tensor_scalar(y.bitcast(I32), y.bitcast(I32), -1.0, 1597463007.0, MUL, ADD))
            for i in range(3):
                stt(a_, y, -0.5, y, MUL, MUL)
                tt(a_, a_, x, MUL)
                t = stt(y, a_, 1.5, y, ADD, MUL)
            return t if scale == 1.0 else ts(y, y, scale, None, MUL)

        def sums(cols_, tiles, *af):
            return mm([(cols_[:, i, j, :], s_[:, 128 * i:128 * i + 128], c("blk")[:, 0:65:64], True)
                       for i in range(2) for j, s_ in enumerate(tiles)], af)

        def spread(b, rs, js, *af):
            return mm([(b.t[64 * h:64 * h + 64, T * q + 128 * i:T * q + 128 * i + 128], rs[:, i, j, h:h + 1].broadcast_to([128, 64]), ident, True)
                       for q, j in enumerate(js) for i in range(2) for h in range(2)], b.free, af)

        def factors(b, rs, n, wide, eps, t, scale=1.0, floor=None):
            r, x, a_ = (z[:, 0:4 * n] for z in rs)
            if floor is None:
                t = ts(x, b.t[:, 0:4 * n], 1.0 / wide, eps, MUL, ADD, t)
            else:
                t = ts(x, b.t[:, 0:4 * n], floor, None, MAX, None, t)
            b.free = [t]
            t = root(x, r, a_, t, scale)
            return r.rearrange("p (i j h) -> p i j h", i=2, h=2), t

        def table(b, n):
            return b.t[:, 0:4 * n].rearrange("p (i j h) -> p i j h", i=2, h=2)

        def half_tanh(out, x, *af, bias=0.0):
            return act(out, x, ACT.Tanh, *af, bias=bias, scale=0.5)

        def one_plus(out, th, x, *af):
            return stt(out, th, 1.0, x, ADD, MUL, *af)

        def recip(out, a, *af):
            return V(lambda e: e.reciprocal(out, a), *af)

        def mset(out, v, *af):
            return G(lambda e: e.memset(out, v), *af)

        def mm(items, *af):
            items = list(items)
            if len(items) > 2 * STEP:
                for k in range(0, len(items), STEP):
                    t = mm(items[k:k + STEP], af if k == 0 else ())
                return t

            def f(e):
                for o, l, r, st in items:
                    x = e.matmul(o, l, r, start=st, stop=True, skip_group_check=True)
                return x
            op = PE(f, *af)
            op.cost = sum(max(64, float(np.prod(r.shape[1:]))) * 0.42e-3 * (1 if r.dtype is R else 4) + 0.02 for _, _, r, _ in items)
            return op

        def tr(items, *af):
            items = list(items)

            def f(e):
                for o, i_, idn in items:
                    x = e.transpose(o, i_, idn)
                return x
            op = PE(f, *af)
            op.cost = 0.25 * len(items)
            return op

        MUL, ADD, SUB, MAX, MIN, POW = ALU.mult, ALU.add, ALU.subtract, ALU.max, ALU.min, ALU.pow
        ident = c("id")

        class Arena:
            def __init__(self, lo, hi):
                self.lo, self.hi, self.at = lo, hi, lo

            def __call__(self, *shape, p=128, dt=F):
                n = int(np.prod(shape))
                assert self.at + n <= self.hi, ("arena", self.at + n, self.hi)
                v = (A_ if dt is F else Z_)[0:p, self.at:self.at + n]
                self.at += n
                if len(shape) == 2:
                    v = v.rearrange("p (a b) -> p a b", a=shape[0])
                if len(shape) == 3:
                    v = v.rearrange("p (a b c) -> p a b c", a=shape[0], b=shape[1])
                top[0] = max(top[0], self.at)
                if len(shape) == 4:
                    v = v.rearrange("p (a b c d) -> p a b c d", a=shape[0], b=shape[1], c=shape[2])
                return v

        top = [0]

        def two_parts(ar, *shape):
            return ar(*shape, dt=R), ar(*shape, dt=R)

        PE_, V_, Aq_, G_ = PE, V, A, G
        streams = [cur[0]]

        def mine(E):
            return cur[0].prev.get(E)

        def last():
            return [o for s_ in streams for o in s_.prev.values()]

        def barrier():
            for E in (PE_, V_, Aq_, G_):
                cur[0].fence[E] = last()

        def settle():
            for E in (PE_, V_, Aq_, G_):
                cur[0].fence[E] = list(cur[0].prev.values())

        def run(*gens):
            parent = cur[0]
            mine_ = [Stream(parent.prev, *(g if isinstance(g, tuple) else (g, 0.0))) for g in gens]
            for s_ in mine_:
                s_.fence.update(parent.fence)
            parent.fence.clear()
            live = list(mine_)
            streams[:] = mine_
            n0 = len(log)
            new, placed = set(), []
            free = dict.fromkeys(engines, max([o.end for o in parent.prev.values()] + [0.0]))
            for E in engines:
                E.hold = len(E.ops)
            while live:
                for s_ in list(live):
                    if not s_.todo:
                        cur[0], n = s_, len(log)
                        try:
                            next(s_.gen)
                        except StopIteration:
                            live.remove(s_)
                        s_.todo = log[n:]
                        new.update(id(o) for o in s_.todo)
                        if s_.todo and s_ not in live:
                            live.append(s_)
                            s_.gen = iter(())
                best = None
                for s_ in live:
                    if s_.todo:
                        o = s_.todo[0]
                        if any(id(x) in new for x in o.after):
                            continue
                        at = max([free[o.eng]] + [x.end + 0.3 for x in o.after])
                        if best is None or at - s_.ahead < best[0]:
                            best = at - s_.ahead, at, s_
                if best is None:
                    continue
                _, at, s_ = best
                o = s_.todo.pop(0)
                new.remove(id(o))
                placed.append(o)
                o.end = at + o.cost + (2.0 if o.sem is not None else 0.0)
                free[o.eng] = at + o.cost
            for E in engines:
                E.ops[E.hold:] = [o for o in placed if o.eng is E]
            for o in placed:
                o.end = 0.0
            cur[0] = parent
            parent.prev = {E: next(o for o in reversed(E.ops) if o.fn is not None) for E in engines[:4]}
            streams[:] = [parent]

        def two(b):
            return b.t[:, :].rearrange("p (t n) -> p t n", t=2)

        def proj(src, rhs, nk, bring, evac, t_rhs):
            f0 = 0
            for s_ in src:
                s, wv, tw = load(s_)
                n = s_.shape[1]
                for j in range(0, n, 256):
                    b = bring()
                    m = min(256, n - j)
                    items = []
                    for i in range(0, m, 128):
                        for k in range(nk):
                            items += mm3(b.t[:, 2 * i:2 * i + 256], cut(wv, lambda z: z[:, k, j + i:j + i + 128]),
                                         cut(rhs, lambda z: z[:, k, :]), k == 0)
                    t = mm(items, tw, t_rhs, b.free)
                    s.free.append(t)
                    b.free = evac(b, f0, (m + 127) // 128, t)
                    f0 += (m + 127) // 128
                    yield

        def cols(W, c0, c1, step=256):
            return [W[:, i:min(i + step, c1)] for i in range(c0, c1, step)]

        def to_sbuf(dst, E="A"):
            def evac(b, f0, nt, t):
                o = dst[:, f0:f0 + nt, :]
                i = two(b)[:, 0:nt, :]
                return [acp(o, i, t)] if E == "A" else [cp(o, i, t)]
            return evac

        def to_silu(dst, tmp):
            u = [None]

            def evac(b, f0, nt, t):
                t = half_tanh(tmp[:, 0:nt, :], two(b)[:, 0:nt, :], t, u[0])
                u[0] = one_plus(dst[:, f0:f0 + nt, :], tmp[:, 0:nt, :], two(b)[:, 0:nt, :], t)
                return [u[0]]
            return evac

        def proj_tok(src, bring, dst, t_rhs):
            n0 = 0
            for s_ in src:
                s, wv, tw = load(s_)
                n = s_.shape[1]
                for i in range(2):
                    b = bring()
                    t = mm([z for k in range(8) for z in mm3(b.t[:, 0:n], cut(H, lambda z: z[:, k, 128 * i:128 * i + 128]),
                                                             cut(wv, lambda z: z[:, k, :]), k == 0)], tw, t_rhs, b.free)
                    b.free = [acp(dst[:, i, n0:n0 + n], b.t[:, 0:n], t)]
                s.free = [t]
                yield
                n0 += n

        rt_ = [R_[:, 96 * j:96 * j + 96] for j in range(3)]
        rt2 = [R_[:, 288 + 8 * j:288 + 8 * j + 8] for j in range(3)]
        rt3 = [R_[:, 312 + 8 * j:312 + 8 * j + 8] for j in range(3)]

        def all_rows(b, tiles, src, t, n, eps, b2):
            x, r, a_ = (z[:, 0:2] for z in rt2)
            t = mm([(b.t[:, i:i + 1], src[:, k, 128 * i:128 * i + 128], c("ones")[:, 0:1], k == tiles[0])
                    for i in range(2) for k in tiles], t, b.free, t_cst)
            t = ts(x, b.t[:, 0:2], 1.0 / n, eps, MUL, ADD, t, t_par)
            b.free = [t]
            t = root(x, r, a_, t)
            return mm([(b2.t[:, 128 * i:128 * i + 128], r[:, i:i + 1].broadcast_to([128, 128]), ident, True) for i in range(2)],
                      t, b2.free)

        def squares(b, f0, nt, t):
            t = act(SQ[:, f0:f0 + nt, :], X[:, f0:f0 + nt, :], ACT.Square, t)
            sum_squares()
            x_todo.append((b, f0, nt, t))

        x_sum, x_todo = [], []

        def sum_squares():
            for b, f0, nt, t in x_todo:
                x_sum[:] = [b, mm([(b.t[:, i:i + 1], SQ[:, k, 128 * i:128 * i + 128], c("ones")[:, 0:1], k == 0 and i == 0)
                                   for i in range(2) for k in range(f0, f0 + nt)], t, b.free, t_cst)]
            x_todo.clear()

        def norm(key, tmp, *af):
            sum_squares()
            b, t = x_sum
            x, r, a_ = (z[:, 0:2] for z in rt2)
            t = ts(x, b.t[:, 0:2], 1.0 / DM, EPS, MUL, ADD, t, t_par)
            t = root(x, r, a_, t)
            t = mm([(b.t[:, 128 * i:128 * i + 128], r[:, i:i + 1].broadcast_to([128, 128]), ident, True) for i in range(2)], t)
            his = []
            for k in range(0, 8, 2):
                for j in (k, k + 1):
                    u = stt(tmp[:, j, :], X[:, j, :], pc(key, j), b.t[:, 0:T], MUL, MUL, t, af)
                his.append(act(H[0][:, k:k + 2, :], tmp[:, k:k + 2, :], ACT.Copy, u, af))
            b.free = [u]
            return [tt(H[1][:, k:k + 2, :], tmp[:, k:k + 2, :], H[0][:, k:k + 2, :].bitcast(F), SUB, his[k // 2], E=G if k == 0 else V)
                    for k in range(0, 8, 2)]

        def bsum(bank, src, n, lhs, *af):
            return mm([(bank.t[:, T * i:T * i + T], lhs, src[:, i, :], True) for i in range(n)], bank.free, af)

        def layernorm(y, bring, tmp, eps, across=False, tabs=None):
            b = bring()
            if across:
                f = lambda s_: [(b.t[:, T * i:T * i + T], c("ones"), s_[:, j, :], j == 0) for i in range(2) for j in range(2)]
                n = 256.0
            else:
                f = lambda s_: [(b.t[:, T * i:T * i + T], c("blk"), s_[:, i, :], True) for i in range(2)]
                n = 64.0
            t = mm(f(y), mine(V_), mine(Aq_), b.free)
            yield
            t = stt(y, two(b), -1.0 / n, y, MUL, ADD, t)
            b.free = [t]
            t = tt(tmp, y, y, MUL)
            b, b2 = bring(), bring()
            if across:
                t = all_rows(b, range(2), tmp, t, 256, eps, b2)
                yield
                f_ = b2.t[:, 0:T].unsqueeze(1).broadcast_to([128, 2, T])
            else:
                t = sums(table(b, 2), [tmp[:, i, :] for i in range(2)], t, b.free)
                yield
                r, t = factors(b, tabs, 2, 64, eps, t)
                t = spread(b2, r, (0, 1), t)
                yield
                f_ = two(b2)
            t = tt(y, y, f_, MUL, t)
            b2.free = [t]

        def sigm(x, out, *af):
            t = half_tanh(out, x, *af)
            return ts(out, out, 0.5, 0.5, MUL, ADD, t)

        def rwkv(l, pz, lora, BT, ar, bring):
            p = ar(8, T)
            ar.at -= 8 * T
            Gm = ar(2, 4, 256)
            Ym = ar(2, 4, 64)
            AR = ar(2, 4, 2, 64)
            at = bz_at = ar.at
            d = ar(8, T)
            ar.at = at
            bz, kz = ar(2, 2, T), ar(2, 2, T)
            t = tt(d, pz[:, :, 0:T], pz[:, :, 1:T + 1], SUB, last())
            for i in range(8):
                t = stt(p[:, i, :], d[:, i, :], pc(f"mu{l}", i), pz[:, i, 1:T + 1], MUL, ADD)
            r, k, v = p[:, 0:2, :], p[:, 2:4, :], p[:, 4:6, :]
            t = act(p[0:64, 6, :], p[0:64, 6, :], ACT.Tanh, t)
            b, b2 = bring(), bring()
            t_l = lora["t"]
            t1 = mm([(b.t[:, T * i:T * i + T], lora["w"][:, 128 * i:128 * i + 128], p[:, 6, :], True) for i in range(2)], t, b.free, t_l)
            t2 = mm([(b2.t[:, T * i:T * i + T], lora["a"][:, 128 * i:128 * i + 128], p[:, 6, :], True) for i in range(2)], b2.free)
            yield
            nb = ar(4)
            t = ts(nb[:, 0:2], P_[:, poff[f"w0{l}"][0]:poff[f"w0{l}"][0] + 2], 0.5, None, MUL)
            t = ts(nb[:, 2:4], P_[:, poff[f"a0{l}"][0]:poff[f"a0{l}"][0] + 2], 0.5, None, MUL)
            sig, aa, cum, kk, tmp, tm2, gg = (ar(2, T) for _ in range(7))
            for i in range(2):
                tb = half_tanh(sig[:, i, :], two(b)[:, i, :], t1, t, bias=nb[:, i:i + 1])
            b.free = [tb]
            for i in range(2):
                tb2 = half_tanh(aa[:, i, :], two(b2)[:, i, :], t2, t, bias=nb[:, 2 + i:3 + i])
            b2.free = [tb2]
            ts(sig, sig, 0.5, 0.5, MUL, ADD, tb)
            ts(aa, aa, 0.5, 0.5, MUL, ADD, tb2)
            t = sigm(p[:, 7, :], tmp[:, 0, :])
            b = bring()
            tg = mm([(b.t[:, T * i:T * i + T], lora["g"][:, 128 * i:128 * i + 128], tmp[:, 0, :], True) for i in range(2)], t, b.free)
            b.free = [acp(gg, two(b), tg)]
            yield
            for i in range(2):
                t = V(lambda e, i=i: e.tensor_tensor_scan(cum[:, i, :], c("rst"), sig[:, i, :], 0.0, MUL, ADD))
            Pp, Pi, Pm = ar(2, T), ar(2, T), ar(2, T)
            t1 = act(Pp, cum, ACT.Exp, t, scale=-RWS)
            t2 = act(Pi, cum, ACT.Exp, scale=RWS)
            t = tt(cum, cum, sig, SUB, t2)
            t3 = act(Pm, cum, ACT.Exp, t, scale=-RWS)
            for i in range(2):
                ts(kk[:, i, :], k[:, i, :], pc(f"kk{l}", i), None, MUL)
            t = tt(tmp, kk, kk, MUL, tg)
            b = bring()
            t = sums(table(b, 2), [tmp[:, i, :] for i in range(2)], t, b.free)
            yield
            r_, t = factors(b, rt3, 2, 1, 0, t, floor=1e-24)
            b = bring()
            t = spread(b, r_, (0, 1), t)
            yield
            t = tt(kk, kk, two(b), MUL, t)
            b.free = [t]
            om = ar(2)
            ts(om, P_[:, poff[f"ka{l}"][0]:poff[f"ka{l}"][0] + 2], -1.0, 1.0, MUL, ADD)
            for i in range(2):
                ts(tmp[:, i, :], aa[:, i, :], pc(f"ka{l}", i), om[:, i:i + 1], MUL, ADD)
            tt(k, k, tmp, MUL)
            ch = lambda a_: a_.rearrange("p t (c n) -> p t c n", c=4)
            for i in range(2):
                tt(AR[:, i, :, 0, :], ch(kk)[:, i], ch(Pm)[:, i], MUL, t3)
                t_ar = tt(AR[:, i, :, 1, :], ch(r)[:, i], ch(Pp)[:, i], MUL, t1)
            be, ka = sig, aa
            mset(bz, 0.0, t)
            tz = mset(kz, 0.0)
            tt(be, kk, aa, MUL)
            tt(be, be, Pi, MUL)
            t = tt(ka, k, Pi, MUL)
            for s_, z in ((be, bz), (ka, kz)):
                for q in range(2):
                    tzz = acp(z[64 * q:64 * q + 64, q, :, :], s_[64 * q:64 * q + 64, :, :], t, tz)
            yield
            for i in range(2):
                t_b = stt(tmp[:, i, :], r[:, i, :], pc(f"rk{l}", i), k[:, i, :], MUL, MUL)
            bon = tm2
            b = bring()
            t_b = bsum(b, tmp, 2, c("blk"), t_b)
            pzf = pz.rearrange("p a b -> p (a b)")
            tok = [pzf[:, 512 * j:512 * j + 512].rearrange("p (a b) -> p a b", a=2) for j in range(3)]
            b.free = [tt(bon, two(b), v, MUL, t_b)]
            for s_, dst in zip((v, be, ka), tok):
                b = bring()
                t = tr([(b.t[:, 256 * j + 128 * i:256 * j + 128 * i + 128], s_[:, i, 128 * j:128 * j + 128], ident)
                        for j in range(2) for i in range(2)], t_b, b.free, mine(V_))
                t_tok = acp(dst, two(b), t)
                b.free = [t_tok]
                yield
            vt, bt, kt = tok
            for q in range(4):
                o = 64 * (q % 2)
                rwm = c("rwm", 64, o).unsqueeze(1).broadcast_to([64, 2, 256])
                for h2 in range(2):
                    b = bring()
                    items = []
                    for hh in range(2):
                        h = 2 * h2 + hh
                        for s_, z in ((0, bz), (1, kz)):
                            a0 = 256 * hh + 128 * s_
                            items.append((b.t[o:o + 64, a0:a0 + 128], z[:, h % 2, h // 2, 64 * q:64 * q + 64],
                                          AR[:, h // 2, q, :, :], True))
                    t = mm(items, tzz, t_ar, b.free)
                    t = tt(Gm[o:o + 64, q // 2, 2 * h2:2 * h2 + 2, :], b.t[o:o + 64, :].rearrange("p (a n) -> p a n", a=2), rwm, MUL, t)
                    b.free = [t]
                    yield
            m3 = lambda a_: a_.rearrange("p a b c -> p (a b) c")
            h8 = lambda a_: a_.rearrange("p a b -> p (a b)").rearrange("p (a b) -> p a b", a=8)
            Xm, Tm, Am = h8(sig), h8(Pi), h8(Pm)
            b3 = lambda b_, hs: b_.t[hs, :].rearrange("p (a n) -> p a n", a=8)
            halves = (slice(0, 64), slice(64, 128))
            full = slice(0, 128)
            Ym8 = m3(Ym)
            for hs in halves:
                eye = ident[hs, hs].unsqueeze(1).broadcast_to([64, 8, 64])
                cp(Ym8[hs], eye)
                t_i = cp(Xm[hs], eye)
            for lv in range(6):
                msk = c("lvl")[:, 64 * lv:64 * lv + 64].unsqueeze(1).broadcast_to([128, 8, 64])
                t_a = tt(Am, m3(Gm)[:, :, 0:64], msk, MUL, t_i, E=G if lv == 0 else V)
                b = bring()
                t = mm([(b.t[hs, 64 * j:64 * j + 64], Am[hs, j, :], Xm[hs, j, :], True) for hs in halves for j in range(8)], t_a, t_i, b.free)
                yield
                t = acp(Tm, b3(b, full), t)
                b.free = [t]
                bx, by = bring(), bring()
                tx = mm([(bx.t[hs, 64 * j:64 * j + 64], Ym8[hs, j, :], Tm[hs, j, :], True) for hs in halves for j in range(8)], t, bx.free)
                ty = mm([(by.t[hs, 64 * j:64 * j + 64], Tm[hs, j, :], Ym8[hs, j, :], True) for hs in halves for j in range(8)], by.free)
                yield
                bx.free = [tt(Xm, Xm, b3(bx, full), SUB, tx, ty)]
                t_i = tt(Ym8, Ym8, b3(by, full), SUB, ty)
                by.free = [t_i]
            S = ar(2, 128)
            y = cum
            t_s = None
            for q in range(4):
                o, j = 64 * (q % 2), q // 2
                hs = slice(o, o + 64)
                W, U = tmp[hs, 0, :], tmp[hs, 1, :]
                g_ = lambda h, k_: Gm[hs, j, h, 64 * k_:64 * k_ + 64]
                b = bring()
                items = []
                for i in range(2):
                    if q:
                        items.append((b.t[hs, 128 * i:128 * i + 128], AR[:, i, q, 0, :], S[:, i, :], True))
                b2 = bring()
                t2 = mm([(b2.t[hs, 64 * h:64 * h + 64], g_(h, 2), vt[hs, j, 64 * h:64 * h + 64], True) for h in range(4)], t_tok, t_i, mine(V_), b2.free)
                if q:
                    t = mm(items, t_s, b.free)
                yield
                t = acp(W, b2.t[hs, 0:256], t2, mine(V_), mine(PE_), scale=-1.0)
                b2.free = [t]
                if q:
                    t = tt(W, W, b.t[hs, 0:256], SUB, t, t_s, mine(PE_))
                    b.free = [t]
                b = bring()
                t = mm([(b.t[hs, 64 * h:64 * h + 64], Ym[hs, j, h, :], W[:, 64 * h:64 * h + 64], True) for h in range(4)], t, b.free)
                yield
                t_u = acp(U, b.t[hs, 0:256], t)
                b.free = [t_u]
                b = bring()
                if q:
                    b2 = bring()
                    t2 = mm([(b2.t[:, 64 * i:64 * i + 64], S[:, i, :], AR[:, i, q, 1, :], True) for i in range(2)], b2.free, t_s)
                items = []
                for h in range(4):
                    po = b.t[64 * (h % 2):64 * (h % 2) + 64, 64 * (h // 2):64 * (h // 2) + 64]
                    items.append((po, U[:, 64 * h:64 * h + 64], g_(h, 1), True))
                    items.append((po, vt[hs, j, 64 * h:64 * h + 64], g_(h, 3), False))
                t = mm(items, t_u, b.free)
                yo = y[:, :, 64 * q:64 * q + 64]
                pv = lambda b_: b_.t[:, 0:128].rearrange("p (t n) -> p t n", t=2)
                b.free = [acp(yo, pv(b), t)]
                t_y = b.free
                if q < 3:
                    b = bring()
                    items = []
                    for i in range(2):
                        po = b.t[:, 128 * i:128 * i + 128]
                        items.append((po, bt[hs, j, 128 * i:128 * i + 128], U[:, 128 * i:128 * i + 128], True))
                        items.append((po, kt[hs, j, 128 * i:128 * i + 128], vt[hs, j, 128 * i:128 * i + 128], False))
                    t = mm(items, b.free)
                    yield
                    ps = b.t[:, 0:256].rearrange("p (t n) -> p t n", t=2)
                    if q:
                        t = tt(S, S, ps, ADD, t)
                        ps = S
                    for i in range(2):
                        t = stt(S[:, i, :], ps[:, i, :], Pp[:, i, 64 * q + 63:64 * q + 64], c("blk"), MUL, MUL, t)
                    t_s = t
                    b.free = [t]
                if q:
                    b2.free = [tt(yo, yo, pv(b2), ADD, t2, t_y)]
            yield from layernorm(y, bring, tmp, 64e-5, tabs=rt3)
            for i in range(2):
                ts(y[:, i, :], y[:, i, :], pc(f"lw{l}", i), pc(f"lb{l}", i), MUL, ADD)
            tt(y, y, bon, ADD)
            BT["t"] = tt(y, y, gg, MUL)
            BT["v"] = y
            BT["p"] = tuple(Z_[:, bz_at + 512 * j:bz_at + 512 * j + 512].rearrange("p (t n) -> p t n", n=T) for j in range(2))

        def kq(b, h, qk):
            r = slice(64 * (h % 2), 64 * (h % 2) + 64)
            k_, q = qk[r, 2 + h // 2, :], qk[r, h // 2, :]
            return [(b.t[:, 0:256], k_[:, 0:128], q, True), (b.t[:, 256:384], k_[:, 128:256], q[:, 128:256], False)]

        def av(b, h, v, at):
            o = b.t[64 * (h % 2):64 * (h % 2) + 64, :]
            return [(o[:, 0:256], v[:, 0, 64 * h:64 * h + 64], at[:, 0:256], True),
                    (o[:, 128:256], v[:, 1, 64 * h:64 * h + 64], at[:, 256:384], False)]

        def stick(l, qk, v, BT, ar, bA, bB):
            BT["p"] = two_parts(Arena(ar.at, ar.hi), 2, T)
            BT["v"] = qk[:, 0:2, :]
            tmp = ar(4, T)
            w_ = [ar(384), ar(384)]
            t = tt(tmp, qk, qk, MUL, last())
            t = sums(table(bA, 4), [tmp[:, i, :] for i in range(4)], t, bA.free)
            yield
            r_, t = factors(bA, rt_, 4, 64, EPS, t)
            t1 = spread(bA, r_, (0, 1), t)
            t2 = spread(bB, r_, (2, 3))
            yield
            for i in range(2):
                t = stt(qk[:, i, :], qk[:, i, :], pc(f"sq{l}"), two(bA)[:, i, :], MUL, MUL, t1)
            bA.free = [t]
            ts(qk[:, 0:2, :], qk[:, 0:2, :], 0.125, None, MUL)
            for i in range(2):
                t_k = stt(qk[:, 2 + i, :], qk[:, 2 + i, :], pc(f"sk{l}"), two(bB)[:, i, :], MUL, MUL, t2)
            bB.free = [t_k]
            tf = tmp.rearrange("p a b -> p (a b)")
            u = [tf[:, 0:384], tf[:, 512:896]]
            ends = [None, None]
            bo, b = bA, bB
            for h in range(4):
                m = h % 2
                t = mm(kq(b, h, qk), t_k, b.free)
                yield
                z = b.t[:, 0:384]
                act(u[m], z, ACT.Abs, t, t_k, ends[m])
                act(u[m], u[m], ACT.Exp, scale=-1.0)
                t = act(u[m], u[m], ACT.Ln, bias=1.0)
                t = stt(u[m], z, 0.0, u[m], MAX, ADD, t)
                for o in (0, 256):
                    t = tt(u[m][:, o:o + 128], u[m][:, o:o + 128], c("sb01"), MUL)
                t = mm([(b.t[:, 0:256], c("rneg"), u[m][:, 0:256], False),
                        (b.t[:, 256:384], c("rneg"), u[m][:, 256:384], False),
                        (b.t[:, 128:256], c("nones"), u[m][:, 256:384], False)], t)
                yield
                t = tt(w_[m], z, c("sbadd"), ADD, t, ends[m])
                b.free = [t]
                t = act(w_[m], w_[m], ACT.Exp, t)
                yield
                t = mm(av(bo, h, v, w_[m]), t, bo.free)
                ends[m] = t
                if m == 1:
                    bo.free = [acp(BT["v"][:, h // 2, :], bo.t[:, 0:256], t)]
                    BT["t"] = bo.free[0]
            yield

        def rotate(src, n, perm, cos, sin, bring, tmp, tm2, dst, *af):
            for i in range(0, n, 2):
                b = bring()
                s_ = src[:, i:i + 2, :]
                t = mm([(b.t[:, T * j:T * j + T], c(perm), s_[:, j, :], True) for j in range(2)], b.free, af)
                bc = lambda k_: c(k_).unsqueeze(1).broadcast_to([128, 2, T])
                tt(tmp, s_, bc(cos), MUL, af)
                t = tt(tm2, two(b), bc(sin), MUL, t)
                b.free = [t]
                dst(i, tmp, tm2)
                yield

        def retention(l, qk, g, v, BT, ar, bring):
            BT["p"] = two_parts(Arena(ar.at, ar.hi), 2, T)
            tmp, tm2 = ar(2, T), ar(2, T)
            tok = {}

            def dst(i, a_, b_):
                tok[i] = tt(qk[:, i:i + 2, :], a_, b_, ADD)
            yield from rotate(qk, 4, "pr", "cr", "sr", bring, tmp, tm2, dst, last())
            y = qk[:, 0:2, :]
            BT["v"] = y
            u = [a_.rearrange("p a b -> p (a b)")[:, 0:384] for a_ in (tmp, tm2)]
            ends = [None, None]
            bo, b = bring(), bring()
            for h in range(4):
                m = h % 2
                t = mm(kq(b, h, qk), tok[0], tok[2], b.free)
                yield
                d = c("dec")[:, T * h:T * h + T]
                t1 = tt(u[m][:, 0:256], b.t[:, 0:256], d, MUL, t, ends[m])
                t = tt(u[m][:, 256:384], b.t[:, 256:384], d[:, 0:128], MUL)
                b.free = [t]
                t = mm(av(bo, h, v, u[m]), t, bo.free)
                ends[m] = t
                if m == 1:
                    bo.free = [acp(y[:, h // 2, :], bo.t[:, 0:256], t)]
                yield
            yield from layernorm(y, bring, tmp, 1e-5, tabs=rt_)
            for i in range(2):
                ts(y[:, i, :], y[:, i, :], pc(f"gn{l}", i), None, MUL)
            t = half_tanh(tmp, g, mine(V_))
            one_plus(tmp, tmp, g, t)
            BT["t"] = stt(y, y, 0.5, tmp, MUL, MUL)

        def conformer(l, ab, BT, ar, bring):
            BT["p"] = two_parts(Arena(ar.at, ar.hi), 2, T)
            up = ar(2, 286)
            acc, e_ = ab[:, 0:2, :], ab[:, 2:4, :]
            BT["v"] = acc
            tz = mset(up[:, :, 0:30], 0.0)
            t = sigm(ab[:, 2:4, :], e_, last())
            t = tt(up[:, :, 30:286], ab[:, 0:2, :], e_, MUL, tz)
            o = poff[f"dw{l}"][0]
            for i in range(2):
                ts(acc[:, i, :], up[:, i, 0:T], P_[:, o + 31 * i:o + 31 * i + 1], pc(f"cb{l}", i), MUL, ADD)
            for j in range(1, 31):
                for i in range(2):
                    stt(acc[:, i, :], up[:, i, j:j + T], P_[:, o + 31 * i + j:o + 31 * i + j + 1], acc[:, i, :], MUL, ADD)
                if j % 3 == 0:
                    yield
            yield from layernorm(acc, bring, e_, 1e-5, across=True)
            for i in range(2):
                t = ts(acc[:, i, :], acc[:, i, :], pc(f"cw{l}", i), pc(f"cl{l}", i), MUL, ADD)
            t = half_tanh(e_, acc, t)
            one_plus(e_, e_, acc, t)
            BT["t"] = ts(acc, e_, 0.5, None, MUL)

        def gates(l, i, M, bring, *af):
            for u in range(4):
                s, wv, tw = load(w["w_gate"][l, i][:, 256 * u:256 * u + 256])
                b = bring()
                t = mm([z for q in range(2) for k in range(8) for z in
                        mm3(b.t[:, T * q:T * q + T], cut(wv, lambda z: z[:, k, 128 * q:128 * q + 128]), cut(H, lambda z: z[:, k, :]), k == 0)],
                       tw, b.free)
                s.free = [t]
                b.free = [half_tanh(M[:, 2 * u:2 * u + 2, :], two(b), t, af)]
                yield

        def branch(BP, s, wv, tB, tB_, b2, f0, j0):
            t = mm([z for q in range(2) for k in range(2) for z in
                    mm3(b2.t[:, T * q:T * q + T], cut(wv, lambda z: z[:, k, j0 + 128 * q:j0 + 128 * q + 128]), cut(BP, lambda z: z[:, k, :]), k == 0)],
                   tB, tB_, b2.free)
            s.free = [t]
            return t

        def gated(l, i, BT, M, bring):
            tB_ = split(BT["p"], BT["v"], BT["t"])
            s, wv, tB = load(w["w_branch"][l, i])
            for u in range(4):
                b2 = bring()
                t = branch(BT["p"], s, wv, tB, tB_, b2, 2 * u, 256 * u)
                Mo = M[:, 2 * u:2 * u + 2, :]
                b2.free = [one_plus(Mo, Mo, two(b2), t, mine(Aq_))]
            yield

        def merge(l, i, BT, M, e_, bring, MP=None, free=None):
            BP = BT["p"]
            tB_ = split(BP, BT["v"], BT["t"])
            for u in range(4):
                s, wv, tw = load(w["w_gate"][l, i][:, 256 * u:256 * u + 256])
                sB, wB, tB = load(w["w_branch"][l, i][:, 256 * u:256 * u + 256])
                b, b2 = bring(), bring()
                t = mm([z for q in range(2) for k in range(8) for z in
                        mm3(b.t[:, T * q:T * q + T], cut(wv, lambda z: z[:, k, 128 * q:128 * q + 128]), cut(H, lambda z: z[:, k, :]), k == 0)],
                       tw, b.free)
                s.free = [t]
                t2 = branch(BP, sB, wB, tB, tB_, b2, 2 * u, 0)
                e = e_()
                t = half_tanh(e["v"], two(b), t, e["t"])
                b.free = [t]
                tm = one_plus(e["v"], e["v"], two(b2), t, t2)
                b2.free = [tm]
                Mo = M[:, 2 * u:2 * u + 2, :]
                tm = tt(Mo, Mo, e["v"], ADD)
                if MP is not None:
                    hi, lo = cut(MP, lambda z: z[:, 2 * u:2 * u + 2, :])
                    tm = acp(hi, Mo, tm, free, scale=0.5)
                    tm = stt(lo, Mo, 0.5, hi.bitcast(F), MUL, SUB, tm)
                e["t"] = tm
                yield

        def residual(b, f0, nt, t):
            t = tt(X[:, f0:f0 + nt, :], X[:, f0:f0 + nt, :], two(b)[:, 0:nt, :], ADD, t)
            squares(banks[4], f0, nt, t)
            return [t]

        def mix_block(l):
            barrier()
            ar = Arena(0, ARENA)
            pz = ar(8, T + 1)
            M = ar(8, T)
            es = Ring([dict(v=ar(2, T), t=None) for _ in range(2)])
            BT = [dict() for _ in range(4)]
            own = ar.at
            MP = two_parts(Arena(own, ARENA), 8, T)
            qk, v = ar(4, T), ar(2, T)
            sub1 = Arena(ar.at, ar.at + 1792)
            ar.at = sub1.hi
            two_at = ar.at
            rqk, rv, rg = ar(4, T), ar(2, T), ar(2, T)
            ab = rqk
            sub2 = Arena(two_at + 4 * T, two_at + 8 * T)
            sub3 = Arena(ar.at, ar.at + 4 * T)
            rw_ar = Arena(sub3.hi, ARENA)
            la = Arena(rw_ar.lo + 8 * T + 512, ARENA)
            lora = {k: la(256) for k in "wag"}
            zt = [mset(pz[:, :, 0:1], 0.0), mset(lora["w"][64:128, :], 0.0), mset(lora["a"][0:64, :], 0.0)]
            t1 = dma(Aq_, "l0", lambda e: e.dma_start(lora["w"][0:64, :], w["rw_w2"][l]), zt)
            t2 = dma(Aq_, "l1", lambda e: e.dma_start(lora["a"][64:128, :], w["rw_a2"][l]), zt)
            t3 = dma(Aq_, "l2", lambda e: e.dma_start(lora["g"], w["rw_g2"][l]), zt)
            lora["t"] = [t1, t2, t3]
            t_h = norm(f"nm{l}", M, zt)
            W = w["w_in"][l]
            first = Ring(banks[0:4])

            def ev(b, f0, nt, t):
                return [acp(pz[:, f0:f0 + nt, 1:T + 1], two(b)[:, 0:nt, :], t)]
            for _ in proj(cols(W, 0, 1024), H, 8, first, ev, t_h):
                pass
            first_consts()
            for E in (PE_, V_, Aq_, G_):
                cur[0].fence[E] = t_c1
            have = set()

            def until(k_):
                while k_ not in have:
                    yield

            def stick_(bA, bB):
                yield from until("stick in")
                yield from stick(l, qk, v, BT[1], sub1, bA, bB)
                have.add("stick")

            def conf_ret(bring):
                yield from until("conformer in")
                yield from conformer(l, ab, BT[3], sub2, bring)
                have.add("conformer")
                yield from until("retention in")
                settle()
                yield from retention(l, rqk, rg, rv, BT[2], sub3, bring)
                have.add("retention")

            def rwkv_(bring):
                yield from rwkv(l, pz, lora, BT[0], rw_ar, bring)
                have.add("rwkv")

            def bulk_(bring):
                yield from proj(cols(W, 2816, 3328), H, 8, bring, to_sbuf(ab), t_h)
                have.add("conformer in")
                yield from proj(cols(W, 1024, 1536), H, 8, bring, to_sbuf(qk), t_h)
                yield from proj_tok([W[:, 1536:1792]], bring, v, t_h)
                have.add("stick in")
                yield from gates(l, 3, M, bring)
                yield from until("conformer")
                yield from gated(l, 3, BT[3], M, bring)
                barrier()
                yield from proj(cols(W, 1792, 2304), H, 8, bring, to_sbuf(rqk), t_h)
                yield from proj_tok([W[:, 2304:2560]], bring, rv, t_h)
                yield from proj([W[:, 2560:2816]], H, 8, bring, to_sbuf(rg), t_h)
                have.add("retention in")
                yield from until("stick")
                yield from merge(l, 1, BT[1], M, es, bring)
                yield from until("retention")
                yield from merge(l, 2, BT[2], M, es, bring)
                yield from until("rwkv")
                yield from merge(l, 0, BT[0], M, es, bring, MP, last())

            run(bulk_(Ring(banks[0:2])), stick_(banks[2], banks[3]), conf_ret(Ring(banks[4:6])), rwkv_(Ring(banks[6:8])))
            for _ in proj(cols(w["w_out"][l], 0, 1024), MP, 8, first, residual, last()):
                pass

        def swiglu(w1, w3, hid, nt, bring, es, t_h, gate=None, free=None):
            n = nt * 128
            t = None
            for c0 in range(0, n, 256):
                c1 = min(c0 + 256, n)
                s1, v1, t1 = load(w1[:, c0:c1])
                s3, v3, t3 = load(w3[:, c0:c1])
                m = (c1 - c0) // 128
                b, b2 = bring(), bring()
                ts_ = []
                for (bb, vv, tw, ss) in ((b, v1, t1, s1), (b2, v3, t3, s3)):
                    t = mm([z for q in range(m) for k in range(8) for z in
                            mm3(bb.t[:, T * q:T * q + T], cut(vv, lambda z: z[:, k, 128 * q:128 * q + 128]), cut(H, lambda z: z[:, k, :]), k == 0)],
                           tw, t_h, bb.free)
                    ss.free = [t]
                    ts_.append(t)
                gb, t_g = gate() if gate is not None else (None, None)
                e = es()
                ev = e["v"][:, 0:m, :]
                t = half_tanh(ev, two(b)[:, 0:m, :], ts_[0], e["t"])
                t = one_plus(ev, ev, two(b)[:, 0:m, :], t)
                b.free = [t]
                f0 = c0 // 128
                t = stt(ev, ev, 0.5, two(b2)[:, 0:m, :], MUL, MUL, ts_[1])
                b2.free = [t]
                if gate is not None:
                    t = tt(ev, ev, gb.unsqueeze(1).broadcast_to([128, m, T]), MUL, t_g)
                t = split(cut(hid, lambda z: z[:, f0:f0 + m, :]), ev, t, free)
                e["t"] = t
                yield t

        def down(w2, hid, nt, acc, first, t_hid):
            for k0 in range(0, nt, 2):
                k1 = min(nt, k0 + 2)
                s, wv, tw = load(w2[128 * k0:128 * k1, :])
                items = []
                for k in range(k0, k1):
                    for d in range(8):
                        items += mm3(acc[d // 2].t[:, T * (d % 2):T * (d % 2) + T], cut(wv, lambda z: z[:, k - k0, 128 * d:128 * d + 128]),
                                     cut(hid, lambda z: z[:, k, :]), first and k == 0 and d % 2 == 0)
                t = mm(items, tw, t_hid[k0 // 2], [b.free for b in acc] if first and k0 == 0 else None)
                s.free = [t]
                yield t

        def add_acc(acc, t, more=True):
            for j in range(4):
                u = tt(X[:, 2 * j:2 * j + 2, :], X[:, 2 * j:2 * j + 2, :], two(acc[j]), ADD, t)
                acc[j].free = [u]
                if more:
                    squares(banks[0], 2 * j, 2, u)

        def ffn(l):
            barrier()
            ar = Arena(0, ARENA)
            tmp = ar(8, T)
            t_h = norm(f"nf{l}", tmp)
            hid = two_parts(ar, 22, T)
            es = Ring([dict(v=ar(2, T), t=None) for _ in range(2)])
            ts_ = []
            dn = down(w["ffn_w2"][0], hid, 22, banks[4:8], True, ts_)
            for n, t in enumerate(swiglu(w["ffn_w1"][0], w["ffn_w3"][0], hid, 22, Ring(banks[0:4]), es, t_h)):
                ts_.append(t)
                if n > 0:
                    next(dn)
            for t in dn:
                pass
            add_acc(banks[4:8], t)

        def moe(l):
            barrier()
            ar = Arena(0, ARENA)
            tmp = ar(8, T)
            t_h = norm(f"nf{l}", tmp)
            b = banks[0]
            o = poff["rt"][0]
            rtp = two_parts(ar, 64)
            t = split(rtp, P_[:, o:o + 64])
            t = mm([z for i in range(2) for k in range(8) for z in
                    mm3(b.t[:, 8 * i:8 * i + 8], cut(H, lambda z: z[:, k, 128 * i:128 * i + 128]), cut(rtp, lambda z: z[:, 8 * k:8 * k + 8]), k == 0)],
                   t_h, t, b.free)
            lg, mx, gt, e1 = ar(2, 8), ar(2, 8), ar(2, 8), ar(2, 8)
            idx = ar(2, 8).bitcast(U32)
            fx, gs = ar(2, 8), ar(2, 8)
            t = cp(lg, b.t[:, 0:16].rearrange("p (i e) -> p i e", i=2), t)
            b.free = [t]
            for i in range(2):
                V(lambda e, i=i: e.max(mx[:, i, :], lg[:, i, :]))
                V(lambda e, i=i: e.max_index(idx[:, i, :], mx[:, i, :], lg[:, i, :]))
                cp(fx[:, i, :], idx[:, i, :])
                t = tt(gs[:, i, 0:1], mx[:, i, 1:2], mx[:, i, 0:1], SUB)
                t = act(gs[:, i, 0:1], gs[:, i, 0:1], ACT.Exp, t)
                ts(gs[:, i, 1:2], gs[:, i, 0:1], 1.0, None, ADD, None, t)
                recip(gs[:, i, 1:2], gs[:, i, 1:2])
                tt(gs[:, i, 2:3], gs[:, i, 0:1], gs[:, i, 1:2], MUL)
                ts(gt[:, i, :], c("iota"), fx[:, i, 0:1], gs[:, i, 1:2], ALU.is_equal, MUL)
                ts(e1[:, i, :], c("iota"), fx[:, i, 1:2], gs[:, i, 2:3], ALU.is_equal, MUL)
                t = tt(gt[:, i, :], gt[:, i, :], e1[:, i, :], ADD)
            gT = ar(T, p=8)
            t_gt = t
            got = []

            def gates_T():
                if not got:
                    b = banks[1]
                    t = tr([(b.t[0:8, 128 * i:128 * i + 128], gt[:, i, :], ident) for i in range(2)], t_gt, b.free)
                    got.append(acp(gT, b.t[0:8, 0:T], t))
                    b.free = [got[0]]
                return got[0]
            hids = [two_parts(ar, 11, T) for _ in range(2)]
            gbs = [ar(T) for _ in range(2)]
            es = Ring([dict(v=ar(2, T), t=None) for _ in range(2)])
            bring = Ring(banks[2:4] + banks[0:1])
            t_d = [None, None]
            pend = iter(())
            for x in range(8):
                gb = gbs[x % 2]
                ready = []

                def gate(x=x, gb=gb, ready=ready):
                    if not ready:
                        t_g, b = gates_T(), banks[1]
                        t = mm([(b.t[:, 0:T], ident[0:8, x:x + 1].broadcast_to([8, 128]), gT, True)], t_g, b.free)
                        ready.append(acp(gb, b.t[:, 0:T], t, mine(V_)))
                        b.free = [ready[0]]
                    return gb, ready[0]
                ts_ = []
                for t in swiglu(w["moe_w1"][0, x], w["moe_w3"][0, x], hids[x % 2], 11, bring, es, t_h, gate, t_d[x % 2]):
                    ts_.append(t)
                    for t_d[(x - 1) % 2] in pend:
                        break
                for t_d[(x - 1) % 2] in pend:
                    pass
                pend = down(w["moe_w2"][0, x], hids[x % 2], 11, banks[4:8], x == 0, ts_)
            for t in pend:
                pass
            add_acc(banks[4:8], t)

        def attend(cases, e, bring, lag):
            for _ in range(lag):
                yield
            for (ready, qs, fq, keys, vals, o_dst) in cases:
                while ready() is None:
                    yield
                at, b, bs, spans = 0, None, [], []
                for k_, mk in keys:
                    n = k_.shape[1]
                    if b is None or at + n > 512:
                        b, at = bring(), 0
                        bs.append(b)
                    spans.append((b, at, n, mk))
                    at += n
                tok = [mm([(b.t[:, s_[1]:s_[1] + s_[2]], qs[j], k_, True) for j, (s_, (k_, _)) in enumerate(zip(spans, keys)) if s_[0] is b],
                          ready(), b.free) for b in bs]
                yield
                pos = 0
                for f_, (b, a0, n, mk) in zip(fq, spans):
                    t = stt(e["v"][:, pos:pos + n], b.t[:, a0:a0 + n], f_, mk, MUL, ADD, tok, e["t"])
                    b.free = [t]
                    pos += n
                V(lambda en, e=e, pos=pos: en.tensor_reduce(e["m"][:, 0:1], e["v"][:, 0:pos], AX.X, MAX))
                t = ts(e["m"][:, 1:2], e["m"][:, 0:1], -1.0, None, MUL)
                t = act(e["v"][:, 0:pos], e["v"][:, 0:pos], ACT.Exp, t, bias=e["m"][:, 1:2], acc=e["m"][:, 2:3])
                yield
                t_r = recip(e["m"][:, 3:4], e["m"][:, 2:3], t)
                blk = pos // 128
                pt = []
                for j0 in range(0, blk, 4):
                    j1 = min(blk, j0 + 4)
                    b = bring()
                    tp = tr([(b.t[:, 128 * (j - j0):128 * (j - j0) + 128], e["v"][:, 128 * j:128 * j + 128], ident) for j in range(j0, j1)], t, b.free)
                    pt.append(acp(e["p"][:, 128 * j0:128 * j1], b.t[:, 0:128 * (j1 - j0)], tp, e["t"]))
                    b.free = [pt[-1]]
                yield
                bo = bring()
                to = mm([(bo.t[:, 0:64], e["p"][:, 128 * j:128 * j + 128], vals[j], j == 0) for j in range(blk)], pt, bo.free)
                t = ts(o_dst, bo.t[:, 0:64], e["m"][:, 3:4], None, MUL, None, to, t_r)
                bo.free = [t]
                e["t"] = t
                yield

        class QK:

            def __init__(self, raw, n, b, sq, free):
                self.raw, self.n, self.b, self.sq, self.todo, self.k, self.t = raw, n, b, sq, [], 0, [free, b.free]

            def evac(self, b, f0, nt, t):
                m = self.k % 2
                self.k += 1
                t1 = acp(self.raw[:, f0:f0 + nt, :], two(b)[:, 0:nt, :], t)
                t2 = act(self.sq[m][:, 0:nt, :], two(b)[:, 0:nt, :], ACT.Square, t, self.t)
                self.flush()
                self.todo = [(f0 + i, self.sq[m][:, i, :], t2) for i in range(nt)]
                return [t2]

            def flush(self):
                for j, s_, t in self.todo:
                    self.t = mm([(table(self.b, self.n)[:, i, j, :], s_[:, 128 * i:128 * i + 128], c("blk")[:, 0:65:64], True)
                                 for i in range(2)], t, self.t)
                self.todo = []

            def factors(self):
                self.flush()
                r, t = factors(self.b, rt_, self.n, 64, EPS, self.t)
                t = ts(r[:, :, 0:self.n // 2, :], r[:, :, 0:self.n // 2, :], 0.125, None, MUL)
                return r, t

        def qk_ready(raw, tiles, ready, rs, t_rs, tmps, bring):
            for n, (j, key, is_k, name) in enumerate(tiles):
                tmp, tm2, un = (tmps[3 * (n % 2) + z][:, 0, :] for z in range(3))
                b = bring()
                if is_k:
                    t = spread(b, rs, [j], t_rs)
                    t = stt(un, raw[:, j, :], pc(key), b.t[:, 0:T], MUL, MUL, t)
                else:
                    t = ts(un, raw[:, j, :], pc(key), None, MUL, None, t_rs)
                t2 = mm([(b.t[:, T:2 * T], c("pp"), un, True)], t, b.free)
                tp = tt(tmp, un, c("cp"), MUL, t, E=G)
                t = tt(tm2, b.t[:, T:2 * T], c("sp"), MUL, t2)
                b.free = [t]
                t = tt(raw[:, j, :], tmp, tm2, ADD, tp)
                if name is not None:
                    ready[name] = t
                yield

        def softplus(x, a_, b_):
            t = act(a_, x, ACT.Abs, mine(V_))
            act(a_, a_, ACT.Exp, scale=-1.0)
            t = act(a_, a_, ACT.Ln, bias=1.0)
            return stt(x, x, 0.0, a_, MAX, ADD, t)

        t_c2 = []

        def second_consts():
            t_c2.append(dma(Aq_, "c2", lambda e: e.dma_start(CT["c2"][:, 0:offsets(CONSTS["c2"])[1]], cst["c2"]), t_c1, last()))

        def even():
            barrier()
            W = w["even_w_in_2"][0]
            ar = Arena(0, ARENA)
            xbc, zs = ar(16, T), ar(8, T)
            t_h = norm("en", zs, t_c2)
            dtT, dtm, cs = ar(T, p=16), ar(T, p=16), ar(T, p=16)
            tokd, nA = ar(2, 2, 16), ar(1, p=16)
            at = ar.at
            xd, cbm = ar(2, 1024), ar(384)
            us = [ar(384), ar(384)]
            second = Arena(8 * T, ar.at)
            raw_at = ar.at
            raw, v, g_, oT = ar(24, T), ar(2, 1536), ar(4, T), ar(4, T)
            tmps = [ar(1, T) for _ in range(6)]
            gt = ar(2, T)
            pa = Arena(at, at + 2048)
            pad = Ring([dict(v=pa(2, T + 3), t=None) for _ in range(2)])
            acc = pa(2, T)
            tz = [mset(p_["v"][:, :, 0:3], 0.0) for p_ in pad.items]
            cw, cbi = ar(16, 4), ar(16)
            t_cw = ts(cw, P_[:, poff["ecw"][0]:poff["ecw"][0] + 64].rearrange("p (a b) -> p a b", a=16), 0.5, None, MUL, None, t_par)
            ts(cbi, P_[:, poff["ecb"][0]:poff["ecb"][0] + 16], 0.5, None, MUL)
            bulk = Ring(banks[0:8])

            def ev(b, f0, nt, t):
                p_ = pad()
                t = acp(p_["v"][:, 0:nt, 3:T + 3], two(b)[:, 0:nt, :], t, tz, p_["t"])
                for i in range(nt):
                    f = f0 + i
                    ts(acc[:, i, :], p_["v"][:, i, 0:T], cw[:, f, 0:1], cbi[:, f:f + 1], MUL, ADD, t)
                    for j in range(1, 4):
                        u = stt(acc[:, i, :], p_["v"][:, i, j:j + T], cw[:, f, j:j + 1], acc[:, i, :], MUL, ADD)
                p_["t"] = u
                xo = xbc[:, f0:f0 + nt, :]
                u = act(xo, acc[:, 0:nt, :], ACT.Tanh, u)
                one_plus(xo, xo, acc[:, 0:nt, :], u)
                return [t]
            for _ in proj(cols(W, 1024, 3072), H, 8, bulk, ev, t_h):
                pass

            def evd(b, f0, nt, t):
                return [acp(dtT, b.t[0:16, 0:T], t)]
            for _ in proj([W[:, 3072:3200]], H, 8, bulk, evd, t_h):
                pass
            for _ in proj(cols(W, 0, 1024), H, 8, bulk, to_silu(zs, gt), t_h):
                pass

            def ssd(bring):
                t = ts(dtT, dtT, pc("edt", 0, 0, 16), None, ADD, None, mine(Aq_))
                softplus(dtT, dtm, None)
                t = act(nA, pc("eal", 0, 0, 16), ACT.Exp)
                ts(nA, nA, -1.0, None, MUL, None, t)
                ts(dtm, dtT, nA, None, MUL)
                t = V(lambda e: e.tensor_tensor_scan(cs, c("ones", 16)[:, 0:1].broadcast_to([16, T]), dtm, 0.0, MUL, ADD))
                yield
                b = bring()
                t = tr([(b.t[:, 16 * (2 * s_ + i):16 * (2 * s_ + i) + 16], src[:, 128 * i:128 * i + 128], ident[0:16, 0:16])
                        for s_, src in enumerate((dtT, cs)) for i in range(2)], t, b.free)
                t_dt = cp(tokd, b.t[:, 0:64].rearrange("p (s i h) -> p s i h", s=2, i=2), t)
                b.free = [t_dt]
                yield
                for i in range(2):
                    for f0 in (0, 4):
                        b = bring()
                        t = tr([(b.t[:, 128 * j:128 * j + 128], xbc[:, f0 + j, 128 * i:128 * i + 128], ident) for j in range(4)], mine(V_), b.free)
                        t = tt(xd[:, i, 128 * f0:128 * f0 + 512].rearrange("p (h n) -> p h n", n=64),
                               b.t[:, :].rearrange("p (h n) -> p h n", n=64),
                               tokd[:, 0, i, 2 * f0:2 * f0 + 8].unsqueeze(2).broadcast_to([128, 8, 64]), MUL, t)
                        b.free = [t]
                        yield
                t_xd = t
                mask = c("ssd")
                ends = [None, None]
                for g in range(4):
                    Bt, Ct = xbc[:, 8 + g, :], xbc[:, 12 + g, :]
                    b = bring()
                    t = mm([(b.t[:, 0:256], Bt[:, 0:128], Ct, True), (b.t[:, 256:384], Bt[:, 128:256], Ct[:, 128:256], True)], t_xd, b.free)
                    tt(cbm[:, 0:256], b.t[:, 0:256], mask, MUL, t)
                    t = tt(cbm[:, 256:384], b.t[:, 256:384], mask[:, 0:128], MUL)
                    b.free = [t]
                    for hh in range(4):
                        h = 4 * g + hh
                        m = h % 2
                        b = bring()
                        t = mm([(b.t[:, 0:T], ident[0:16, h:h + 1].broadcast_to([16, 128]), cs, True)], t_dt, b.free)
                        u = us[m]
                        ts(u[:, 0:256], b.t[:, 0:256], tokd[:, 1, 0, h:h + 1], 0.0, SUB, MIN, t, ends[m])
                        t = ts(u[:, 256:384], b.t[:, 128:256], tokd[:, 1, 1, h:h + 1], 0.0, SUB, MIN)
                        b.free = [t]
                        t = act(u, u, ACT.Exp, t)
                        t_u = tt(u, u, cbm, MUL, t)
                        yield
                        if m == 0:
                            bo = bring()
                        o = bo.t[64 * m:64 * m + 64, :]
                        t = mm([(o[:, 0:256], xd[:, 0, 64 * h:64 * h + 64], u[:, 0:256], True),
                                (o[:, 128:256], xd[:, 1, 64 * h:64 * h + 64], u[:, 256:384], False)], t_u, bo.free, t_xd)
                        ends[m] = t
                        if m == 1:
                            f = h // 2
                            t = stt(xbc[:, f, :], xbc[:, f, :], pc("eds", f), bo.t[:, 0:T], MUL, ADD, t)
                            bo.free = [t]
                y = xbc[:, 0:8, :]
                stt(y, y, 0.5, zs, MUL, MUL)
                t = tt(zs, y, y, MUL)
                for g in range(4):
                    b, b2 = bring(), bring()
                    t2 = all_rows(b, range(2 * g, 2 * g + 2), zs, t, 256, EPS, b2)
                    for j in range(2):
                        f = 2 * g + j
                        u = stt(y[:, f, :], y[:, f, :], pc("esn", f), b2.t[:, 0:T], MUL, MUL, t2)
                    b2.free = [u]
                    yield

            fac = []

            def dil_proj():
                b_ = Ring(banks[4:7])
                q_ = QK(raw, 24, banks[7], [oT[:, 0:2, :], oT[:, 2:4, :]], [])
                yield from proj(cols(W, 3088, 6160), H, 8, b_, q_.evac, t_h)
                fac.append(q_.factors())
                yield from proj_tok(cols(W, 6160, 7696), b_, v, t_h)
                yield from proj(cols(W, 7696, 8208), H, 8, b_, to_silu(g_, gt), t_h)
            tiles, ready = [], {}
            for hp in range(4):
                tiles += [(4 * g + hp, "eqn", False, None) for g in range(3)]
                tiles += [(12 + 4 * g + hp, "ekn", True, hp if g == 2 else None) for g in range(3)]

            def queries_keys():
                while not fac:
                    yield
                yield from qk_ready(raw, tiles, ready, *fac[0], tmps, Ring([banks[3], banks[7]]))
            run((dil_proj(), 0.5), ssd(Ring(banks[0:3])), queries_keys())
            barrier()
            o_tok = second(2, 512)
            es = [dict(v=second(768), p=second(768), m=second(4), t=None) for _ in range(4)]
            dm = c("dil").rearrange("p (g n) -> p g n", g=3)
            bk = Ring(banks[0:2])
            rs = fac[0][0]
            cases = []
            for hp in range(4):
                for hh in range(2):
                    h, r = 2 * hp + hh, slice(64 * hh, 64 * hh + 64)
                    for i in range(2):
                        n = 128 * (i + 1)
                        cases.append((lambda hp=hp: ready.get(hp), [raw[r, 4 * g + hp, 128 * i:128 * i + 128] for g in range(3)],
                                      [rs[:, i, 4 * g + hp, hh:hh + 1] for g in range(3)],
                                      [(raw[r, 12 + 4 * g + hp, 0:n], dm[:, g, 256 - n:256]) for g in range(3)],
                                      [v[:, j, 64 * (8 * g + h):64 * (8 * g + h) + 64] for g in range(3) for j in range(i + 1)],
                                      o_tok[:, i, 64 * h:64 * h + 64]))
            it = iter(cases)
            run(*(attend(it, es[z], Ring(banks[2 * z:2 * z + 2]), z) for z in range(4)))
            for i in range(2):
                b = bk()
                t = tr([(b.t[:, 128 * j:128 * j + 128], o_tok[:, i, 128 * j:128 * j + 128], ident) for j in range(4)], mine(V_), b.free)
                t = acp(oT[:, :, 128 * i:128 * i + 128], b.t[:, :].rearrange("p (j n) -> p j n", j=4), t)
                b.free = [t]
            t = stt(oT, oT, 0.5, g_, MUL, MUL, t)
            out_proj(w["even_w_out_2"][0], [xbc[:, k:k + 2, :] for k in range(0, 8, 2)] + [oT[:, 0:2, :], oT[:, 2:4, :]],
                     two_parts(Arena(raw_at, ARENA), 12, T), 12, t, True)

        def out_proj(W, src, parts_, nt, t, more):
            ts_ = [split(cut(parts_, lambda z: z[:, 2 * k:2 * k + 2, :]), s_, t) for k, s_ in enumerate(src)]
            for t in down(W, parts_, nt, banks[4:8], True, ts_):
                pass
            add_acc(banks[4:8], t, more)

        def odd():
            barrier()
            W = w["odd_w_in_2"][0]
            ar = Arena(0, ARENA)
            raw = ar(16, T)
            t_h = norm("on", raw[:, 0:8, :], t_c2)
            bulk = Ring(banks[0:8])
            v, g_, oT = ar(2, 1024), ar(8, T), ar(8, T)
            q_ = QK(raw, 16, banks[7], [oT[:, 0:2, :], oT[:, 2:4, :]], [])
            fac, ready = [], {}
            o_tok = ar(2, 1024)
            tmps = [ar(1, T) for _ in range(6)]
            causal = ar(256)
            mset(causal[:, 0:128], 0.0)
            tz = cp(causal[:, 128:256], c("dil")[:, 128:256], mine(G_))
            es = [dict(v=ar(256), p=ar(256), m=ar(4), t=tz) for _ in range(4)]
            gt = ar(2, T)
            rs = rt_[0][:, 0:64].rearrange("p (i j h) -> p i j h", i=2, h=2)
            tiles = []
            for hp in range(8):
                tiles += [(hp, "oqn", False, None), (8 + hp, "okn", True, hp)]
            cases = []
            for hp in range(8):
                for hh in range(2):
                    h, r = 2 * hp + hh, slice(64 * hh, 64 * hh + 64)
                    for i in range(2):
                        cases.append((lambda hp=hp: ready.get("v") and ready.get(hp) and [ready["v"], ready[hp]],
                                      [raw[r, hp, 128 * i:128 * i + 128]], [rs[:, i, hp, hh:hh + 1]],
                                      [(raw[r, 8 + hp, 0:128 * i + 128], causal[:, 128 - 128 * i:256])],
                                      [v[:, j, 64 * h:64 * h + 64] for j in range(i + 1)],
                                      o_tok[:, i, 64 * h:64 * h + 64]))
            it = iter(cases)

            def projections(bring):
                yield from proj(cols(W, 0, 2048), H, 8, bring, q_.evac, t_h)
                fac.append(q_.factors())
                yield from proj_tok(cols(W, 2048, 3072), bring, v, t_h)
                ready["v"] = mine(Aq_)
                yield from proj(cols(W, 3072, 4096), H, 8, bring, to_silu(g_, gt), t_h)

            def queries_keys():
                while not fac:
                    yield
                yield from qk_ready(raw, tiles, ready, *fac[0], tmps, Ring([banks[6], banks[7]]))
            run((projections(Ring(banks[4:6])), 0.5), queries_keys(), *(attend(it, es[z], Ring(banks[z:z + 1]), z) for z in range(4)))
            bk = Ring(banks[0:2])
            for i in range(2):
                for f0 in (0, 4):
                    b = bk()
                    t = tr([(b.t[:, 128 * j:128 * j + 128], o_tok[:, i, 128 * (f0 + j):128 * (f0 + j) + 128], ident) for j in range(4)],
                           mine(V_), b.free)
                    t = acp(oT[:, f0:f0 + 4, 128 * i:128 * i + 128], b.t[:, :].rearrange("p (j n) -> p j n", j=4), t)
                    b.free = [t]
            t = stt(oT, oT, 0.5, g_, MUL, MUL, t)
            out_proj(w["odd_w_out_2"][0], [oT[:, k:k + 2, :] for k in range(0, 8, 2)], two_parts(Arena(0, ARENA), 8, T), 8, t, False)

        squares(banks[0], 0, 8, t_x)
        mix_block(0)
        ffn(0)
        mix_block(1)
        second_consts()
        moe(1)
        even()
        odd()
        t_out = dma(SP, "out", lambda e: e.dma_start(outT.rearrange("(t p) n -> p t n", p=128), X), last())
        SP(lambda e: e.nop(), t_out)
        place_splits()
        number(engines)

        block = ctx.enter_context(nc.Block())
        for E, name in ((PE_, "tensor"), (V_, "vector"), (Aq_, "scalar"), (G_, "gpsimd"), (SP, "sync")):
            def body(e, E=E):
                E.run(e)
            {"tensor": block.tensor, "vector": block.vector, "scalar": block.scalar, "gpsimd": block.gpsimd,
             "sync": block.sync}[name](body)


_W = ["w_in", "rw_w2", "rw_a2", "rw_g2", "w_gate", "w_branch", "w_out", "ffn_w1", "ffn_w3", "ffn_w2", "moe_w1", "moe_w3",
      "moe_w2", "even_w_in_2", "even_w_out_2", "odd_w_in_2", "odd_w_out_2"]


def kernel(**inputs):
    import concourse.bacc as _bacc
    from concourse.bass_utils import run_bass_kernel_spmd as _run

    nc = _bacc.Bacc("TRN2", target_bir_lowering=False, num_devices=1)
    i = {k: np.asarray(v) for k, v in inputs.items()}
    arrays = {k: np.ascontiguousarray(i[k]) for k in _W}
    arrays.update(consts())
    arrays["par"] = params(i)
    arrays["xT"] = np.ascontiguousarray(i["x"][0].T)
    h = {k: nc.dram_tensor(k, a.shape, F, kind="ExternalInput").ap() for k, a in arrays.items()}
    outT = nc.dram_tensor("outT", (DM, T), F, kind="ExternalOutput").ap()
    build(nc, {k: h[k] for k in _W}, {k: h[k] for k in CONSTS}, h["par"], h["xT"], outT)
    r = _run(nc, [arrays], core_ids=[0])
    return np.ascontiguousarray(r.results[0]["outT"].T)[None]
```
